# Optimizing a Trainium2 kernel written in Bass

```python
import jax, jax.numpy as jnp
from jax import lax
import numpy as np
import jax
import jax.numpy as jnp

D_MODEL = 1024
BATCH = 1
SEQ = 512
DEPTH = 1

GRID_W = 64
CTX_LEN = 256
RET_HEADS = 4
RET_DK = 128
RET_DV = 128
RET_CHUNK = 128
WIN_HEADS = 8
WIN_KV_HEADS = 2
WIN_HEAD_DIM = 64
WINDOW = 128
WIN_BLOCK = 128
NA_HEADS = 8
NA_HEAD_DIM = 64
NA_ROWS_MAX = 8
NA_COLS = 16
N_EXPERTS = 16
EXPERT_HIDDEN = 1024
CAPACITY_FACTOR = 2
N_BRANCHES = 3
N_MOD = 6
ROPE_BASE = 10000.0
EPS = 1e-6
NEG_INF = -1e30
RET_QK = RET_HEADS * RET_DK
RET_V = RET_HEADS * RET_DV
WIN_Q = WIN_HEADS * WIN_HEAD_DIM
WIN_KV = WIN_KV_HEADS * WIN_HEAD_DIM
NA_W = NA_HEADS * NA_HEAD_DIM
IN_SPLITS = (('q_r', RET_QK), ('k_r', RET_QK), ('v_r', RET_V), ('g_r', RET_V),
             ('q_w', WIN_Q), ('k_w', WIN_KV), ('v_w', WIN_KV),
             ('q_n', NA_W), ('k_n', NA_W), ('v_n', NA_W),
             ('gates', N_BRANCHES * D_MODEL))
IN_COLS = 2 * RET_QK + 2 * RET_V + WIN_Q + 2 * WIN_KV + 3 * NA_W + N_BRANCHES * D_MODEL
KV_NAMES = ('k_r', 'v_r', 'k_w', 'v_w', 'k_n', 'v_n')


def rms_norm(x, g):
    xf = x.astype(jnp.float32)
    y = xf * lax.rsqrt(jnp.mean(xf * xf, axis=-1, keepdims=True) + EPS)
    return (y * g.astype(jnp.float32)).astype(x.dtype)

def modulate(h, shift, scale):
    return h * (1 + scale[:, None, :]) + shift[:, None, :]

def column_layout():
    layout, off = {}, 0
    for name, size in IN_SPLITS:
        layout[name] = (off, size)
        off += size
    return layout

def split_columns(p):
    return {n: p[..., o:o + s] for n, (o, s) in column_layout().items()}

def heads(t, n_heads):
    return t.reshape(t.shape[0], t.shape[1], n_heads, -1)

def axial_rope(x):
    n, d = x.shape[1], x.shape[-1]
    nf = d // 4
    t = jnp.arange(n)
    row = (t // GRID_W).astype(jnp.float32)
    col = (t % GRID_W).astype(jnp.float32)
    inv = ROPE_BASE ** (-jnp.arange(nf, dtype=jnp.float32) / nf)
    ang = jnp.concatenate([row[:, None] * inv, col[:, None] * inv], axis=-1)
    cos = jnp.cos(ang)[None, :, None, :]
    sin = jnp.sin(ang)[None, :, None, :]
    xf = x.astype(jnp.float32)
    x1, x2 = xf[..., :d // 2], xf[..., d // 2:]
    return jnp.concatenate([x1 * cos - x2 * sin, x1 * sin + x2 * cos], axis=-1).astype(x.dtype)

def retention_final_state(k, v, log_gamma):
    n = k.shape[2]
    w = jnp.exp((n - 1 - jnp.arange(n, dtype=jnp.float32))[None, :] * log_gamma[:, None])
    return jnp.einsum('bhnd,bhne->bhde', k * w[None, :, :, None], v)

def retention_chunkwise(q, k, v, log_gamma, state0, include_diag):
    b, h, n, dk = q.shape
    dv = v.shape[-1]
    ch = RET_CHUNK
    nc = n // ch
    qc = q.reshape(b, h, nc, ch, dk)
    kc = k.reshape(b, h, nc, ch, dk)
    vc = v.reshape(b, h, nc, ch, dv)
    i = jnp.arange(ch, dtype=jnp.float32)
    diff = i[:, None] - i[None, :]
    lg = log_gamma[:, None, None]
    dmat = jnp.where(diff >= (0.0 if include_diag else 1.0), jnp.exp(jnp.maximum(diff, 0.0) * lg), 0.0)
    inner = jnp.einsum('bhnid,bhnjd->bhnij', qc, kc) * dmat[None, :, None]
    inner = jnp.einsum('bhnij,bhnje->bhnie', inner, vc)
    zeta = jnp.exp((ch - 1 - i)[None, :] * log_gamma[:, None])
    s = jnp.einsum('bhnjd,bhnje->nbhde', kc * zeta[None, :, None, :, None], vc)
    chunk_decay = jnp.exp(ch * log_gamma)[None, :, None, None]

    def step(r, s_n):
        return chunk_decay * r + s_n, r

    _, r_prev = lax.scan(step, state0, s)
    xi = jnp.exp((i + 1)[None, :] * log_gamma[:, None])
    cross = jnp.einsum('bhnid,nbhde->bhnie', qc, r_prev) * xi[None, :, None, :, None]
    return (inner + cross).reshape(b, h, n, dv)

def bidirectional_retention(q, k, v, lg_f, lg_b, state_f, state_b):
    flip = lambda t: jnp.flip(t, axis=2)
    fwd = retention_chunkwise(q, k, v, lg_f, state_f, True)
    bwd = retention_chunkwise(flip(q), flip(k), flip(v), lg_b, state_b, False)
    return fwd + flip(bwd)

def retention_readout(y, g, gn_gain):
    mu = jnp.mean(y, axis=-1, keepdims=True)
    var = jnp.mean(jnp.square(y - mu), axis=-1, keepdims=True)
    y = (y - mu) * lax.rsqrt(var + EPS)
    y = jnp.swapaxes(y, 1, 2).reshape(y.shape[0], y.shape[2], -1) * gn_gain.astype(jnp.float32)
    return (y * jax.nn.silu(g.astype(jnp.float32))).astype(g.dtype)

def retention_mixer(px, pc, decay_logit, gn_gain, need_ctx):
    lg_f = jax.nn.log_sigmoid(decay_logit[0].astype(jnp.float32))
    lg_b = jax.nn.log_sigmoid(decay_logit[1].astype(jnp.float32))
    to_bhnd = lambda t: jnp.swapaxes(t, 1, 2).astype(jnp.float32)
    k_scale = RET_DK ** -0.5
    qx = to_bhnd(axial_rope(heads(px['q_r'], RET_HEADS)))
    kx = to_bhnd(axial_rope(heads(px['k_r'], RET_HEADS))) * k_scale
    vx = to_bhnd(heads(px['v_r'], RET_HEADS))
    kc = to_bhnd(heads(pc['k_r'], RET_HEADS)) * k_scale
    vc = to_bhnd(heads(pc['v_r'], RET_HEADS))
    flip = lambda t: jnp.flip(t, axis=2)
    state_f = retention_final_state(kc, vc, lg_f)
    state_b = retention_final_state(flip(kc), flip(vc), lg_b)
    yx = retention_readout(bidirectional_retention(qx, kx, vx, lg_f, lg_b, state_f, state_b), px['g_r'], gn_gain)
    yc = None
    if need_ctx:
        qc = to_bhnd(heads(pc['q_r'], RET_HEADS))
        zero = jnp.zeros(state_f.shape, jnp.float32)
        yc = retention_readout(bidirectional_retention(qc, kc, vc, lg_f, lg_b, zero, zero), pc['g_r'], gn_gain)
    return yx, yc

def context_self_attention(q, k, v, sink):
    b, l, hq, d = q.shape
    hkv = k.shape[2]
    g = hq // hkv
    qg = q.reshape(b, l, hkv, g, d)
    s = jnp.einsum('bqhgd,bkhd->bhgqk', qg, k).astype(jnp.float32) * d ** -0.5
    if sink is not None:
        s_sink = jnp.broadcast_to(sink.astype(jnp.float32).reshape(1, hkv, g, 1, 1), s.shape[:-1] + (1,))
        s = jnp.concatenate([s, s_sink], axis=-1)
    p = jax.nn.softmax(s, axis=-1)[..., :l].astype(v.dtype)
    return jnp.einsum('bhgqk,bkhd->bqhgd', p, v).reshape(b, l, hq * d)

def banded_window_attention(q, k, v, kc, vc, sink):
    b, n, hq, d = q.shape
    hkv = k.shape[2]
    g = hq // hkv
    l = kc.shape[1]
    nb = n // WIN_BLOCK
    pad = ((0, 0), (WIN_BLOCK, WIN_BLOCK), (0, 0), (0, 0))

    def band(t):
        tb = jnp.pad(t, pad).reshape(b, nb + 2, WIN_BLOCK, hkv, d)
        return jnp.concatenate([tb[:, :-2], tb[:, 1:-1], tb[:, 2:]], axis=2)

    kb, vb = band(k), band(v)
    qb = q.reshape(b, nb, WIN_BLOCK, hkv, g, d)
    scale = d ** -0.5
    s_loc = jnp.einsum('bnqhgd,bnkhd->bnhgqk', qb, kb).astype(jnp.float32) * scale
    s_ctx = jnp.einsum('bnqhgd,blhd->bnhgql', qb, kc).astype(jnp.float32) * scale
    qpos = jnp.arange(WIN_BLOCK)[:, None]
    kpos = jnp.arange(3 * WIN_BLOCK)[None, :] - WIN_BLOCK
    kabs = jnp.arange(nb)[:, None, None] * WIN_BLOCK + kpos[None]
    valid = (jnp.abs(kpos - qpos) <= WINDOW)[None] & (kabs >= 0) & (kabs < n)
    s_loc = jnp.where(valid[None, :, None, None], s_loc, NEG_INF)
    s_sink = jnp.broadcast_to(sink.astype(jnp.float32).reshape(1, 1, hkv, g, 1, 1), s_ctx.shape[:-1] + (1,))
    p = jax.nn.softmax(jnp.concatenate([s_loc, s_ctx, s_sink], axis=-1), axis=-1)
    kl = 3 * WIN_BLOCK
    p_loc = p[..., :kl].astype(v.dtype)
    p_ctx = p[..., kl:kl + l].astype(v.dtype)
    out = jnp.einsum('bnhgqk,bnkhd->bnqhgd', p_loc, vb) + jnp.einsum('bnhgql,blhd->bnqhgd', p_ctx, vc)
    return out.reshape(b, n, hq * d)

def window_mixer(px, pc, sink, need_ctx):
    q = axial_rope(heads(px['q_w'], WIN_HEADS))
    k = axial_rope(heads(px['k_w'], WIN_KV_HEADS))
    v = heads(px['v_w'], WIN_KV_HEADS)
    kc = heads(pc['k_w'], WIN_KV_HEADS)
    vc = heads(pc['v_w'], WIN_KV_HEADS)
    yx = banded_window_attention(q, k, v, kc, vc, sink)
    yc = context_self_attention(heads(pc['q_w'], WIN_HEADS), kc, vc, sink) if need_ctx else None
    return yx, yc

def neighbourhood_attention(q, k, v, kc, vc, rpb):
    b, n, h, d = q.shape
    rows = n // GRID_W
    kr = min(NA_ROWS_MAX, rows)
    r = jnp.arange(rows)
    row_idx = jnp.clip(r - kr // 2, 0, rows - kr)[:, None] + jnp.arange(kr)[None, :]
    cq = jnp.arange(GRID_W)
    col_start = jnp.clip(cq - NA_COLS // 2, 0, GRID_W - NA_COLS)
    col_valid = (cq[None, :] >= col_start[:, None]) & (cq[None, :] < col_start[:, None] + NA_COLS)
    ri = row_idx - r[:, None] + NA_ROWS_MAX - 1
    ci = jnp.clip(cq[None, :] - cq[:, None], -(NA_COLS - 1), NA_COLS - 1) + NA_COLS - 1
    bias = rpb.astype(jnp.float32)[:, ri[:, None, :, None], ci[None, :, None, :]]
    qg = q.reshape(b, rows, GRID_W, h, d)
    k_rows = k.reshape(b, rows, GRID_W, h, d)[:, row_idx]
    v_rows = v.reshape(b, rows, GRID_W, h, d)[:, row_idx]
    scale = d ** -0.5
    s_loc = jnp.einsum('brchd,brkwhd->bhrckw', qg, k_rows).astype(jnp.float32) * scale + bias[None]
    s_loc = jnp.where(col_valid[:, None, :], s_loc, NEG_INF).reshape(b, h, rows, GRID_W, kr * GRID_W)
    s_ctx = jnp.einsum('brchd,blhd->bhrcl', qg, kc).astype(jnp.float32) * scale
    p = jax.nn.softmax(jnp.concatenate([s_loc, s_ctx], axis=-1), axis=-1)
    nl = kr * GRID_W
    p_loc = p[..., :nl].reshape(b, h, rows, GRID_W, kr, GRID_W).astype(v.dtype)
    p_ctx = p[..., nl:].astype(v.dtype)
    out = jnp.einsum('bhrckw,brkwhd->brchd', p_loc, v_rows) + jnp.einsum('bhrcl,blhd->brchd', p_ctx, vc)
    return out.reshape(b, n, h * d)

def na_mixer(px, pc, rpb, need_ctx):
    q = heads(px['q_n'], NA_HEADS)
    k = heads(px['k_n'], NA_HEADS)
    v = heads(px['v_n'], NA_HEADS)
    kc = heads(pc['k_n'], NA_HEADS)
    vc = heads(pc['v_n'], NA_HEADS)
    yx = neighbourhood_attention(q, k, v, kc, vc, rpb)
    yc = context_self_attention(heads(pc['q_n'], NA_HEADS), kc, vc, None) if need_ctx else None
    return yx, yc

def gated_merge(gates, ya, yb, yc, w_ret, w_win, w_na, w_out):
    ga, gb, gc = jnp.split(jax.nn.sigmoid(gates), N_BRANCHES, axis=-1)
    return (ga * (ya @ w_ret) + gb * (yb @ w_win) + gc * (yc @ w_na)) @ w_out

def hybrid_mixer(hx, hc, w_in, decay_logit, gn_gain, w_ret, sink, w_win, rpb, w_na, w_out, need_ctx):
    px = split_columns(hx @ w_in)
    if need_ctx:
        pc = split_columns(hc @ w_in)
    else:
        lay = column_layout()
        pc = {nm: hc @ w_in[:, lay[nm][0]:lay[nm][0] + lay[nm][1]] for nm in KV_NAMES}
    ya, yca = retention_mixer(px, pc, decay_logit, gn_gain, need_ctx)
    yb, ycb = window_mixer(px, pc, sink, need_ctx)
    yc, ycc = na_mixer(px, pc, rpb, need_ctx)
    mx = gated_merge(px['gates'], ya, yb, yc, w_ret, w_win, w_na, w_out)
    mc = gated_merge(pc['gates'], yca, ycb, ycc, w_ret, w_win, w_na, w_out) if need_ctx else None
    return mx, mc

def expert_choice_ffn(h, w_router, w_gate, w_up, w_down):
    b, n, d = h.shape
    cap = CAPACITY_FACTOR * n // N_EXPERTS
    aff = jax.nn.softmax((h @ w_router).astype(jnp.float32), axis=-1)
    gate, idx = lax.top_k(jnp.swapaxes(aff, 1, 2), cap)
    bidx = jnp.arange(b)[:, None, None]
    xe = h[bidx, idx]
    hid = jax.nn.silu(jnp.einsum('becd,edf->becf', xe, w_gate)) * jnp.einsum('becd,edf->becf', xe, w_up)
    ye = jnp.einsum('becf,efd->becd', hid, w_down) * gate[..., None].astype(h.dtype)
    return jnp.zeros_like(h).at[bidx, idx].add(ye)

def first_inputs(seed: int = 0) -> dict:
    key = jax.random.key(seed)
    ks = jax.random.split(key, 24)
    f32 = jnp.float32
    d = D_MODEL
    nrm = lambda k, shape, s: jax.random.normal(k, shape, f32) * s
    gamma0 = 1.0 - 2.0 ** (-5.0 - np.arange(RET_HEADS))
    logit0 = jnp.asarray(np.log(gamma0 / (1.0 - gamma0)).astype(np.float32))
    return {
        'x': nrm(ks[0], (BATCH, SEQ, d), 1.0),
        'c': nrm(ks[1], (BATCH, d), 1.0),
        'ctx': nrm(ks[2], (BATCH, CTX_LEN, d), 1.0),
        'c_ctx': nrm(ks[3], (d,), 1.0),
        'w_mod': nrm(ks[4], (DEPTH, d, N_MOD * d), 0.5 * d ** -0.5),
        'b_mod': nrm(ks[5], (DEPTH, N_MOD * d), 0.02),
        'g_mix': 1.0 + nrm(ks[6], (DEPTH, d), 0.02),
        'g_ffn': 1.0 + nrm(ks[7], (DEPTH, d), 0.02),
        'w_in': nrm(ks[8], (DEPTH, d, IN_COLS), d ** -0.5),
        'ret_decay_logit': logit0[None, None, :] + nrm(ks[9], (DEPTH, 2, RET_HEADS), 0.1),
        'ret_gn': 1.0 + nrm(ks[10], (DEPTH, RET_V), 0.02),
        'w_ret': nrm(ks[11], (DEPTH, RET_V, d), RET_V ** -0.5),
        'win_sink': nrm(ks[12], (DEPTH, WIN_HEADS), 1.0),
        'w_win': nrm(ks[13], (DEPTH, WIN_Q, d), WIN_Q ** -0.5),
        'na_rpb': nrm(ks[14], (DEPTH, NA_HEADS, 2 * NA_ROWS_MAX - 1, 2 * NA_COLS - 1), 0.1),
        'w_na': nrm(ks[15], (DEPTH, NA_W, d), NA_W ** -0.5),
        'w_out': nrm(ks[16], (DEPTH, d, d), d ** -0.5),
        'w_router': nrm(ks[17], (DEPTH, d, N_EXPERTS), d ** -0.5),
        'w_exp_gate': nrm(ks[18], (DEPTH, N_EXPERTS, d, EXPERT_HIDDEN), d ** -0.5),
        'w_exp_up': nrm(ks[19], (DEPTH, N_EXPERTS, d, EXPERT_HIDDEN), d ** -0.5),
        'w_exp_down': nrm(ks[20], (DEPTH, N_EXPERTS, EXPERT_HIDDEN, d), EXPERT_HIDDEN ** -0.5),
        'g_final': 1.0 + nrm(ks[21], (d,), 0.02),
    }

def first_block(x, c, ctx, c_ctx, w_mod, b_mod, g_mix, g_ffn, w_in, ret_decay_logit, ret_gn, w_ret,
              win_sink, w_win, na_rpb, w_na, w_out, w_router, w_exp_gate, w_exp_up, w_exp_down, g_final):
    d = x.shape[-1]
    sc = jax.nn.silu(c)
    scc = jax.nn.silu(c_ctx)[None]
    for layer in range(DEPTH):
        need_ctx = layer < DEPTH - 1
        mod_x = (sc @ w_mod[layer] + b_mod[layer]).reshape(-1, N_MOD, d)
        n_mod_c = N_MOD if need_ctx else 2
        mod_c = (scc @ w_mod[layer][:, :n_mod_c * d] + b_mod[layer][:n_mod_c * d]).reshape(1, n_mod_c, d)
        hx = modulate(rms_norm(x, g_mix[layer]), mod_x[:, 0], mod_x[:, 1])
        hc = modulate(rms_norm(ctx, g_mix[layer]), mod_c[:, 0], mod_c[:, 1])
        mx, mc = hybrid_mixer(hx, hc, w_in[layer], ret_decay_logit[layer], ret_gn[layer], w_ret[layer],
                              win_sink[layer], w_win[layer], na_rpb[layer], w_na[layer], w_out[layer], need_ctx)
        x = x + mod_x[:, 2, None] * mx
        hx = modulate(rms_norm(x, g_ffn[layer]), mod_x[:, 3], mod_x[:, 4])
        x = x + mod_x[:, 5, None] * expert_choice_ffn(hx, w_router[layer], w_exp_gate[layer],
                                                      w_exp_up[layer], w_exp_down[layer])
        if need_ctx:
            ctx = ctx + mod_c[:, 2, None] * mc
            hc = modulate(rms_norm(ctx, g_ffn[layer]), mod_c[:, 3], mod_c[:, 4])
            ctx = ctx + mod_c[:, 5, None] * expert_choice_ffn(hc, w_router[layer], w_exp_gate[layer],
                                                              w_exp_up[layer], w_exp_down[layer])
    return rms_norm(x, g_final)


DEPTH_2 = 2

NORM_EPS = 1e-6

MLA_HEADS = 8
MLA_Q_RANK = 256
MLA_KV_RANK = 128
MLA_NOPE = 64
MLA_ROPE = 32
MLA_V = 64
MLA_WIDTH = MLA_HEADS * MLA_V
Q_BLOCK = 128

POOL_WINDOWS = (2, 4, 8, 16)
POOL_WIDTH = 512
POOL_GROUP = POOL_WIDTH // len(POOL_WINDOWS)

GLA_HEADS = 4
GLA_DK = 64
GLA_DV = 128
GLA_KW = GLA_HEADS * GLA_DK
GLA_WIDTH = GLA_HEADS * GLA_DV
GLA_GATE_RANK = 16
GLA_TAU = 16.0
GLA_CHUNK = 64

N_BRANCH = 3

IN_NAMES = ('mla_q', 'mla_kv', 'mla_kr', 'mla_gate', 'pool_x', 'pool_gate',
            'gla_q', 'gla_k', 'gla_v', 'gla_af', 'gla_ab', 'gla_gate', 'merge')
IN_SIZES = (MLA_Q_RANK, MLA_KV_RANK, MLA_ROPE, MLA_WIDTH, POOL_WIDTH, POOL_WIDTH,
            GLA_KW, GLA_KW, GLA_WIDTH, GLA_GATE_RANK, GLA_GATE_RANK, GLA_WIDTH, N_BRANCH * D_MODEL)
D_IN = sum(IN_SIZES)


def rmsnorm(x, g):
    xf = x.astype(jnp.float32)
    y = xf * lax.rsqrt(jnp.mean(xf * xf, axis=-1, keepdims=True) + NORM_EPS)
    return (y * g.astype(jnp.float32)).astype(x.dtype)

def split_columns_2(z):
    offsets = [int(o) for o in np.cumsum(IN_SIZES)[:-1]]
    return dict(zip(IN_NAMES, jnp.split(z, offsets, axis=-1)))

def flip(t):
    return t[:, ::-1]

def axial_rope_tables(row, col):
    half = MLA_ROPE // 2
    inv = ROPE_BASE ** (-jnp.arange(0, half, 2, dtype=jnp.float32) / half)
    ang_r = row.astype(jnp.float32)[:, None] * inv
    ang_c = col.astype(jnp.float32)[:, None] * inv
    ang = jnp.concatenate([ang_r, ang_r, ang_c, ang_c], axis=-1)
    return jnp.cos(ang), jnp.sin(ang)

def apply_rope(x, cos, sin):
    half = MLA_ROPE // 2
    quarter = half // 2

    def rot(v):
        return jnp.concatenate([-v[..., quarter:], v[..., :quarter]], axis=-1)

    rotated = jnp.concatenate([rot(x[..., :half]), rot(x[..., half:])], axis=-1)
    return (x * cos + rotated * sin).astype(x.dtype)

def softmax_attention(q, k, v, scale):
    s = jnp.einsum('bqhd,bkhd->bhqk', q, k).astype(jnp.float32) * scale
    p = jax.nn.softmax(s, axis=-1).astype(v.dtype)
    return jnp.einsum('bhqk,bkhd->bqhd', p, v)

def blocked_attention(q, k, v, scale):
    B, L, H, dk = q.shape
    nblk = L // Q_BLOCK
    qb = q.reshape(B, nblk, Q_BLOCK, H, dk).transpose(1, 0, 2, 3, 4)
    ob = lax.map(lambda qq: softmax_attention(qq, k, v, scale), qb)
    return ob.transpose(1, 0, 2, 3, 4).reshape(B, L, H, v.shape[-1])

def mla_queries(zz, q_norm, w_uq):
    B, L, _ = zz['mla_q'].shape
    q = (rmsnorm(zz['mla_q'], q_norm) @ w_uq).reshape(B, L, MLA_HEADS, MLA_NOPE + MLA_ROPE)
    return q[..., :MLA_NOPE], q[..., MLA_NOPE:]

def mla_keys_values(zz, kv_norm, w_ukv):
    B, L, _ = zz['mla_kv'].shape
    kv = (rmsnorm(zz['mla_kv'], kv_norm) @ w_ukv).reshape(B, L, MLA_HEADS, MLA_NOPE + MLA_V)
    return kv[..., :MLA_NOPE], kv[..., MLA_NOPE:]

def assemble_keys(k_nope, k_rope):
    B, L, H, _ = k_nope.shape
    return jnp.concatenate([k_nope, jnp.broadcast_to(k_rope[:, :, None, :], (B, L, H, MLA_ROPE))], axis=-1)

def mla_branch(z, zc, cos, sin, q_norm, w_uq, kv_norm, w_ukv, with_ctx_out):
    B, L, _ = z['mla_q'].shape
    scale = (MLA_NOPE + MLA_ROPE) ** -0.5
    q_nope, q_rope = mla_queries(z, q_norm, w_uq)
    q = jnp.concatenate([q_nope, apply_rope(q_rope, cos[:, None, :], sin[:, None, :])], axis=-1)
    k_nope, v = mla_keys_values(z, kv_norm, w_ukv)
    k = assemble_keys(k_nope, apply_rope(z['mla_kr'], cos, sin))
    kc_nope, vc = mla_keys_values(zc, kv_norm, w_ukv)
    kc = assemble_keys(kc_nope, zc['mla_kr'])
    k_all = jnp.concatenate([kc, k], axis=1)
    v_all = jnp.concatenate([vc, v], axis=1)
    y = blocked_attention(q, k_all, v_all, scale).reshape(B, L, MLA_WIDTH)
    y = y * jax.nn.silu(z['mla_gate'])
    if with_ctx_out:
        Bc, Lc, _ = zc['mla_q'].shape
        qc = jnp.concatenate(mla_queries(zc, q_norm, w_uq), axis=-1)
        yc = softmax_attention(qc, kc, vc, scale).reshape(Bc, Lc, MLA_WIDTH) * jax.nn.silu(zc['mla_gate'])
    else:
        yc = None
    return y, yc

def multiscale_pool(u):
    B, L, W = u.shape
    uf = u.astype(jnp.float32)
    csum = jnp.concatenate([jnp.zeros((B, 1, W), jnp.float32), jnp.cumsum(uf, axis=1)], axis=1)
    t = jnp.arange(L)
    outs = []
    for g, w in enumerate(POOL_WINDOWS):
        lo = jnp.clip(t - w // 2, 0, L)
        hi = jnp.clip(t + w // 2, 0, L)
        cs = csum[..., g * POOL_GROUP:(g + 1) * POOL_GROUP]
        count = (hi - lo).astype(jnp.float32)[None, :, None]
        outs.append((jnp.take(cs, hi, axis=1) - jnp.take(cs, lo, axis=1)) / count)
    return (jnp.concatenate(outs, axis=-1) - uf).astype(u.dtype)

def pool_branch(zz, pool_w, pool_scale):
    B, L, _ = zz['pool_x'].shape
    pooled = multiscale_pool(zz['pool_x']).reshape(B, L, len(POOL_WINDOWS), POOL_GROUP)
    mixed = jnp.einsum('blgi,gio->blgo', pooled, pool_w).reshape(B, L, POOL_WIDTH)
    return mixed * pool_scale * jax.nn.silu(zz['pool_gate'])

def gla_scan(q, k, v, log_a, s0, with_out):
    B, L, H, _ = q.shape
    n = L // GLA_CHUNK

    def to_chunks(t):
        return t.reshape(B, n, GLA_CHUNK, H, t.shape[-1]).transpose(1, 0, 3, 2, 4)

    mask = jnp.tril(jnp.ones((GLA_CHUNK, GLA_CHUNK), bool))[:, :, None]

    def step(s, inp):
        qq, kk, vv, aa = inp
        b = jnp.cumsum(aa, axis=2)
        b_last = b[:, :, -1:, :]
        s_new = jnp.exp(b_last)[:, :, 0, :, None] * s + jnp.einsum('bhcd,bhce->bhde', kk * jnp.exp(b_last - b), vv)
        if not with_out:
            return s_new, None
        inter = jnp.einsum('bhcd,bhde->bhce', qq * jnp.exp(b), s)
        decay = jnp.exp(jnp.where(mask, b[:, :, :, None, :] - b[:, :, None, :, :], -jnp.inf))
        attn = jnp.einsum('bhid,bhjd,bhijd->bhij', qq, kk, decay)
        intra = jnp.einsum('bhij,bhje->bhie', attn, vv)
        return s_new, inter + intra

    s_fin, out = lax.scan(step, s0, (to_chunks(q), to_chunks(k), to_chunks(v), to_chunks(log_a)))
    if with_out:
        out = out.transpose(1, 0, 3, 2, 4).reshape(B, L, H, v.shape[-1])
    return s_fin, out

def gla_inputs(zz, af_w2, af_b, ab_w2, ab_b):
    B, L, _ = zz['gla_v'].shape
    f32 = jnp.float32
    q = zz['gla_q'].astype(f32).reshape(B, L, GLA_HEADS, GLA_DK) * GLA_DK ** -0.5
    k = zz['gla_k'].astype(f32).reshape(B, L, GLA_HEADS, GLA_DK)
    v = zz['gla_v'].astype(f32).reshape(B, L, GLA_HEADS, GLA_DV)
    log_a_f = (jax.nn.log_sigmoid((zz['gla_af'] @ af_w2 + af_b).astype(f32)) / GLA_TAU).reshape(B, L, GLA_HEADS, GLA_DK)
    log_a_b = (jax.nn.log_sigmoid((zz['gla_ab'] @ ab_w2 + ab_b).astype(f32)) / GLA_TAU).reshape(B, L, GLA_HEADS, GLA_DK)
    return q, k, v, log_a_f, log_a_b

def gla_output(o, zz, g):
    B, L = o.shape[:2]
    o = rmsnorm(o, g).reshape(B, L, GLA_WIDTH).astype(zz['gla_gate'].dtype)
    return o * jax.nn.silu(zz['gla_gate'])

def gla_branch(z, zc, af_w2, af_b, ab_w2, ab_b, gla_norm, with_ctx_out):
    qc, kc, vc, afc, abc = gla_inputs(zc, af_w2, af_b, ab_w2, ab_b)
    s0 = jnp.zeros((qc.shape[0], GLA_HEADS, GLA_DK, GLA_DV), jnp.float32)
    sc_f, oc_f = gla_scan(qc, kc, vc, afc, s0, with_ctx_out)
    sc_b, oc_b = gla_scan(flip(qc), flip(kc), flip(vc), flip(abc), s0, with_ctx_out)
    q, k, v, af, ab = gla_inputs(z, af_w2, af_b, ab_w2, ab_b)
    _, o_f = gla_scan(q, k, v, af, sc_f, True)
    _, o_b = gla_scan(flip(q), flip(k), flip(v), flip(ab), sc_b, True)
    y = gla_output(o_f + flip(o_b), z, gla_norm)
    yc = gla_output(oc_f + flip(oc_b), zc, gla_norm) if with_ctx_out else None
    return y, yc

def merge_branches(zz, y_mla, y_pool, y_gla, w_bm, w_bp, w_bg, w_out):
    gates = jax.nn.sigmoid(zz['merge'].astype(jnp.float32)).astype(y_mla.dtype)
    g_mla, g_pool, g_gla = jnp.split(gates, N_BRANCH, axis=-1)
    merged = g_mla * (y_mla @ w_bm) + g_pool * (y_pool @ w_bp) + g_gla * (y_gla @ w_bg)
    return merged @ w_out

def trunk_layer(x, xc, mod, mod_c, cos, sin, pre_g, post_g, w_in, mla_q_norm, mla_w_uq, mla_kv_norm,
                mla_w_ukv, pool_w, pool_scale, gla_af_w2, gla_af_b, gla_ab_w2, gla_ab_b, gla_norm,
                w_branch_mla, w_branch_pool, w_branch_gla, w_out, with_ctx_out):
    shift, scale, gate = jnp.split(mod[:, None, :], 3, axis=-1)
    shift_c, scale_c, gate_c = jnp.split(mod_c[None, None, :], 3, axis=-1)
    z = split_columns_2((rmsnorm(x, pre_g) * (1 + scale) + shift) @ w_in)
    zc = split_columns_2((rmsnorm(xc, pre_g) * (1 + scale_c) + shift_c) @ w_in)
    y_mla, yc_mla = mla_branch(z, zc, cos, sin, mla_q_norm, mla_w_uq, mla_kv_norm, mla_w_ukv, with_ctx_out)
    y_pool = pool_branch(z, pool_w, pool_scale)
    y_gla, yc_gla = gla_branch(z, zc, gla_af_w2, gla_af_b, gla_ab_w2, gla_ab_b, gla_norm, with_ctx_out)
    out = merge_branches(z, y_mla, y_pool, y_gla, w_branch_mla, w_branch_pool, w_branch_gla, w_out)
    x = x + gate * rmsnorm(out, post_g)
    if with_ctx_out:
        yc_pool = pool_branch(zc, pool_w, pool_scale)
        out_c = merge_branches(zc, yc_mla, yc_pool, yc_gla, w_branch_mla, w_branch_pool, w_branch_gla, w_out)
        xc = xc + gate_c * rmsnorm(out_c, post_g)
    return x, xc

def second_inputs(seed: int = 0) -> dict:
    key = jax.random.key(seed)
    ks = jax.random.split(key, 24)
    f32 = jnp.float32

    def nrm(k, shape, s):
        return jax.random.normal(k, shape, f32) * s

    def gain(k, n):
        return 1.0 + 0.1 * jax.random.normal(k, (DEPTH_2, n), f32)

    return {
        'x': nrm(ks[0], (BATCH, SEQ, D_MODEL), 1.0),
        'c': nrm(ks[1], (BATCH, D_MODEL), 1.0),
        'ctx': nrm(ks[2], (BATCH, CTX_LEN, D_MODEL), 1.0),
        'c_ctx': nrm(ks[3], (D_MODEL,), 1.0),
        'mod_w': nrm(ks[4], (DEPTH_2, D_MODEL, 3 * D_MODEL), 0.5 * D_MODEL ** -0.5),
        'mod_b': nrm(ks[5], (DEPTH_2, 3 * D_MODEL), 0.02),
        'pre_norm': gain(ks[6], D_MODEL),
        'post_norm': gain(ks[7], D_MODEL),
        'w_in': nrm(ks[8], (DEPTH_2, D_MODEL, D_IN), D_MODEL ** -0.5),
        'mla_q_norm': gain(ks[9], MLA_Q_RANK),
        'mla_w_uq': nrm(ks[10], (DEPTH_2, MLA_Q_RANK, MLA_HEADS * (MLA_NOPE + MLA_ROPE)), MLA_Q_RANK ** -0.5),
        'mla_kv_norm': gain(ks[11], MLA_KV_RANK),
        'mla_w_ukv': nrm(ks[12], (DEPTH_2, MLA_KV_RANK, MLA_HEADS * (MLA_NOPE + MLA_V)), MLA_KV_RANK ** -0.5),
        'pool_w': nrm(ks[13], (DEPTH_2, len(POOL_WINDOWS), POOL_GROUP, POOL_GROUP), POOL_GROUP ** -0.5),
        'pool_scale': gain(ks[14], POOL_WIDTH),
        'gla_af_w2': nrm(ks[15], (DEPTH_2, GLA_GATE_RANK, GLA_KW), GLA_GATE_RANK ** -0.5),
        'gla_af_b': nrm(ks[16], (DEPTH_2, GLA_KW), 0.1),
        'gla_ab_w2': nrm(ks[17], (DEPTH_2, GLA_GATE_RANK, GLA_KW), GLA_GATE_RANK ** -0.5),
        'gla_ab_b': nrm(ks[18], (DEPTH_2, GLA_KW), 0.1),
        'gla_norm': gain(ks[19], GLA_DV),
        'w_branch_mla': nrm(ks[20], (DEPTH_2, MLA_WIDTH, D_MODEL), MLA_WIDTH ** -0.5),
        'w_branch_pool': nrm(ks[21], (DEPTH_2, POOL_WIDTH, D_MODEL), POOL_WIDTH ** -0.5),
        'w_branch_gla': nrm(ks[22], (DEPTH_2, GLA_WIDTH, D_MODEL), GLA_WIDTH ** -0.5),
        'w_out': nrm(ks[23], (DEPTH_2, D_MODEL, D_MODEL), D_MODEL ** -0.5),
    }

def second_block(x, c, ctx, c_ctx, mod_w, mod_b, pre_norm, post_norm, w_in, mla_q_norm, mla_w_uq,
              mla_kv_norm, mla_w_ukv, pool_w, pool_scale, gla_af_w2, gla_af_b, gla_ab_w2, gla_ab_b,
              gla_norm, w_branch_mla, w_branch_pool, w_branch_gla, w_out):
    n_tok = x.shape[1]
    rows = n_tok // GRID_W
    row = jnp.repeat(jnp.arange(rows), GRID_W)
    col = jnp.tile(jnp.arange(GRID_W), rows)
    cos, sin = axial_rope_tables(row, col)
    silu_c = jax.nn.silu(c)
    silu_cc = jax.nn.silu(c_ctx)
    xc = ctx
    for l in range(DEPTH_2):
        mod = silu_c @ mod_w[l] + mod_b[l]
        mod_c = silu_cc @ mod_w[l] + mod_b[l]
        x, xc = trunk_layer(x, xc, mod, mod_c, cos, sin, pre_norm[l], post_norm[l], w_in[l],
                            mla_q_norm[l], mla_w_uq[l], mla_kv_norm[l], mla_w_ukv[l], pool_w[l],
                            pool_scale[l], gla_af_w2[l], gla_af_b[l], gla_ab_w2[l], gla_ab_b[l],
                            gla_norm[l], w_branch_mla[l], w_branch_pool[l], w_branch_gla[l], w_out[l],
                            l < DEPTH_2 - 1)
    return x


def setup_inputs(seed=0):
    out = dict(first_inputs(seed))
    for name, value in second_inputs(seed + 1).items():
        if name != "x":
            out[name + "_2"] = value
    return out


def reference(
    x, c, ctx, c_ctx, w_mod, b_mod, g_mix, g_ffn, w_in, ret_decay_logit, ret_gn, w_ret,
    win_sink, w_win, na_rpb, w_na, w_out, w_router, w_exp_gate, w_exp_up, w_exp_down, g_final,
    c_2, ctx_2, c_ctx_2, mod_w_2, mod_b_2, pre_norm_2, post_norm_2, w_in_2, mla_q_norm_2,
    mla_w_uq_2, mla_kv_norm_2, mla_w_ukv_2, pool_w_2, pool_scale_2, gla_af_w2_2, gla_af_b_2,
    gla_ab_w2_2, gla_ab_b_2, gla_norm_2, w_branch_mla_2, w_branch_pool_2, w_branch_gla_2,
    w_out_2,
):
    x = first_block(
        x, c, ctx, c_ctx, w_mod, b_mod, g_mix, g_ffn, w_in, ret_decay_logit, ret_gn, w_ret,
        win_sink, w_win, na_rpb, w_na, w_out, w_router, w_exp_gate, w_exp_up, w_exp_down,
        g_final,
    )
    return second_block(
        x, c_2, ctx_2, c_ctx_2, mod_w_2, mod_b_2, pre_norm_2, post_norm_2, w_in_2, mla_q_norm_2,
        mla_w_uq_2, mla_kv_norm_2, mla_w_ukv_2, pool_w_2, pool_scale_2, gla_af_w2_2, gla_af_b_2,
        gla_ab_w2_2, gla_ab_b_2, gla_norm_2, w_branch_mla_2, w_branch_pool_2, w_branch_gla_2,
        w_out_2,
    )


_drawn_inputs = setup_inputs


def setup_inputs(seed=0):
    import zlib

    import numpy as np

    out = dict(_drawn_inputs(seed))
    spreads = {}
    factors = {'b_mod': 2.985,
     'g_mix': 7.649,
     'g_ffn': 7.759,
     'ret_gn': 8.0,
     'win_sink': 8.0,
     'na_rpb': 8.0,
     'mla_q_norm_2': 8.0,
     'mla_kv_norm_2': 6.026,
     'gla_af_b_2': 5.416,
     'gla_ab_b_2': 5.725,
     'pool_scale_2': 4.481,
     'gla_af_w2_2': 3.973,
     'gla_ab_w2_2': 3.941,
     'gla_norm_2': 4.794}
    for name, (base, spread) in spreads.items():
        noise = np.random.default_rng([zlib.crc32(name.encode()), seed]).standard_normal(out[name].shape)
        drawn = base * np.exp(spread * noise) if base else spread * noise
        out[name] = jnp.asarray(drawn.astype(out[name].dtype))
    for name, factor in factors.items():
        out[name] = (out[name] * factor).astype(out[name].dtype)
    return out
```

```python
import concourse.bass as bass
from concourse import mybir
from contextlib import ExitStack
import numpy as np

P = 128
D = 1024
KT = D // P
CTX, SEQ = 256, 512
TOK = CTX + SEQ
TT = TOK // P
EPS = 1e-6
NE, CAP, FF = 16, 64, 1024
PAIRS = NE // 2
UNIT = 2048
NSLOT = 6
ALL = ((0, 384), (384, 384))
IMG = ((CTX, SEQ),)
CLAMP = 1280.0

B1 = dict(q_r=0, k_r=512, v_r=1024, g_r=1536, q_w=2048, k_w=2560, v_w=2688, q_n=2816, k_n=3328,
          v_n=3840, gates=4352)
B2 = dict(q=0, kv=256, kr=384, mgate=416, px=928, pgate=1440, gq=1952, gk=2208, gv=2464, af=2976,
          ab=2992, ggate=3008, merge=3520)
LAYERS = (0, 1)
SCAN = ((0, 1, 2, 3, 4, 5), (1, 0, 5, 4, 3, 2))
OWN_CHUNKS = (range(TT), range(2, TT))
PASSES = ("win", "na", ("mla", 0), ("mlac", 0), ("mla", 1))


def window_q_cols(t):
    return np.r_[t * 64:t * 64 + 64, (t + 4) * 64:(t + 4) * 64 + 64]


def stream_plan():
    def cols(w, lead, name, c0, n):
        return [((name, t), w, lead, None, np.arange(c0 + t * P, c0 + t * P + P)) for t in range(n)]

    def rhs(w, lead, name, c0, n, per=2):
        return [((name, i), w, lead, np.arange(i * per * P, (i + 1) * per * P), np.arange(c0, c0 + n))
                for i in range(KT // per)]

    out = cols("w_mod", (0,), "mod", 0, 48)
    out += cols("w_in", (0,), "q_r", B1["q_r"], 4) + cols("w_in", (0,), "k_r", B1["k_r"], 4)
    out += rhs("w_in", (0,), "v_r", B1["v_r"], 512) + cols("w_in", (0,), "g_r", B1["g_r"], 4)
    out += [(("q_w", t), "w_in", (0,), None, B1["q_w"] + window_q_cols(t)) for t in range(4)]
    out += cols("w_in", (0,), "k_w", B1["k_w"], 1) + cols("w_in", (0,), "v_w", B1["v_w"], 1)
    out += cols("w_in", (0,), "q_n", B1["q_n"], 4) + cols("w_in", (0,), "k_n", B1["k_n"], 4)
    out += rhs("w_in", (0,), "v_n", B1["v_n"], 512)
    win_rows = np.concatenate([window_q_cols(t) for t in range(4)])
    for f in range(0, KT, 2):
        for b, w, rows in ((0, "w_ret", None), (1, "w_win", win_rows), (2, "w_na", None)):
            for g in (f, f + 1):
                c0 = B1["gates"] + b * D + g * P
                out.append((("gate", b, g), "w_in", (0,), None, np.arange(c0, c0 + P)))
            out.append((("branch", b, f), w, (0,), rows, np.arange(f * P, f * P + 2 * P)))
    out += cols("w_out", (0,), "w_out", 0, KT)
    for j in range(PAIRS):
        for e in (0, 1):
            out += cols("w_exp_gate", (0, 2 * j + e), ("exp_gate", j, e), 0, KT)
            out += cols("w_exp_up", (0, 2 * j + e), ("exp_up", j, e), 0, KT)
        for e in (0, 1):
            out += cols("w_exp_down", (0, 2 * j + e), ("exp_down", j, e), 0, KT)
    for l in LAYERS:
        w = "w_in_2"
        out += cols("mod_w_2", (l,), ("mod2", l), 0, 24)
        out += cols(w, (l,), ("gq", l), B2["gq"], 2) + cols(w, (l,), ("gk", l), B2["gk"], 2)
        out += rhs(w, (l,), ("gv", l), B2["gv"], 512)
        small = np.full(P, -1)
        small[0:16] = B2["af"] + np.arange(16)
        small[32:48] = B2["ab"] + np.arange(16)
        small[64:96] = B2["kr"] + np.arange(32)
        out.append((("small", l), w, (l,), None, small))
        out.append((("decay_w2", l), None, (l,), None, None))
        out += cols(w, (l,), ("ggate", l), B2["ggate"], 4)
        out += cols(w, (l,), ("mq", l), B2["q"], 2) + cols(w, (l,), ("mkv", l), B2["kv"], 1)
        for h in (0, 4):
            out.append((("uq", l, h), "mla_w_uq_2", (l,), None, np.arange(h * 96, h * 96 + 384)))
        ukv = np.arange(8)[:, None] * 128 + np.arange(64)[None, :]
        out.append((("ukv", l), "mla_w_ukv_2", (l,), None, np.r_[ukv.ravel(), ukv.ravel() + 64]))
        out += cols(w, (l,), ("mgate", l), B2["mgate"], 4)
        for g in range(4):
            out += cols(w, (l,), ("px", l, g), B2["px"] + g * P, 1)
            out += cols(w, (l,), ("pgate", l, g), B2["pgate"] + g * P, 1)
        out.append((("pool_w", l), None, (l,), None, None))
        for f in range(0, KT, 2):
            for b, wb in ((0, "w_branch_mla_2"), (1, "w_branch_pool_2"), (2, "w_branch_gla_2")):
                for g in (f, f + 1):
                    c0 = B2["merge"] + b * D + g * P
                    out.append((("gate", l, b, g), w, (l,), None, np.arange(c0, c0 + P)))
                out.append((("branch", l, b, f), wb, (l,), None, np.arange(f * P, f * P + 2 * P)))
        out += cols("w_out_2", (l,), ("w_out", l), 0, KT)
    return out


def padded_tiles(n):
    per = NSLOT * (UNIT // 1024)
    return -(-n // per) * per


PARAMS = (("bmod", 96), ("gmix", 16), ("gffn", 8), ("gfinal", 8), ("cond", 16), ("cond2", 16),
          ("retgn", 4), ("sink", 8), ("decay", 8)) + tuple(
    (f"{n}{l}", c) for l in LAYERS for n, c in
    (("bmod2", 48), ("pre", 16), ("post", 16), ("qnorm", 2), ("kvnorm", 1), ("pscale", 4),
     ("afb", 2), ("abb", 2), ("glan", 1)))
PCOL, _at = {}, 0
for _n, _c in PARAMS:
    PCOL[_n] = (_at, _at + _c)
    _at += _c
NPAR = _at
CONST = (("ident", 128), ("ones", 128), ("rot_r", 128), ("rot_w", 128), ("rot_m", 128), ("flip", 128),
         ("slots", 64), ("upper", 128), ("lower", 128), ("wleft", 128), ("wright", 128), ("eps", 1))
CCOL, _at = {}, 0
for _n, _c in CONST:
    CCOL[_n] = (_at, _at + _c)
    _at += _c
NCONST = _at
DW = 1408
ARENA = 53184 - 2 * KT * TOK - NSLOT * UNIT - NPAR - NCONST - 520


def constants():
    f = np.float32
    c = np.zeros((P, NCONST), f)
    put = lambda n, a: c.__setitem__((slice(None), slice(*CCOL[n])), a)
    put("ident", np.eye(P))
    put("ones", 1.0)

    def half_rot(d, blocks):
        m = np.zeros((P, P), f)
        for b in blocks:
            for i in range(d // 2):
                m[b + d // 2 + i, b + i] = -1.0
                m[b + i, b + d // 2 + i] = 1.0
        return m

    put("rot_r", half_rot(128, [0]))
    put("rot_w", half_rot(64, [0, 64]))
    put("rot_m", half_rot(16, [64, 80]))
    flip = np.zeros((P, P), f)
    q = np.arange(P)
    flip[63 - q % 64 + 64 * (q // 64), q] = 1.0
    put("flip", flip)
    put("slots", np.arange(64)[None, :])
    put("upper", (q[:, None] <= q[None, :]))
    put("lower", (q[:, None] >= q[None, :]))
    put("wleft", np.where(q[None, :] >= q[:, None], 0.0, -1e30))
    put("wright", np.where(q[None, :] <= q[:, None], 0.0, -1e30))
    put("eps", EPS)
    t = np.arange(SEQ)
    row, col = (t // 64).astype(f), (t % 64).astype(f)

    def tables(d):
        inv = (f(10000.0) ** (-np.arange(d // 4, dtype=f) / f(d // 4))).astype(f)
        ang = np.concatenate([row[:, None] * inv, col[:, None] * inv], -1).astype(f)
        ang = np.concatenate([ang, ang], -1)
        ang = np.concatenate([ang] * (P // d), -1)
        return np.cos(ang).T.astype(f), np.sin(ang).T.astype(f)

    inv = (f(10000.0) ** (-np.arange(0, 16, 2, dtype=f) / f(16))).astype(f)
    ar, ac = row[:, None] * inv, col[:, None] * inv
    ang = np.concatenate([ar, ar, ac, ac], -1).T.astype(f)
    cm, sm = np.ones((P, SEQ), f), np.zeros((P, SEQ), f)
    cm[64:96], sm[64:96] = np.cos(ang), np.sin(ang)
    u = np.arange(DW)[None, :] - 640 - q[:, None]
    ck = np.arange(64)[None, :]
    cq = (63 - q % 64)[:, None]
    start = np.clip(cq - 8, 0, 48)
    colmask = np.where((ck >= start) & (ck < start + 16), 0.0, -1e30)
    inv_count = np.zeros((4, TOK), f)
    for g, w in enumerate((2, 4, 8, 16)):
        for n, off in ((CTX, 0), (SEQ, CTX)):
            tt = np.arange(n)
            inv_count[g, off:off + n] = 1.0 / (np.clip(tt + w // 2, 0, n) - np.clip(tt - w // 2, 0, n))
    return {
        "consts": c,
        "t_ret": np.concatenate([*tables(128), u], 1).astype(f),
        "t_win": np.concatenate(tables(64), 1).astype(f),
        "t_mla": np.concatenate([cm, sm], 1).astype(f),
        "t_colmask": colmask.astype(f),
        "t_count": np.broadcast_to(inv_count.reshape(1, -1), (P, 4 * TOK)).astype(f),
    }


def program(nc, dram, out):
    f32 = mybir.dt.float32
    ACT = mybir.ActivationFunctionType
    ALU = mybir.AluOpType
    AXX = mybir.AxisListType.X
    plan = [p[0] for p in stream_plan()]
    rounds = padded_tiles(len(plan)) // (NSLOT * 2)

    with ExitStack() as ctx:
        def sbuf(name, cols):
            return ctx.enter_context(nc.sbuf_tensor(name, [P, cols], f32))

        R3 = sbuf("residual", KT * TOK)[:, :].rearrange("p (k t) -> p k t", k=KT)
        H3 = sbuf("hidden", KT * TOK)[:, :].rearrange("p (k t) -> p k t", k=KT)
        ring = sbuf("ring", NSLOT * UNIT)
        par = sbuf("params_sb", NPAR)
        con = sbuf("consts_sb", NCONST)
        arena = sbuf("arena", ARENA)
        small = sbuf("small", 520)
        psum = ctx.enter_context(nc.psum_tensor("psum", [P, 8 * 512], f32))

        sems = {}

        def sem(name):
            if name not in sems:
                sems[name] = ctx.enter_context(nc.semaphore(name))
            return sems[name]

        psum_free = [sem(f"psum_free{i}") for i in range(3)]
        loaded = [sem(f"weights_loaded{i}") for i in range(NSLOT)]
        psum_full = sem("psum_full")
        group_no = {}

        def cols(*name):
            g = group_no[name]
            return psum[:, (g % 3) * 1024:(g % 3) * 1024 + 1024]

        def C(name, n=None):
            a, b = CCOL[name]
            return con[:, a:b]

        def Pm(name):
            a, b = PCOL[name]
            return par[:, a:b]

        def area(at, n):
            assert at + n <= ARENA, (at, n, ARENA)
            return arena[:, at:at + n]

        def split(ap, **kw):
            (k, v), = kw.items()
            return ap.rearrange(f"p ({k} n) -> p {k} n", **kw)

        def bank_view(ps, chunks):
            if chunks is ALL:
                return split(ps, a=2)[:, :, 0:384]
            return ps[:, 0:SEQ]

        def tok_view(ap, chunks):
            if chunks is ALL:
                return split(ap, a=2)
            return ap[:, CTX:TOK]

        def wide(col, like):
            return col.to_broadcast([P, like])

        modA = split(small[:, 0:96], a=48)
        gmA = split(small[:, 96:112], a=KT)
        gmF = small[:, 112:120]
        cond = split(small[:, 120:136], a=KT)
        cond2 = split(small[:, 136:152], a=KT)
        modB = split(small[:, 152:200], a=24)
        gmB = split(small[:, 200:216], a=KT)
        pgB = split(small[:, 216:232], a=KT)
        negmax = small[:, 232:248]
        sums = small[:, 248:264]
        esink = small[:, 264:280]
        rinv = small[:, 280:296]
        nsink = small[:, 296:304]
        lg = small[:, 304:312]
        lt1 = small[:, 312:320]
        lt2 = small[:, 320:328]
        expT = small[:, 328:352]
        m16 = small[:, 352:356]
        s16 = small[:, 356:360]
        r16 = small[:, 360:364]
        top8 = small[:, 364:372]
        aff = split(small[:, 372:436], a=4)
        posn = split(small[:, 436:500], a=4)
        tick = small[:, 500:512]
        totals = {}

        class Eng:

            def __init__(self, e, name):
                self.e, self.name, self.seen, self.it, self.per = e, name, {}, None, {}
                self.made, self.last = {}, None

            def at(self, value, key):
                return value if self.it is None else self.it * self.per.get(key, 0) + value

            def next(self, name, n=1):
                self.seen[name] = self.seen.get(name, 0) + n
                return sem(name), self.at(self.seen[name], name)

            def upto(self, name, total):
                self.seen[name] = max(total, self.seen.get(name, 0))
                return sem(name), self.at(total, name)

            def sig(self, name, n=1):
                self.made[name] = self.made.get(name, 0) + n
                self.last = (sem(name), self.made[name], name)
                return sem(name), n

            def read(self, *name):
                g = group_no[name]
                self.last = (psum_free[g % 3], g // 3 + 1, "slot")
                return psum_free[g % 3], 1

            def own(self):
                s, v, key = self.last
                return s, self.at(v, key)

            def written(self, *name):
                return psum_full, self.at(group_no[name] + 1, "groups")

            def taken(self, *name):
                g = group_no[name]
                return psum_free[g % 3], self.at(g // 3 + 1, "slot")

            def begin(self, it, per):
                self.it, self.per, self.start = it, per, (dict(self.seen), dict(self.made))

            def end(self, turns):
                seen, made = self.start
                for k, v in list(self.seen.items()):
                    d = v - seen.get(k, 0)
                    assert d == self.per.get(k, 0), (self.name, k, d)
                    self.seen[k] = v + (turns - 1) * d
                for k, v in list(self.made.items()):
                    self.made[k] = v + (turns - 1) * (v - made.get(k, 0))
                self.it = None

        block = ctx.enter_context(nc.Block())

        YA, YB, YC = (area(i * 2048, 2048) for i in range(3))
        RET = 6144
        rQ, rK = split(area(RET, 2048), a=4), split(area(RET + 2048, 3072), a=4)
        rV = split(area(RET + 5120, 3072), a=TT)
        rSG = split(area(RET + 8192, 2048), a=4)
        rTab = area(RET + 10240, 1024 + DW)
        rCos, rSin, rDist = rTab[:, 0:512], rTab[:, 512:1024], rTab[:, 1024:1024 + DW]
        rE = area(RET + 12672, DW)
        rCW = split(area(RET + 14080, 1024), a=2)
        rP = split(area(RET + 15104, 4096), a=4)
        rTmp = area(RET + 15104, 1024)
        rSq = split(area(RET + 15104, 2048), a=4)
        rRs = split(area(RET + 15104 + 2048, 2048), a=4)
        A3 = split(YA, a=4)

        WIN = 6144
        wQ = split(area(WIN, 2048), a=4)
        wK, wV = area(WIN + 2048, TOK), split(area(WIN + 2816, TOK), a=TT)
        wCos, wSin = area(WIN + 3584, 512), area(WIN + 4096, 512)
        wTmp = area(WIN + 4608, 1024)
        AT1 = WIN + 5632

        NA = 6144
        nQ, nK = split(area(NA, 2048), a=4), split(area(NA + 2048, 3072), a=4)
        nV = split(area(NA + 5120, 3072), a=TT)
        AT2 = NA + 8192
        nB = split(area(NA + 12288, 7168), h=8)
        nMask = area(NA + 19456, 64)

        MRG = 9216
        mSG = split(area(MRG, 6 * TOK), a=6)
        mTmp = split(area(MRG + 6 * TOK, 2 * TOK), a=2)
        mMG = split(area(MRG + 8 * TOK, KT * TOK), a=KT)
        mOUT = split(area(MRG, KT * TOK), a=KT)

        nSq = split(area(ARENA - 4 * TOK, 3 * TOK), a=3)
        nRs = area(ARENA - TOK, TOK)

        def attn_area(at):
            return (split(area(at, 2 * TOK), a=2), split(area(at + 2 * TOK, 2 * TOK), a=2),
                    split(area(at + 4 * TOK, 1024), a=2))

        XP = 0
        eP = H3[:, :, :].rearrange("p k t -> p (k t)")[:, 0:4096].rearrange("p (t n) -> p t n", t=4)
        eHT = split(area(XP, 4096), a=4)
        ePG = split(area(XP + 4096, 4096), a=PAIRS)
        eYE = split(area(XP + 8192, 8192), a=PAIRS)
        ePg = split(area(XP + 16384, 4096), a=4)
        eXE = split(area(XP + 16384, 1024), a=KT)
        eSG = split(area(XP + 17408, 1024), a=2)
        eHID = split(area(XP + 18432, 1024), a=2)
        eYT = split(area(XP + 19456, 1024), a=KT)
        eWR = split(area(XP + 20480, 128), a=KT)
        eA = area(XP + 20608, 512)
        eW = split(area(XP + 21120, 1024), a=2)
        eM = area(XP + 22144, 512)
        eC = area(XP + 22656, 512)

        YG, YM, YP = (split(area(i * 3072, 3072), a=4) for i in range(3))
        G = 3072
        gQ, gK = split(area(G, 1536), a=2), split(area(G + 1536, 1536), a=2)
        gV = split(area(G + 3072, 3072), a=TT)
        gSM = area(G + 6144, TOK)
        gB = split(area(G + 6912, 3072), a=4)
        gS = area(G + 9984, 3072).rearrange("p (d c t n) -> p d c t n", d=2, c=TT, t=2)
        gT1 = split(area(G + 13056, 3072), a=4)
        gLM = split(area(G + 17152, 3072), a=4)
        gKT = area(G + 17152, 3072)

        def gChunk(i):
            at = G + 13056 + 4096 * i
            return (split(area(at, 512), a=4), split(area(at + 512, 512), a=4),
                    area(at + 1024, 2048).rearrange("p (d t s n) -> p d t s n", d=2, t=2, s=4),
                    split(area(at + 3072, 1024), a=2))
        gSq = split(area(G + 13056, 3072), a=4)
        gRs = split(area(G + 17152, 3072), a=4)
        SILU = split(area(G + 20224, 2 * TOK), a=2)

        M = 6144
        mQ, mK = split(area(M, 6144), a=8), split(area(M + 6144, 6144), a=8)
        mV = split(area(M + 12288, 3072), a=TT)
        MW = M + 15360
        mCos, mSin = area(MW, 512), area(MW + 512, 512)
        mRaw = split(area(MW + 1024, 2 * TOK), a=2)
        mKV = area(MW + 1024 + 2 * TOK, TOK)
        mKR = area(3072, TOK)
        mTp = area(3072 + TOK, TOK)
        mSil = split(area(23040, 2 * TOK), a=2)
        mSq, mRs = split(area(3072 + 2 * TOK, TOK), a=1), area(3072 + 3 * TOK, TOK)
        PB = 9216
        pX = area(PB, 2 * (TOK + 32))
        pCnt = split(area(PB + 4096, 4 * TOK), a=4)
        pS = area(PB + 8192, 2 * (TOK + 32))
        pO = split(area(PB + 10240, 4 * TOK), a=4)

        def units(qts):
            return [(t, hh, qi) for t in range(4) for hh in range(2) for qi in range(len(qts))]

        ATT = {n: range(2) if n[0] == "mlac" else range(4) for n in PASSES}
        unit_base = {n: sum(8 * len(ATT[m]) for m in PASSES[:i]) for i, n in enumerate(PASSES)}

        def spans(name, qi):
            if name == "win":
                lo, hi = max(qi - 1, 0), min(qi + 1, 3)
                return (hi - lo + 1) * P, [2 + b for b in range(lo, hi + 1)] + [0, 1]
            if name[0] == "mlac":
                return 0, [0, 1]
            return SEQ, [2, 3, 4, 5, 0, 1]

        @block.tensor
        def _(pe):
            E = Eng(pe, "pe")
            state = dict(g=0, tile=0, owed=0, ended=0)

            def group(*name):
                g = state["g"]
                group_no[name] = g
                state["g"] += 1
                if g >= 3:
                    pe.wait_ge(psum_free[g % 3], E.at(g // 3, "slot"))
                return psum[:, (g % 3) * 1024:(g % 3) * 1024 + 1024]

            def mm(o, lhsT, rhs, start, stop):
                return nc.tensor.matmul(o, lhsT, rhs, start=start, stop=stop)

            def flip(o, a):
                return nc.tensor.transpose(o, a, C("ident")[0:a.shape[0], 0:a.shape[0]])

            def refill(ins):
                if state["owed"]:
                    ins.then_inc(sem("weights_used"), state["owed"])
                    state["owed"] = 0

            def weights(*name):
                n = state["tile"]
                assert plan[n] == name, (plan[n], name)
                state["tile"] += 1
                if n % 2 == 0:
                    u = n // 2
                    pe.wait_ge(loaded[u % NSLOT], E.at(16 * (u // NSLOT + 1), "ring"))
                at = (n // 2 % NSLOT) * UNIT + (n % 2) * 1024
                return ring[:, at:at + 1024]

            def done(n=1):
                for _ in range(n):
                    state["ended"] += 1
                    if state["ended"] % 2 == 0:
                        state["owed"] += 1

            def project(name, w, src, nk, chunks, M=P, src0=0):
                ps = group(*name)
                for k in range(nk):
                    for ci, (c0, n) in enumerate(chunks):
                        ins = mm(ps[0:M, ci * 512:ci * 512 + n], w[:, k, 0:M],
                                 src[:, k, c0 - src0:c0 - src0 + n], k == 0, k == nk - 1)
                        if k == 0 and ci == 0:
                            refill(ins)
                ins.then_inc(psum_full, 1)

            def project_tile(tile, name, chunks):
                w = split(weights(*tile), a=KT)
                project(name, w, H3, KT, chunks)
                done()

            def project_tokens(tiles, name, src, n=512):
                ws = [split(weights(*t), a=2) for t in tiles]
                for t in range(TT):
                    ps = group(*name, t)
                    for k in range(KT):
                        ins = mm(ps[:, 0:n], src[:, k, t * P:(t + 1) * P], ws[k // 2][:, k % 2, :],
                                 k == 0, k == KT - 1)
                        if k == 0:
                            refill(ins)
                    ins.then_inc(psum_full, 1)
                done(len(tiles))

            def modulation(name, tiles, c):
                ps = group(name)
                for i, tname in enumerate(tiles):
                    w = split(weights(*tname), a=KT)
                    for k in range(KT):
                        ins = mm(ps[:, 2 * i:2 * i + 2], w[:, k, :], c[:, k, :], k == 0, k == KT - 1)
                        if k == 0:
                            refill(ins)
                    done()
                ins.then_inc(psum_full, 1)

            def statistics(name, nk, chunks, sq, slots=3):
                ps = group("stat", name)
                for k in range(nk):
                    pe.wait_ge(*E.next("squares_ready"))
                    for ci, (c0, n) in enumerate(chunks):
                        ins = mm(ps[:, ci * 512:ci * 512 + n], C("ones"), sq[:, k % slots, c0:c0 + n],
                                 k == 0, k == nk - 1)
                    if k < nk - 1:
                        ins.then_inc(sem("squares_used"), 1)
                ins.then_inc(psum_full, 1)

            def rotations(name, rot, src, tiles, M=P):
                for t in tiles:
                    ps = group("rot", *name, t)
                    ins = mm(ps[0:M, 0:SEQ], rot[0:M, 0:M], src(t), True, True)
                    ins.then_inc(psum_full, 1)

            def attention(name, score, value, pw):
                pP, pT, pO_ = pw
                us = units(ATT[name])
                nq = len(ATT[name])

                def scores(i):
                    ps = group("S", name, i)
                    mms = score(ps, *us[i])
                    for n, (o, a, b, st, sp) in enumerate(mms):
                        ins = mm(o, a, b, st, sp)
                    ins.then_inc(psum_full, 1)

                def turn(i):
                    pe.wait_ge(*E.taken("S", name, i))
                    ps = group("T", name, i)
                    _, tiles = spans(name, us[i][2])
                    for b in range(len(tiles)):
                        ins = flip(ps[:, b * P:(b + 1) * P], pP[:, i % 2, b * P:(b + 1) * P])
                    ins.then_inc(psum_full, 1)

                def outputs(i):
                    pe.wait_ge(*E.taken("T", name, i))
                    t, hh, qi = us[i]
                    o = psum[:, (6 + t % 2) * 512 + qi * P + hh * 64:(6 + t % 2) * 512 + qi * P + hh * 64 + 64]
                    _, tiles = spans(name, qi)
                    for b, kt in enumerate(tiles):
                        ins = mm(o, pT[:, i % 2, b * P:(b + 1) * P], value(t, hh, kt), b == 0,
                                 b == len(tiles) - 1)
                    ins.then_inc(sem("outputs_done"), 1)

                def back(t):
                    pe.wait_ge(*E.next("outputs_scaled"))
                    ps = group("O", name, t)
                    for qi in range(nq):
                        ins = flip(ps[:, qi * P:(qi + 1) * P], pO_[:, t % 2, qi * P:(qi + 1) * P])
                    ins.then_inc(psum_full, 1)

                scores(0)
                for i in range(len(us)):
                    if i + 1 < len(us):
                        scores(i + 1)
                    turn(i)
                    if i >= 1:
                        outputs(i - 1)
                    if i >= 2 * nq + 2 and (i - 2) % (2 * nq) == 0:
                        back((i - 2) // (2 * nq) - 1)
                outputs(len(us) - 1)
                back(3)

            def merge(key, chunks, ys, tags, src0=0):
                for f in range(0, KT, 2):
                    for b in range(3):
                        for g in (f, f + 1):
                            project_tile(("gate", *tags, b, g), ("gate", key, b, g), chunks)
                        w = split(weights("branch", *tags, b, f), a=4)
                        for i, g in enumerate((f, f + 1)):
                            project(("branch", key, b, g), w[:, :, i * P:(i + 1) * P], ys[b], 4, chunks,
                                    src0=src0)
                        done()

            def w_out(key, tiles, chunks):
                pe.wait_ge(*E.next("merged_ready", KT))
                for f in range(KT):
                    w = split(weights(*tiles(f)), a=KT)
                    project(("out", key, f), w, mMG, KT, chunks)
                    done()

            pe.wait_ge(*E.next("cond_ready"))
            modulation("mod1", [("mod", i) for i in range(48)], cond)
            statistics("mix", KT, ALL, nSq)
            pe.wait_ge(*E.next("hidden_ready", KT))
            for t in range(4):
                project_tile(("q_r", t), ("q_r", t), IMG)
            for t in range(4):
                project_tile(("k_r", t), ("k_r", t), ALL)
            for t in range(4):
                pe.wait_ge(*E.taken("q_r", t))
            rotations(("q_r",), C("rot_r"), lambda t: rQ[:, t, :], range(4))
            for t in range(4):
                pe.wait_ge(*E.taken("k_r", t))
            rotations(("k_r",), C("rot_r"), lambda t: rK[:, t, CTX:TOK], range(4))
            project_tokens([("v_r", i) for i in range(4)], ("v_r",), H3)
            for t in range(4):
                project_tile(("g_r", t), ("g_r", t), IMG)
            pe.wait_ge(*E.next("rotated", 8))
            for t in range(TT):
                pe.wait_ge(*E.taken("v_r", t))

            def ret_scores(h):
                for pr in range(3):
                    ps = group("rS", h, pr)
                    for i in range(2):
                        kt = 2 * pr + i
                        ins = mm(ps[:, i * 512:(i + 1) * 512], rK[:, h, kt * P:(kt + 1) * P], rQ[:, h, :],
                                 True, True)
                    ins.then_inc(psum_full, 1)

            def ret_values(h):
                ps = group("rY", h)
                for pr in range(3):
                    pe.wait_ge(*E.taken("rS", h, pr))
                    n = 3 * h + pr
                    for i in range(2):
                        kt = 2 * pr + i
                        ins = mm(ps[:, 0:SEQ], rV[:, kt, h * P:(h + 1) * P], rP[:, n % 4, i * 512:(i + 1) * 512],
                                 kt == 0, kt == TT - 1)
                ins.then_inc(psum_full, 1)

            for h in range(4):
                ret_scores(h)
                ret_values(h)
            for kind in ("mean", "var"):
                for h in range(4):
                    if kind == "mean":
                        pe.wait_ge(*E.taken("rY", h))
                        src = A3[:, h, :]
                    else:
                        pe.wait_ge(*E.next("squares_ready"))
                        src = rSq[:, h, :]
                    ps = group("r" + kind, h)
                    ins = mm(ps[:, 0:SEQ], C("ones"), src, True, True)
                    ins.then_inc(psum_full, 1)
            for t in range(4):
                project_tile(("q_w", t), ("q_w", t), IMG)
            project_tile(("k_w", 0), ("k_w",), ALL)
            w = split(weights("v_w", 0), a=KT)
            ps = group("v_w")
            for t in range(TT):
                for k in range(KT):
                    ins = mm(ps[:, t * P:(t + 1) * P], H3[:, k, t * P:(t + 1) * P], w[:, k, :], k == 0,
                             k == KT - 1)
            ins.then_inc(psum_full, 1)
            done()
            for t in range(4):
                pe.wait_ge(*E.taken("q_w", t))
            rotations(("q_w",), C("rot_w"), lambda t: wQ[:, t, :], range(4))
            pe.wait_ge(*E.taken("k_w"))
            rotations(("k_w",), C("rot_w"), lambda t: wK[:, CTX:TOK], range(1))
            pe.wait_ge(*E.next("rotated", 5))
            pe.wait_ge(*E.taken("v_w"))

            def win_score(ps, t, hh, qi):
                L, tiles = spans("win", qi)
                q = wQ[hh * 64:hh * 64 + 64, t, qi * P:(qi + 1) * P]
                k = wK[hh * 64:hh * 64 + 64, :]
                lo = tiles[0] * P
                r = [(ps[:, 512 - L:512], q, k[:, lo:lo + L], True, False)]
                if qi > 0:
                    r.append((ps[:, 512 - L:512 - L + P], C("ident"), C("wleft"), False, qi == 3))
                if qi < 3:
                    r.append((ps[:, 512 - P:512], C("ident"), C("wright"), False, True))
                r.append((ps[:, 512:768], q, k[:, 0:CTX], True, True))
                return r

            attention("win", win_score, lambda t, hh, kt: wV[:, kt, hh * 64:hh * 64 + 64], attn_area(AT1))
            for t in range(4):
                project_tile(("q_n", t), ("q_n", t), IMG)
            for t in range(4):
                project_tile(("k_n", t), ("k_n", t), ALL)
            project_tokens([("v_n", i) for i in range(4)], ("v_n",), H3)
            for t in range(4):
                pe.wait_ge(*E.taken("q_n", t))
                pe.wait_ge(*E.taken("k_n", t))
            for t in range(TT):
                pe.wait_ge(*E.taken("v_n", t))
            pe.wait_ge(*E.next("bias_ready", 8))

            def na_score(ps, t, hh, qi):
                q = nQ[hh * 64:hh * 64 + 64, t, qi * P:(qi + 1) * P]
                k = nK[hh * 64:hh * 64 + 64, t, :]
                a0 = 6 - 2 * qi
                return [(ps[:, 0:512], q, k[:, CTX:TOK], True, False),
                        (ps[:, 0:512], C("flip"), nB[:, 2 * t + hh, a0 * 64:(a0 + 8) * 64], False, True),
                        (ps[:, 512:768], q, k[:, 0:CTX], True, True)]

            attention("na", na_score,
                      lambda t, hh, kt: nV[:, kt, (2 * t + hh) * 64:(2 * t + hh) * 64 + 64], attn_area(AT2))
            for n in ("win", "na"):
                pe.wait_ge(*E.taken("O", n, 3))
            pe.wait_ge(*E.next("retention_ready", 4))
            merge(0, IMG, [split(Y, a=4) for Y in (YA, YB, YC)], (), src0=CTX)
            w_out(0, lambda f: ("w_out", f), IMG)
            statistics("ffn", KT, IMG, nSq)
            pe.wait_ge(*E.next("hidden_ready", KT))
            for tt in range(4):
                ps = group("HT", tt)
                for k in range(KT):
                    ins = flip(ps[:, k * P:(k + 1) * P], H3[:, k, CTX + tt * P:CTX + (tt + 1) * P])
                    if k == 0:
                        refill(ins)
                ins.then_inc(psum_full, 1)
            pe.wait_ge(*E.next("router_loaded", 16))
            ps = group("router")
            for tt in range(4):
                for k in range(KT):
                    ins = mm(ps[:, tt * NE:(tt + 1) * NE], H3[:, k, CTX + tt * P:CTX + (tt + 1) * P], eWR[:, k, :],
                             k == 0, k == KT - 1)
            ins.then_inc(psum_full, 1)
            pe.wait_ge(*E.next("router_softmax"))
            ps = group("affT")
            for tt in range(4):
                ins = flip(ps[0:NE, tt * P:(tt + 1) * P], aff[:, tt, :])
            ins.then_inc(psum_full, 1)
            pe.wait_ge(*E.next("slots_ready"))
            ps = group("pos")
            for tt in range(4):
                ins = nc.tensor.transpose(ps[:, tt * NE:(tt + 1) * NE], eC[0:NE, tt * P:(tt + 1) * P],
                                          C("ident")[0:NE, 0:NE])
            ins.then_inc(psum_full, 1)
            pe.wait_ge(*E.next("assigned", 4))
            for q in range(4):
                ps = group("PG", q)
                for i in range(2):
                    for tt in range(4):
                        j = 2 * q + i
                        ins = flip(ps[:, i * 512 + tt * P:i * 512 + (tt + 1) * P], ePg[:, tt, j * P:(j + 1) * P])
                ins.then_inc(psum_full, 1)
            for q in range(4):
                pe.wait_ge(*E.taken("PG", q))
                pe.wait_ge(*E.taken("HT", q))
            while state["g"] % 3:
                ps = group("pad", state["g"])
                ins = mm(ps[:, 0:2], C("ident"), C("ident")[:, 0:2], True, True)
                ins.then_inc(psum_full, 1)
            assert state["owed"] == 0 and state["tile"] % 2 == 0, state
            assert state["ended"] == state["tile"]
            with pe.Fori(0, PAIRS) as it:
                E.begin(it, {"groups": 6, "slot": 2, "ring": 16 * 4})
                ps = group("XE")
                for k in range(KT):
                    for tt in range(4):
                        ins = mm(ps[:, k * P:(k + 1) * P], eHT[:, tt, k * P:(k + 1) * P],
                                 eP[:, tt, bass.ds(it * P, P)], tt == 0, tt == 3)
                ins.then_inc(psum_full, 1)
                pe.wait_ge(*E.taken("XE"))
                for e in range(2):
                    ps = group("GU", e)
                    for u, kind in enumerate(("exp_gate", "exp_up")):
                        for f in range(KT):
                            w = split(weights((kind, 0, e), f), a=KT)
                            for k in range(KT):
                                ins = mm(ps[:, u * 512 + f * 64:u * 512 + f * 64 + 64], w[:, k, :],
                                         eXE[:, k, e * 64:(e + 1) * 64], k == 0, k == KT - 1)
                                if k == 0:
                                    refill(ins)
                            done()
                    ins.then_inc(psum_full, 1)
                for e in range(2):
                    pe.wait_ge(*E.taken("GU", e))
                    ps = group("DN", e)
                    for f in range(KT):
                        w = split(weights(("exp_down", 0, e), f), a=KT)
                        for k in range(KT):
                            ins = mm(ps[:, f * 64:f * 64 + 64], w[:, k, :], eHID[:, e, k * 64:(k + 1) * 64],
                                     k == 0, k == KT - 1)
                            if k == 0:
                                refill(ins)
                        done()
                    ins.then_inc(psum_full, 1)
                for e in range(2):
                    pe.wait_ge(*E.taken("DN", e))
                ps = group("YE")
                for f in range(KT):
                    ins = flip(ps[:, f * P:(f + 1) * P], eYT[:, f, :])
                    if f == 0:
                        refill(ins)
                ins.then_inc(psum_full, 1)
                assert state["owed"] == 0
                E.end(PAIRS)
            state["g"] += 6 * (PAIRS - 1)
            for n in [k for k in group_no if k[0] in ("XE", "GU", "DN", "YE")]:
                group_no[("last",) + n] = group_no[n] + 6 * (PAIRS - 1)
            state["tile"] += 48 * (PAIRS - 1)
            state["ended"] = state["tile"]
            pe.wait_ge(*E.taken("last", "YE"))
            for q in range(4):
                ps = group("comb", q)
                for i in range(2):
                    f = 2 * q + i
                    for j in range(PAIRS):
                        ins = mm(ps[:, i * 512:(i + 1) * 512], eYE[:, j, f * P:(f + 1) * P], ePG[:, j, :],
                                 j == 0, j == PAIRS - 1)
                ins.then_inc(psum_full, 1)
            statistics("final", KT, IMG, nSq)
            for l in LAYERS:
                own = ALL if l == 0 else IMG
                if l == 0:
                    pe.wait_ge(*E.next("cond2_ready"))
                modulation(("mod2", l), [(("mod2", l), i) for i in range(24)], cond2)
                statistics(("pre", l), KT, ALL, nSq)
                pe.wait_ge(*E.next("hidden_ready", KT))
                for t in range(2):
                    project_tile((("gq", l), t), ("gq", l, t), own)
                for t in range(2):
                    project_tile((("gk", l), t), ("gk", l, t), ALL)
                project_tokens([(("gv", l), i) for i in range(4)], ("gv", l), H3)
                project_tile(("small", l), ("small", l), ALL)
                w2 = weights("decay_w2", l)
                pe.wait_ge(*E.taken("small", l))
                for d in range(2):
                    for t in range(2):
                        ps = group("decay", l, d, t)
                        for ci, (c0, n) in enumerate(ALL):
                            ins = mm(ps[:, ci * 512:ci * 512 + n], w2[32 * d:32 * d + 16, t * P:(t + 1) * P],
                                     gSM[32 * d:32 * d + 16, c0:c0 + n], True, True)
                        ins.then_inc(psum_full, 1)
                done()
                pe.wait_ge(*E.next("decayed_keys", 2))
                for d in range(2):
                    for cp in range(3):
                        ps = group("KT", l, d, cp)
                        for i in range(2):
                            for t in range(2):
                                c = 2 * cp + i
                                ins = flip(ps[:, (2 * i + t) * P:(2 * i + t + 1) * P],
                                           gT1[:, 2 * d + t, c * P:(c + 1) * P])
                        ins.then_inc(psum_full, 1)
                for t in range(TT):
                    pe.wait_ge(*E.taken("gv", l, t))
                for d in range(2):
                    for cp in range(3):
                        pe.wait_ge(*E.taken("KT", l, d, cp))
                for d, order in enumerate(SCAN):
                    for c in order[:-1]:
                        ps = group("U", l, d, c)
                        for h in range(4):
                            hp = 64 * (h % 2)
                            at = d * 1536 + c * 256 + (h // 2) * P + hp
                            ins = mm(ps[hp:hp + 64, (h // 2) * P:(h // 2 + 1) * P], gKT[:, at:at + 64],
                                     gV[:, c, h * P:(h + 1) * P], True, True)
                        ins.then_inc(psum_full, 1)
                for d in range(2):
                    pe.wait_ge(*E.taken("U", l, d, SCAN[d][-2]))
                for c in OWN_CHUNKS[l]:
                    QI, QS, KS, AT = gChunk(c % 2)
                    pe.wait_ge(*E.next("chunk_operands"))
                    ps = group("A", l, c)
                    for d in range(2):
                        for h in range(4):
                            hp = 64 * (h % 2)
                            for s in range(4):
                                at = (h % 2) * 512 + (2 * d + h // 2) * P + s * 32
                                ins = mm(ps[:, at:at + 32],
                                         KS[hp:hp + 64, d, h // 2, s, :],
                                         QS[hp:hp + 64, 2 * d + h // 2, s * 32:(s + 1) * 32], True, True)
                    ins.then_inc(psum_full, 1)
                    pe.wait_ge(*E.next("chunk_weights"))
                    ps = group("Y", l, c)
                    for h in range(4):
                        hp = 64 * (h % 2)
                        terms = [(gV[:, c, h * P:(h + 1) * P], AT[:, 0, h * P:(h + 1) * P])]
                        for d in range(2):
                            if c != SCAN[d][0]:
                                terms.append((gS[hp:hp + 64, d, c, h // 2, :],
                                              QI[hp:hp + 64, 2 * d + h // 2, :]))
                        for n, (a, b) in enumerate(terms):
                            at = (h % 2) * 512 + (h // 2) * P
                            ins = mm(ps[:, at:at + P], a, b, n == 0, n == len(terms) - 1)
                    ins.then_inc(psum_full, 1)
                for h in range(4):
                    statistics(("gla", l, h), 1, own, gSq[:, h:h + 1, :])
                for t in range(4):
                    project_tile((("ggate", l), t), ("ggate", l, t), own)
                for t in range(2):
                    project_tile((("mq", l), t), ("mq", l, t), own)
                project_tile((("mkv", l), 0), ("mkv", l), ALL)
                for t in range(2):
                    pe.wait_ge(*E.next("squares_ready"))
                    if t == 0:
                        ps = group("stat", ("qn", l))
                    for ci, (c0, n) in enumerate(own):
                        ins = mm(ps[:, ci * 512:ci * 512 + n], C("ones"), mSq[:, 0, c0:c0 + n],
                                 t == 0, t == 1)
                    if t == 0:
                        ins.then_inc(sem("squares_used"), 1)
                ins.then_inc(psum_full, 1)
                statistics(("kvn", l), 1, ALL, mSq)
                pe.wait_ge(*E.next("rank_norms", 3))
                for hb in (0, 4):
                    w = weights("uq", l, hb)[:, 0:768].rearrange("p (a n) -> p a n", a=2)
                    for h in range(hb, hb + 4):
                        project(("uq", l, h), w[:, :, (h - hb) * 96:(h - hb + 1) * 96], mRaw, 2, own, M=96)
                    done()
                w = weights("ukv", l)
                kv1 = mKV.rearrange("p (a n) -> p a n", a=1)
                for h in range(8):
                    project(("uk", l, h), w[:, h * 64:(h + 1) * 64].rearrange("p (a n) -> p a n", a=1),
                            kv1, 1, ALL, M=64)
                for t in range(TT):
                    ps = group("uv", l, t)
                    ins = mm(ps[:, 0:512], mKV[:, t * P:(t + 1) * P], w[:, 512:1024], True, True)
                    ins.then_inc(psum_full, 1)
                done()
                for h in range(8):
                    pe.wait_ge(*E.taken("uq", l, h))
                rotations(("uq", l), C("rot_m"), lambda h: mQ[0:96, h, CTX:TOK], range(8), M=96)
                ps = group("rot", "kr", l)
                ins = mm(ps[64:96, 0:SEQ], C("rot_m")[64:96, 64:96], mKR[64:96, CTX:TOK], True, True)
                ins.then_inc(psum_full, 1)
                pe.wait_ge(*E.next("rotated", 8))
                pe.wait_ge(*E.next("keys_complete", 8))
                for t in range(TT):
                    pe.wait_ge(*E.taken("uv", l, t))

                def mla_score(q0, whole):
                    def score(ps, t, hh, qi):
                        h = 2 * t + hh
                        q = mQ[0:96, h, q0 + qi * P:q0 + (qi + 1) * P]
                        r = [(ps[:, 0:512], q, mK[0:96, h, CTX:TOK], True, True)] if whole else []
                        return r + [(ps[:, 512:768], q, mK[0:96, h, 0:CTX], True, True)]
                    return score

                mla_value = lambda t, hh, kt: mV[:, kt, (2 * t + hh) * 64:(2 * t + hh) * 64 + 64]
                attention(("mla", l), mla_score(CTX, True), mla_value, attn_area(MW))
                if l == 0:
                    attention(("mlac", 0), mla_score(0, False), mla_value, attn_area(MW))
                for t in range(4):
                    project_tile((("mgate", l), t), ("mgate", l, t), own)
                for g in range(4):
                    project_tile((("px", l, g), 0), ("px", l, g), own)
                    project_tile((("pgate", l, g), 0), ("pgate", l, g), own)
                w = split(weights("pool_w", l)[:, 0:512], a=4)
                for g in range(4):
                    pe.wait_ge(*E.next("pooled"))
                    ps = group("mixed", l, g)
                    for ci, (c0, n) in enumerate(own):
                        ins = mm(ps[:, ci * 512:ci * 512 + n], w[:, g, :], pO[:, g, c0:c0 + n], True, True)
                    ins.then_inc(psum_full, 1)
                done()
                pe.wait_ge(*E.next("branches_ready", 4))
                merge(("l", l), own, [YM, YP, YG], (l,))
                w_out(("l", l), lambda f: (("w_out", l), f), own)
                statistics(("post", l), KT, own, nSq)
            assert state["tile"] == len(plan)
            totals["groups"] = state["g"]


        @block.scalar
        def _(act):
            E = Eng(act, "act")
            act_ = nc.scalar.activation

            def squares(src, nk, sq, view=lambda a: a, slots=3, before=None):
                for k in range(nk):
                    if before:
                        before(k)
                    if k >= slots:
                        act.wait_ge(*E.next("squares_used"))
                    act_(view(sq[:, k % slots, :]), view(src[:, k, :]), ACT.Square)\
                        .then_inc(*E.sig("squares_ready"))
                if nk > slots:
                    act.wait_ge(*E.next("squares_used", slots - 1))

            def root(rs, need="var_ready"):
                act.wait_ge(*E.next(need))
                act_(rs, rs, ACT.Sqrt).then_inc(*E.sig("std_ready"))

            def shift_in(mod, col, chunks):
                for k in range(KT):
                    act.wait_ge(*E.next("scaled_ready"))
                    if chunks is ALL:
                        act_(H3[:, k, 0:CTX], H3[:, k, 0:CTX], ACT.Identity, bias=mod[:, col + k, 1:2])
                    act_(H3[:, k, CTX:TOK], H3[:, k, CTX:TOK], ACT.Identity, bias=mod[:, col + k, 0:1])\
                        .then_inc(*E.sig("hidden_ready"))

            def evac(name, dst, chunks=None, n=None, func=ACT.Copy, parts=(0, P), **kw):
                act.wait_ge(*E.written(*name))
                ps = cols(*name)[parts[0]:parts[1], :]
                src = ps[:, 0:n] if chunks is None else bank_view(ps, chunks)
                act_(dst, src, func, **kw).then_inc(*E.read(*name))

            def attention(name, pw, sink=False, before=None):
                pP, pT, _ = pw
                us = units(ATT[name])
                base = unit_base[name]

                def exps(i):
                    t, hh, qi = us[i]
                    L, _ = spans(name, qi)
                    col = (t % 2) * 8 + qi * 2 + hh
                    act.wait_ge(*E.next("negmax_ready"))
                    if sink:
                        h = t + 4 * hh
                        act_(esink[:, col:col + 1], negmax[:, col:col + 1], ACT.Exp,
                             bias=Pm("sink")[:, h:h + 1])
                    if i >= 2:
                        act.wait_ge(*E.written("T", name, i - 2))
                    elif before:
                        act.wait_ge(*E.written("T", before, 8 * len(ATT[before]) - 1))
                    act.wait_ge(*E.written("S", name, i))
                    ps = cols("S", name, i)
                    act_(pP[:, i % 2, 0:L + CTX], ps[:, 512 - L:768], ACT.Exp,
                                bias=negmax[:, col:col + 1], accum_out=sums[:, col:col + 1]).then_inc(*E.read("S", name, i))

                exps(0)
                for i in range(len(us)):
                    if i + 1 < len(us):
                        exps(i + 1)
                    if i % 2:
                        act.wait_ge(*E.written("T", name, i))
                        ps = cols("T", name, i)
                        n = len(spans(name, us[i][2])[1]) * P
                        if base + i > 1:
                            act.wait_ge(*E.upto("outputs_done", base + i - 1))
                        act_(pT[:, i % 2, 0:n], ps[:, 0:n], ACT.Copy).then_inc(*E.read("T", name, i))

            def gates(key, chunks):
                base = E.seen.get("merged_ready", 0)
                for f in range(0, KT, 2):
                    if f:
                        act.wait_ge(*E.upto("merged_ready", base + f))
                    for b in range(3):
                        for g in (f, f + 1):
                            evac(("gate", key, b, g), tok_view(mSG[:, 2 * b + g % 2, :], chunks),
                                 chunks, func=ACT.Sigmoid)
                act.wait_ge(*E.upto("merged_ready", base + KT))

            act.wait_ge(*E.next("params_loaded", 16))
            act_(cond.rearrange("p a b -> p (a b)"), Pm("cond"), ACT.Silu).then_inc(*E.sig("cond_ready"))
            act_(cond2.rearrange("p a b -> p (a b)"), Pm("cond2"), ACT.Silu).then_inc(*E.sig("cond2_ready"))
            act_(lt1, Pm("decay"), ACT.Abs).then_inc(*E.sig("act_step"))
            act.wait_ge(*E.own())
            act_(lt2, lt1, ACT.Exp, scale=-1.0).then_inc(*E.sig("act_step"))
            act.wait_ge(*E.own())
            act_(lt1, lt2, ACT.Ln, bias=1.0).then_inc(*E.sig("decay_ln"))
            act.wait_ge(*E.next("residual_loaded", 16))
            squares(R3, KT, nSq)
            root(nRs)
            shift_in(modA, 0, ALL)
            for t in range(4):
                evac(("q_r", t), rQ[:, t, :], IMG)
            for t in range(4):
                evac(("k_r", t), tok_view(rK[:, t, :], ALL), ALL)
            for t in range(TT):
                evac(("v_r", t), rV[:, t, :], n=512)
            for t in range(4):
                evac(("g_r", t), rSG[:, t, :], IMG, func=ACT.Silu)
            for h in range(4):
                act.wait_ge(*E.next("exponent_ready"))
                e = rE if h % 2 == 0 else YC[:, 0:DW]
                act_(e, e, ACT.Exp).then_inc(*E.sig("decay_ready"))
                if h:
                    evac(("rY", h - 1), A3[:, h - 1, :], n=512)
            evac(("rY", 3), A3[:, 3, :], n=512)
            for h in range(4):
                act.wait_ge(*E.taken("rmean", h))
                act_(rSq[:, h, :], A3[:, h, :], ACT.Square).then_inc(*E.sig("squares_ready"))
            for h in range(4):
                act.wait_ge(*E.taken("rvar", h))
                act_(rRs[:, h, :], rRs[:, h, :], ACT.Sqrt).then_inc(*E.sig("std_ready"))
            act.wait_ge(*E.own())
            act_(tick[:, 0:1], C("eps"), ACT.Copy).then_inc(*E.sig("act_stage_done"))
            act.wait_ge(*E.next("dve_stage_done"))
            act.wait_ge(*E.next("pool_stage_done"))
            for t in range(4):
                evac(("q_w", t), wQ[:, t, :], IMG, scale=0.125)
            evac(("k_w",), tok_view(wK, ALL), ALL)
            evac(("v_w",), wV.rearrange("p a n -> p (a n)"), n=TOK)
            attention("win", attn_area(AT1), sink=True)
            act.wait_ge(*E.own())
            act_(tick[:, 0:1], C("eps"), ACT.Copy).then_inc(*E.sig("act_stage_done"))
            act.wait_ge(*E.next("dve_stage_done"))
            act.wait_ge(*E.next("pool_stage_done"))
            for t in range(4):
                evac(("q_n", t), nQ[:, t, :], IMG, scale=0.125)
            for t in range(4):
                evac(("k_n", t), tok_view(nK[:, t, :], ALL), ALL)
            for t in range(TT):
                evac(("v_n", t), nV[:, t, :], n=512)
            attention("na", attn_area(AT2))
            act.wait_ge(*E.own())
            act_(tick[:, 0:1], C("eps"), ACT.Copy).then_inc(*E.sig("act_stage_done"))
            act.wait_ge(*E.next("dve_stage_done"))
            act.wait_ge(*E.next("pool_stage_done"))
            gates(0, IMG)
            img = lambda a: a[:, CTX:TOK]
            squares(R3, KT, nSq, img, before=lambda k: act.wait_ge(*E.next("residual_ready")))
            root(img(nRs))
            shift_in(modA, 24, IMG)
            act.wait_ge(*E.own())
            act_(tick[:, 0:1], C("eps"), ACT.Copy).then_inc(*E.sig("act_stage_done"))
            act.wait_ge(*E.next("dve_stage_done"))
            act.wait_ge(*E.next("pool_stage_done"))
            for tt in (0, 2):
                evac(("HT", tt), eHT[:, tt, :], n=1024)
            act.wait_ge(*E.next("router_max"))
            act.wait_ge(*E.written("router"))
            ps = cols("router")
            for tt in range(4):
                ins = act_(aff[:, tt, :], ps[:, tt * NE:(tt + 1) * NE], ACT.Exp, bias=m16[:, tt:tt + 1],
                           accum_out=s16[:, tt:tt + 1])
            ins.then_inc(*E.read("router"))
            for q in (0, 2):
                evac(("PG", q), ePG[:, 2 * q:2 * q + 2, :].rearrange("p a n -> p (a n)"), n=1024)
            with act.Fori(0, PAIRS) as it:
                E.begin(it, {"groups": 6, "slot": 2})
                evac(("XE",), eXE.rearrange("p a n -> p (a n)"), n=1024)
                for e in range(2):
                    act.wait_ge(*E.written("GU", e))
                    ps = cols("GU", e)
                    act_(eSG[:, e, :], ps[:, 0:512], ACT.Silu).then_inc(*E.sig("gate_silu"))
                act.wait_ge(*E.written("YE"))
                ps = cols("YE")
                act_(arena[:, bass.ds(it * D + (XP + 8192), D)], ps[:, 0:D], ACT.Copy).then_inc(*E.read("YE"))
                E.end(PAIRS)
            squares(R3, KT, nSq, img, before=lambda k: act.wait_ge(*E.next("residual_ready")))
            root(img(nRs))
            for l in LAYERS:
                own = ALL if l == 0 else IMG
                view = (lambda a: a) if l == 0 else img
                if l == 0:
                    act.wait_ge(*E.next("ctx2_loaded", 16))
                    act.wait_ge(*E.next("residual_ready", KT))
                    squares(R3, KT, nSq)
                else:
                    squares(R3, KT, nSq, before=lambda k: act.wait_ge(*E.next("residual_updated")))
                root(nRs)
                shift_in(modB, 0, ALL)
                for t in range(2):
                    evac(("gq", l, t), tok_view(gQ[:, t, :], own), own, scale=0.125)
                for t in range(2):
                    evac(("gk", l, t), tok_view(gK[:, t, :], ALL), ALL)
                for t in range(TT):
                    evac(("gv", l, t), gV[:, t, :], n=512)
                evac(("small", l), tok_view(gSM, ALL), ALL)
                for d in range(2):
                    for t in range(2):
                        act.wait_ge(*E.written("decay", l, d, t))
                        ps = cols("decay", l, d, t)
                        bias = Pm(("afb", "abb")[d] + str(l))[:, t:t + 1]
                        act_(tok_view(gT1[:, 2 * d + t, :], ALL), bank_view(ps, ALL), ACT.Abs, bias=bias)\
                            .then_inc(*E.sig("decay_abs"))
                flat = gT1.rearrange("p a n -> p (a n)")
                act.wait_ge(*E.next("decay_abs", 4))
                act_(flat, flat, ACT.Exp, scale=-1.0).then_inc(*E.sig("act_step"))
                act.wait_ge(*E.own())
                act_(flat, flat, ACT.Ln, bias=1.0).then_inc(*E.sig("gla_ln"))
                act.wait_ge(*E.next("scans_ready"))
                last = gB.rearrange("p a (c n) -> p (a c) n", n=P)[:, :, P - 1:P]
                act_(expT.rearrange("p (a b) -> p a b", b=1), last, ACT.Exp, scale=1.0 / 16)\
                    .then_inc(*E.sig("chunk_decay_ready"))
                act.wait_ge(*E.next("key_exponents"))
                act_(flat, flat, ACT.Exp, scale=1.0 / 16).then_inc(*E.sig("key_decays"))
                for d in range(2):
                    for cp in range(3):
                        at = d * 1536 + cp * 512
                        evac(("KT", l, d, cp), gKT[:, at:at + 512], n=512)

                def chunk_exps(c):
                    QI, QS, KS, _ = gChunk(c % 2)
                    act.wait_ge(*E.next("chunk_exponents"))
                    act_(QS, QS, ACT.Exp, scale=1.0 / 16)
                    ks = KS.rearrange("p d t s n -> p (d t s n)")
                    act_(ks, ks, ACT.Exp, scale=1.0 / 16)
                    act_(QI, gB[:, :, c * P:(c + 1) * P], ACT.Exp, scale=1.0 / 16)\
                        .then_inc(*E.sig("chunk_decays"))

                chunk_exps(OWN_CHUNKS[l][0])
                for c in OWN_CHUNKS[l]:
                    if c + 1 < TT:
                        chunk_exps(c + 1)
                    act.wait_ge(*E.written("Y", l, c))
                    ps = cols("Y", l, c)
                    y = YG[:, :, c * P:(c + 1) * P].rearrange("p (t b) n -> p t b n", b=2)
                    src = split(ps, b=2)[:, :, 0:256].rearrange("p b (t n) -> p t b n", t=2)
                    act_(y, src, ACT.Copy).then_inc(*E.read("Y", l, c))
                act.wait_ge(*E.taken("Y", l, TT - 1))
                for h in range(4):
                    act_(view(gSq[:, h, :]), view(YG[:, h, :]), ACT.Square).then_inc(*E.sig("squares_ready"))
                for h in range(4):
                    act.wait_ge(*E.taken("stat", ("gla", l, h)))
                    act_(view(gRs[:, h, :]), view(gRs[:, h, :]), ACT.Sqrt).then_inc(*E.sig("std_ready"))
                base = 8 * l
                for t in range(4):
                    if t >= 2:
                        act.wait_ge(*E.upto("silu_used", base + t - 1))
                    evac(("ggate", l, t), tok_view(SILU[:, t % 2, :], own), own, func=ACT.Silu)
                act.wait_ge(*E.own())
                act_(tick[:, 0:1], C("eps"), ACT.Copy).then_inc(*E.sig("act_stage_done"))
                act.wait_ge(*E.next("dve_stage_done"))
                act.wait_ge(*E.next("pool_stage_done"))
                act_(mKR[64:96, :], gSM[64:96, :], ACT.Copy).then_inc(*E.sig("rope_key_ready"))
                act.wait_ge(*E.next("rope_key_ready"))
                for t in range(2):
                    act.wait_ge(*E.written("mq", l, t))
                    ps = cols("mq", l, t)
                    if t:
                        act.wait_ge(*E.next("squares_used"))
                    act_(tok_view(mSq[:, 0, :], own), bank_view(ps, own), ACT.Square)\
                        .then_inc(*E.sig("squares_ready"))
                    evac(("mq", l, t), tok_view(mRaw[:, t, :], own), own)
                root(view(mRs))
                act.wait_ge(*E.written("mkv", l))
                ps = cols("mkv", l)
                act_(tok_view(mSq[:, 0, :], ALL), bank_view(ps, ALL), ACT.Square)\
                    .then_inc(*E.sig("squares_ready"))
                evac(("mkv", l), tok_view(mKV, ALL), ALL)
                root(mRs)
                for h in range(8):
                    evac(("uq", l, h), tok_view(mQ[0:96, h, :], own), own, parts=(0, 96), scale=96 ** -0.5)
                for t in range(TT):
                    evac(("uv", l, t), mV[:, t, :], n=512)
                attention(("mla", l), attn_area(MW))
                if l == 0:
                    attention(("mlac", 0), attn_area(MW), before=("mla", 0))
                act.wait_ge(*E.own())
                act_(tick[:, 0:1], C("eps"), ACT.Copy).then_inc(*E.sig("act_stage_done"))
                act.wait_ge(*E.next("dve_stage_done"))
                act.wait_ge(*E.next("pool_stage_done"))
                base = 8 * l + 4
                for t in range(4):
                    if t >= 2:
                        act.wait_ge(*E.upto("silu_used", base + t - 1))
                    evac(("mgate", l, t), tok_view(mSil[:, t % 2, :], own), own, func=ACT.Silu)
                act.wait_ge(*E.next("pads_zero"))
                base = E.seen.get("pooled", 0)
                for g in range(4):
                    if g >= 2:
                        act.wait_ge(*E.upto("pooled", base + g - 1))
                    act.wait_ge(*E.written("px", l, g))
                    ps = cols("px", l, g)
                    x0 = (g % 2) * (TOK + 32)
                    if l == 0:
                        act_(pX[:, x0 + 8:x0 + 8 + CTX], ps[:, 0:CTX], ACT.Copy)
                        act_(pX[:, x0 + 280:x0 + 408], ps[:, CTX:384], ACT.Copy)
                        act_(pX[:, x0 + 408:x0 + 792], ps[:, 512:896], ACT.Copy).then_inc(*E.read("px", l, g))
                    else:
                        act_(pX[:, x0 + 280:x0 + 792], ps[:, 0:SEQ], ACT.Copy).then_inc(*E.read("px", l, g))
                    evac(("pgate", l, g), tok_view(YP[:, g, :], own), own, func=ACT.Silu)
                act.wait_ge(*E.upto("pooled", base + 4))
                gates(("l", l), own)
                for f in range(KT):
                    evac(("out", ("l", l), f), tok_view(mOUT[:, f, :], own), own)
                act.wait_ge(*E.taken("out", ("l", l), KT - 1))
                squares(mOUT, KT, nSq, view)
                root(view(nRs))

        @block.vector
        def _(dve):
            E = Eng(dve, "dve")
            V = nc.vector
            stt, tt_, ts_ = V.scalar_tensor_tensor, V.tensor_tensor, V.tensor_scalar

            def inverse_std(name, rs, width, chunks, n, mark="var_ready"):
                dve.wait_ge(*E.written("stat", name))
                ps = cols("stat", name)
                dve.wait_ge(*E.own())
                ins = ts_(tok_view(rs, chunks), bank_view(ps, chunks), 1.0 / n, EPS, ALU.mult, ALU.add)
                ins.then_inc(*E.read("stat", name))
                dve.wait_ge(*E.taken("stat", name))
                V.tensor_copy(tick[:, 3:4], rs[:, CTX:CTX + 1]).then_inc(*E.sig(mark))
                dve.wait_ge(*E.next("std_ready"))
                r = rs if chunks is ALL else rs[:, CTX:TOK]
                V.reciprocal(r, r).then_inc(*E.sig("dve_step"))
                dve.wait_ge(*E.own())

            def scale_in(gain, chunks):
                for k in range(KT):
                    if chunks is ALL:
                        stt(H3[:, k, 0:CTX], R3[:, k, 0:CTX], gain(k, 1), nRs[:, 0:CTX], ALU.mult, ALU.mult)
                    stt(H3[:, k, CTX:TOK], R3[:, k, CTX:TOK], gain(k, 0), nRs[:, CTX:TOK],
                        ALU.mult, ALU.mult).then_inc(*E.sig("scaled_ready"))

            def rope(name, x, cos, sin, tmp, mark=True):
                dve.wait_ge(*E.written("rot", *name))
                ps = cols("rot", *name)
                dve.wait_ge(*E.own())
                p0, p1 = (64, 96) if name[0] == "kr" else (0, x.shape[0])
                tt_(tmp, ps[p0:p1, 0:SEQ], sin, ALU.mult).then_inc(*E.read("rot", *name))
                tt_(x, x, cos, ALU.mult).then_inc(*E.sig("dve_step"))
                dve.wait_ge(*E.own())
                dve.wait_ge(*E.taken("rot", *name))
                ins = tt_(x, x, tmp, ALU.add)
                if mark:
                    ins.then_inc(*E.sig("rotated"))
                else:
                    ins.then_inc(*E.sig("dve_step"))
                    dve.wait_ge(*E.own())

            def attention(name, pw, y, col0, sink=False):
                pP, pT, pO_ = pw
                us = units(ATT[name])
                nq, base = len(ATT[name]), unit_base[name]

                def maxes(i):
                    t, hh, qi = us[i]
                    L, _ = spans(name, qi)
                    col = (t % 2) * 8 + qi * 2 + hh
                    dve.wait_ge(*E.written("S", name, i))
                    ps = cols("S", name, i)
                    nm = negmax[:, col:col + 1]
                    ins = V.reduce_max(nm, ps[:, 512 - L:768], AXX, negate=True)
                    if sink:
                        ins.then_inc(*E.sig("dve_step"))
                        dve.wait_ge(*E.own())
                        h = t + 4 * hh
                        ins = V.tensor_scalar_min(nm, nm, nsink[:, h:h + 1])
                    ins.then_inc(*E.sig("negmax_ready"))

                def scale_outputs(t):
                    c0, n = (t % 2) * 8, 2 * nq
                    dve.wait_ge(*E.taken("S", name, 2 * nq * (t + 1) - 1))
                    r = rinv[:, c0:c0 + n]
                    if sink:
                        tt_(r, sums[:, c0:c0 + n], esink[:, c0:c0 + n], ALU.add).then_inc(*E.sig("dve_step"))
                        dve.wait_ge(*E.own())
                        V.reciprocal(r, r).then_inc(*E.sig("dve_step"))
                        dve.wait_ge(*E.own())
                    else:
                        V.reciprocal(r, sums[:, c0:c0 + n]).then_inc(*E.sig("dve_step"))
                        dve.wait_ge(*E.own())
                    dve.wait_ge(*E.upto("outputs_done", base + 2 * nq * (t + 1)))
                    dve.wait_ge(*E.own())
                    if t >= 2:
                        dve.wait_ge(*E.written("O", name, t - 2))
                    o = psum[:, (6 + t % 2) * 512:(6 + t % 2) * 512 + nq * P]
                    tt_(split(pO_[:, t % 2, 0:nq * P], a=n), split(o, a=n),
                        r.unsqueeze(2).to_broadcast([P, n, 64]), ALU.mult).then_inc(*E.sig("outputs_scaled"))

                def collect(t):
                    dve.wait_ge(*E.written("O", name, t))
                    ps = cols("O", name, t)
                    V.tensor_copy(y[:, t, col0:col0 + nq * P], ps[:, 0:nq * P]).then_inc(*E.read("O", name, t))

                maxes(0)
                for i in range(len(us)):
                    if i + 1 < len(us):
                        maxes(i + 1)
                    if i % 2 == 0:
                        dve.wait_ge(*E.written("T", name, i))
                        ps = cols("T", name, i)
                        n = len(spans(name, us[i][2])[1]) * P
                        if base + i > 1:
                            dve.wait_ge(*E.upto("outputs_done", base + i - 1))
                        V.tensor_copy(pT[:, i % 2, 0:n], ps[:, 0:n]).then_inc(*E.read("T", name, i))
                    if i >= 2 * nq + 1 and (i - 1) % (2 * nq) == 0:
                        scale_outputs((i - 1) // (2 * nq) - 1)
                    if i >= 2 * nq + 2 and (i - 2) % (2 * nq) == 0:
                        collect((i - 2) // (2 * nq) - 1)
                scale_outputs(3)
                collect(3)

            def merge(key, chunks):
                for f in range(0, KT, 2):
                    for b in range(3):
                        for g in (f, f + 1):
                            dve.wait_ge(*E.taken("gate", key, b, g))
                            dve.wait_ge(*E.written("branch", key, b, g))
                            ps = cols("branch", key, b, g)
                            o = tok_view(mMG[:, g, :], chunks)
                            to = o if b == 0 else tok_view(mTmp[:, g % 2, :], chunks)
                            dve.wait_ge(*E.own())
                            tt_(to, tok_view(mSG[:, 2 * b + g % 2, :], chunks),
                                       bank_view(ps, chunks), ALU.mult).then_inc(*E.read("branch", key, b, g))
                            dve.wait_ge(*E.taken("branch", key, b, g))
                            if b:
                                ins = tt_(o, o, to, ALU.add)
                                if b == 1:
                                    ins.then_inc(*E.sig("dve_step"))
                                    dve.wait_ge(*E.own())
                                else:
                                    ins.then_inc(*E.sig("merged_ready"))

            def modulation(name, mod, bias, gm, gain):
                dve.wait_ge(*E.written(name))
                ps = cols(name)
                n = mod.shape[1]
                tt_(mod.rearrange("p a b -> p (a b)"), ps[:, 0:2 * n], Pm(bias), ALU.add).then_inc(*E.read(name))
                dve.wait_ge(*E.taken(name))
                stt(gm, mod[:, 8:16, :], 1.0, split(Pm(gain), a=KT), ALU.add, ALU.mult).then_inc(*E.sig("dve_step"))
                dve.wait_ge(*E.own())

            dve.wait_ge(*E.next("params_loaded", 16))
            dve.wait_ge(*E.next("consts_loaded", 16))
            ts_(nsink, Pm("sink"), -1.0, None, ALU.mult)
            dve.wait_ge(*E.next("decay_ln"))
            ts_(lt2, Pm("decay"), 0.0, None, ALU.min).then_inc(*E.sig("dve_step"))
            dve.wait_ge(*E.own())
            tt_(lg, lt2, lt1, ALU.subtract).then_inc(*E.sig("dve_step"))
            dve.wait_ge(*E.own())
            ts_(lg[:, 4:8], lg[:, 4:8], -1.0, None, ALU.mult).then_inc(*E.sig("dve_step"))
            dve.wait_ge(*E.own())
            modulation("mod1", modA, "bmod", gmA, "gmix")
            stt(gmF.rearrange("p (a b) -> p a b", b=1), modA[:, 32:40, 0:1], 1.0,
                       Pm("gffn").rearrange("p (a b) -> p a b", b=1), ALU.add, ALU.mult).then_inc(*E.sig("dve_step"))
            dve.wait_ge(*E.own())
            inverse_std("mix", nRs, TOK, ALL, D)
            dve.wait_ge(*E.next("residual_loaded", 16))
            scale_in(lambda k, c: gmA[:, k, c:c + 1], ALL)
            dve.wait_ge(*E.next("ret_tables_loaded", 16))
            for t in range(4):
                rope(("q_r", t), rQ[:, t, :], rCos, rSin, rTmp[:, 0:512])
            for t in range(4):
                rope(("k_r", t), rK[:, t, CTX:TOK], rCos, rSin, rTmp[:, 0:512])

            def exponents(h):
                e = rE if h % 2 == 0 else YC[:, 0:DW]
                x2 = YB[:, 0:DW]
                dve.wait_ge(*E.own())
                ts_(x2, rDist, 0.0, lg[:, 4 + h:5 + h], ALU.min, ALU.mult)
                ts_(e, rDist, 0.0, lg[:, h:h + 1], ALU.max, ALU.mult).then_inc(*E.sig("dve_step"))
                dve.wait_ge(*E.own())
                tt_(e, e, x2, ALU.add).then_inc(*E.sig("exponent_ready"))

            exponents(0)
            for h in range(4):
                if h < 3:
                    exponents(h + 1)
                dve.wait_ge(*E.next("decay_ready"))
                e = rE if h % 2 == 0 else YC[:, 0:DW]
                dve.wait_ge(*E.own())
                for m in range(2):
                    a, b = 896 - P * m, P - P * m
                    ins = tt_(rCW[:, m, :], e[:, a:a + 512], e[:, b:b + 512], ALU.add)
                ins.then_inc(*E.sig("dve_step"))
                dve.wait_ge(*E.own())
                for pr in range(3):
                    dve.wait_ge(*E.written("rS", h, pr))
                    ps = cols("rS", h, pr)
                    n = 3 * h + pr
                    if n >= 4:
                        dve.wait_ge(*E.written("rY", (n - 4) // 3))
                    for i in range(2):
                        kt = 2 * pr + i
                        w = rCW[:, kt, :] if kt < 2 else e[:, 640 - P * (kt - 2):640 - P * (kt - 2) + 512]
                        ins = stt(rP[:, n % 4, i * 512:(i + 1) * 512], ps[:, i * 512:(i + 1) * 512],
                                  128 ** -0.5, w, ALU.mult, ALU.mult)
                    ins.then_inc(*E.read("rS", h, pr))
            for h in range(4):
                dve.wait_ge(*E.written("rmean", h))
                ps = cols("rmean", h)
                stt(A3[:, h, :], ps[:, 0:512], -1.0 / P, A3[:, h, :], ALU.mult, ALU.add).then_inc(*E.read("rmean", h))
            dve.wait_ge(*E.own())
            for h in range(4):
                dve.wait_ge(*E.written("rvar", h))
                ps = cols("rvar", h)
                ts_(rRs[:, h, :], ps[:, 0:512], 1.0 / P, EPS, ALU.mult, ALU.add).then_inc(*E.read("rvar", h))
            for h in range(4):
                dve.wait_ge(*E.next("std_ready"))
                V.reciprocal(rRs[:, h, :], rRs[:, h, :]).then_inc(*E.sig("dve_step"))
                dve.wait_ge(*E.own())
                stt(A3[:, h, :], A3[:, h, :], Pm("retgn")[:, h:h + 1], rRs[:, h, :], ALU.mult, ALU.mult).then_inc(*E.sig("dve_step"))
                dve.wait_ge(*E.own())
                dve.wait_ge(*E.taken("g_r", h))
                tt_(A3[:, h, :], A3[:, h, :], rSG[:, h, :], ALU.mult).then_inc(*E.sig("retention_ready"))
            dve.wait_ge(*E.own())
            V.memset(tick[:, 1:2], 0.0).then_inc(*E.sig("dve_stage_done"))
            dve.wait_ge(*E.next("act_stage_done"))
            dve.wait_ge(*E.next("pool_stage_done"))
            dve.wait_ge(*E.next("win_tables_loaded", 16))
            for t in range(4):
                rope(("q_w", t), wQ[:, t, :], wCos, wSin, wTmp[:, 0:512])
            rope(("k_w", 0), wK[:, CTX:TOK], wCos, wSin, wTmp[:, 0:512])
            attention("win", attn_area(AT1), split(YB, a=4), 0, sink=True)
            dve.wait_ge(*E.own())
            V.memset(tick[:, 1:2], 0.0).then_inc(*E.sig("dve_stage_done"))
            dve.wait_ge(*E.next("act_stage_done"))
            dve.wait_ge(*E.next("pool_stage_done"))
            attention("na", attn_area(AT2), split(YC, a=4), 0)
            dve.wait_ge(*E.own())
            V.memset(tick[:, 1:2], 0.0).then_inc(*E.sig("dve_stage_done"))
            dve.wait_ge(*E.next("act_stage_done"))
            dve.wait_ge(*E.next("pool_stage_done"))
            merge(0, IMG)
            for f in range(KT):
                dve.wait_ge(*E.written("out", 0, f))
                ps = cols("out", 0, f)
                stt(R3[:, f, CTX:TOK], ps[:, 0:SEQ], modA[:, 16 + f, 0:1], R3[:, f, CTX:TOK],
                           ALU.mult, ALU.add).then_inc(*E.read("out", 0, f))
                dve.wait_ge(*E.taken("out", 0, f))
                V.tensor_copy(tick[:, 4:5], R3[:, f, TOK - 1:TOK]).then_inc(*E.sig("residual_ready"))
            inverse_std("ffn", nRs, SEQ, IMG, D)
            scale_in(lambda k, c: gmF[:, k:k + 1], IMG)
            dve.wait_ge(*E.own())
            V.memset(tick[:, 1:2], 0.0).then_inc(*E.sig("dve_stage_done"))
            dve.wait_ge(*E.next("act_stage_done"))
            dve.wait_ge(*E.next("pool_stage_done"))
            for tt in (1, 3):
                dve.wait_ge(*E.written("HT", tt))
                ps = cols("HT", tt)
                V.tensor_copy(eHT[:, tt, :], ps[:, 0:1024]).then_inc(*E.read("HT", tt))
            dve.wait_ge(*E.written("router"))
            ps = cols("router")
            V.reduce_max(m16, split(ps[:, 0:4 * NE], a=4), AXX, negate=True).then_inc(*E.sig("router_max"))
            dve.wait_ge(*E.taken("router"))
            V.reciprocal(r16, s16).then_inc(*E.sig("dve_step"))
            dve.wait_ge(*E.own())
            tt_(aff, aff, r16.unsqueeze(2).to_broadcast([P, 4, NE]), ALU.mult)\
                .then_inc(*E.sig("router_softmax"))
            dve.wait_ge(*E.written("affT"))
            ps = cols("affT")
            V.tensor_copy(eW[0:NE, 0, :], ps[0:NE, 0:512]).then_inc(*E.read("affT"))
            dve.wait_ge(*E.taken("affT"))
            for n in range(CAP // 8):
                a, b = eW[0:NE, n % 2, :], eW[0:NE, (n + 1) % 2, :]
                V.max(top8[0:NE, :], a).then_inc(*E.sig("dve_step"))
                dve.wait_ge(*E.own())
                V.match_replace(b, top8[0:NE, :], a, -1.0).then_inc(*E.sig("dve_step"))
                dve.wait_ge(*E.own())
            ts_(eM[0:NE, :], eW[0:NE, (CAP // 8) % 2, :], 0.0, None, ALU.is_lt).then_inc(*E.sig("dve_step"))
            dve.wait_ge(*E.own())
            V.memset(eA[0:NE, :], 1.0).then_inc(*E.sig("dve_step"))
            dve.wait_ge(*E.own())
            V.tensor_tensor_scan(eC[0:NE, :], eA[0:NE, :], eM[0:NE, :], 0.0, ALU.mult, ALU.add).then_inc(*E.sig("dve_step"))
            dve.wait_ge(*E.own())
            tt_(eC[0:NE, :], eC[0:NE, :], eM[0:NE, :], ALU.mult).then_inc(*E.sig("dve_step"))
            dve.wait_ge(*E.own())
            V.tensor_scalar_add(eC[0:NE, :], eC[0:NE, :], -1.0).then_inc(*E.sig("slots_ready"))
            dve.wait_ge(*E.written("pos"))
            ps = cols("pos")
            V.tensor_copy(posn, split(ps[:, 0:4 * NE], a=4)).then_inc(*E.read("pos"))
            dve.wait_ge(*E.taken("pos"))
            slots = C("slots").unsqueeze(1).to_broadcast([P, NE, CAP])
            for tt in range(4):
                p3 = split(eP[:, tt, :], a=NE)
                tt_(p3, slots, posn[:, tt, :].unsqueeze(2).to_broadcast([P, NE, CAP]), ALU.is_equal).then_inc(*E.sig("dve_step"))
                dve.wait_ge(*E.own())
                tt_(split(ePg[:, tt, :], a=NE), p3, aff[:, tt, :].unsqueeze(2).to_broadcast([P, NE, CAP]),
                    ALU.mult).then_inc(*E.sig("assigned"))
            for q in (1, 3):
                dve.wait_ge(*E.written("PG", q))
                ps = cols("PG", q)
                V.tensor_copy(ePG[:, 2 * q:2 * q + 2, :].rearrange("p a n -> p (a n)"),
                                     ps[:, 0:1024]).then_inc(*E.read("PG", q))
            for n in [k for k in group_no if k[0] == "pad"]:
                dve.wait_ge(*E.written(*n))
                ps = cols(*n)
                dve.wait_ge(*E.own())
                V.tensor_copy(tick[:, 6:7], ps[:, 0:1]).then_inc(*E.read(*n))
            with dve.Fori(0, PAIRS) as it:
                E.begin(it, {"groups": 6, "slot": 2, "gate_silu": 2})
                for e in range(2):
                    dve.wait_ge(*E.next("gate_silu"))
                    dve.wait_ge(*E.written("GU", e))
                    ps = cols("GU", e)
                    tt_(eHID[:, e, :], eSG[:, e, :], ps[:, 512:1024], ALU.mult).then_inc(*E.read("GU", e))
                for e in range(2):
                    dve.wait_ge(*E.written("DN", e))
                    ps = cols("DN", e)
                    V.tensor_copy(eYT[:, :, e * 64:(e + 1) * 64], split(ps[:, 0:512], a=KT)).then_inc(*E.read("DN", e))
                E.end(PAIRS)
            for q in range(4):
                dve.wait_ge(*E.written("comb", q))
                ps = cols("comb", q)
                for i in range(2):
                    f = 2 * q + i
                    ins = stt(R3[:, f, CTX:TOK], ps[:, i * 512:(i + 1) * 512], modA[:, 40 + f, 0:1],
                              R3[:, f, CTX:TOK], ALU.mult, ALU.add)
                    if i == 0:
                        ins.then_inc(*E.sig("residual_ready"))
                    else:
                        ins.then_inc(*E.read("comb", q))
                        dve.wait_ge(*E.taken("comb", q))
                        V.tensor_copy(tick[:, 4:5], R3[:, f, TOK - 1:TOK]).then_inc(*E.sig("residual_ready"))
            inverse_std("final", nRs, SEQ, IMG, D)
            for k in range(KT):
                stt(R3[:, k, CTX:TOK], R3[:, k, CTX:TOK], Pm("gfinal")[:, k:k + 1], nRs[:, CTX:TOK],
                    ALU.mult, ALU.mult).then_inc(*E.sig("residual_ready"))
            for l in LAYERS:
                own = ALL if l == 0 else IMG
                view = (lambda a: a) if l == 0 else (lambda a: a[:, CTX:TOK])
                L = str(l)
                modulation(("mod2", l), modB, "bmod2" + L, gmB, "pre" + L)
                tt_(pgB, modB[:, 16:24, :], split(Pm("post" + L), a=KT), ALU.mult).then_inc(*E.sig("dve_step"))
                dve.wait_ge(*E.own())
                inverse_std(("pre", l), nRs, TOK, ALL, D)
                if l == 0:
                    dve.wait_ge(*E.next("ctx2_loaded", 16))
                    dve.wait_ge(*E.next("residual_ready", 3 * KT))
                else:
                    dve.wait_ge(*E.next("residual_updated", KT))
                scale_in(lambda k, c: gmB[:, k, c:c + 1], ALL)
                for d in range(2):
                    for t in range(2):
                        dve.wait_ge(*E.next("decay_abs"))
                        dve.wait_ge(*E.written("decay", l, d, t))
                        ps = cols("decay", l, d, t)
                        bias = Pm(("afb", "abb")[d] + L)[:, t:t + 1]
                        ts_(tok_view(gLM[:, 2 * d + t, :], ALL), bank_view(ps, ALL), bias, 0.0,
                                   ALU.add, ALU.min).then_inc(*E.read("decay", l, d, t))
                flat = lambda a: a.rearrange("p a n -> p (a n)")
                dve.wait_ge(*E.next("gla_ln"))
                dve.wait_ge(*E.taken("decay", l, 1, 1))
                tt_(flat(gLM), flat(gLM), flat(gT1), ALU.subtract).then_inc(*E.sig("dve_step"))
                dve.wait_ge(*E.own())
                for a in range(4):
                    for c in range(TT):
                        sl = slice(c * P, (c + 1) * P)
                        ins = V.tensor_tensor_scan(gB[:, a, sl], C("ones"), gLM[:, a, sl], 0.0,
                                                   ALU.mult, ALU.add)
                ins.then_inc(*E.sig("scans_ready"))
                dve.wait_ge(*E.next("scans_ready"))
                dve.wait_ge(*E.next("chunk_decay_ready"))
                chunks = lambda a: a.rearrange("p a (c n) -> p (a c) n", n=P)
                gBc, gTc = chunks(gB), chunks(gT1)
                end = lambda lo, hi, j: gBc[:, lo:hi, j:j + 1].to_broadcast([P, hi - lo, P])
                tt_(gTc[:, 12:24, :], end(12, 24, P - 1), gBc[:, 12:24, :], ALU.subtract).then_inc(*E.sig("dve_step"))
                dve.wait_ge(*E.own())
                tt_(flat(gB[:, 2:4, :]), flat(gT1[:, 2:4, :]), flat(gLM[:, 2:4, :]), ALU.add).then_inc(*E.sig("dve_step"))
                dve.wait_ge(*E.own())
                tt_(gTc[:, 0:12, :], end(0, 12, P - 1), gBc[:, 0:12, :], ALU.subtract)
                tt_(gTc[:, 12:24, :], end(12, 24, 0), gBc[:, 12:24, :], ALU.subtract)\
                    .then_inc(*E.sig("key_exponents"))
                dve.wait_ge(*E.next("key_decays"))
                dve.wait_ge(*E.taken("gk", l, 1))
                for d in range(2):
                    a = flat(gT1[:, 2 * d:2 * d + 2, :])
                    tt_(a, a, flat(gK), ALU.mult).then_inc(*E.sig("decayed_keys"))
                for d, order in enumerate(SCAN):
                    for n, c in enumerate(order[:-1]):
                        dve.wait_ge(*E.written("U", l, d, c))
                        ps = cols("U", l, d, c)
                        to = order[n + 1]
                        if n == 0:
                            ins = V.tensor_copy(gS[:, d, to, :, :], split(ps[:, 0:256], a=2))
                        else:
                            for t in range(2):
                                ins = stt(gS[:, d, to, t, :], gS[:, d, c, t, :],
                                          expT[:, (2 * d + t) * TT + c:(2 * d + t) * TT + c + 1],
                                          ps[:, t * P:(t + 1) * P], ALU.mult, ALU.add)
                        ins.then_inc(*E.read("U", l, d, c))
                        dve.wait_ge(*E.taken("U", l, d, c))

                def chunk_exponents(c):
                    QI, QS, KS, _ = gChunk(c % 2)
                    b = gB[:, :, c * P:(c + 1) * P]
                    b4 = b.rearrange("p a (s n) -> p a s n", s=4)
                    mid = b4[:, :, :, 15:16]
                    dve.wait_ge(*E.own())
                    tt_(QS.rearrange("p a (s n) -> p a s n", s=4), b4, mid.to_broadcast([P, 4, 4, 32]),
                        ALU.subtract)
                    for d in range(2):
                        E_in = mid[:, 2 * d:2 * d + 2, :, :].to_broadcast([P, 2, 4, P])
                        E_b = b[:, 2 * d:2 * d + 2, :].unsqueeze(2).to_broadcast([P, 2, 4, P])
                        ins = tt_(KS[:, d, :, :, :], E_in, E_b, ALU.subtract)
                    ins.then_inc(*E.sig("dve_step"))
                    dve.wait_ge(*E.own())
                    q, k = QS.rearrange("p a n -> p (a n)"), KS.rearrange("p d t s n -> p (d t s n)")
                    V.tensor_scalar_min(q, q, CLAMP)
                    V.tensor_scalar_min(k, k, CLAMP).then_inc(*E.sig("chunk_exponents"))

                def chunk_products(c):
                    QI, QS, KS, _ = gChunk(c % 2)
                    dve.wait_ge(*E.next("chunk_decays"))
                    dve.wait_ge(*E.own())
                    for d in range(2):
                        for X in (QI, QS):
                            x = X[:, 2 * d:2 * d + 2, :]
                            tt_(x, x, gQ[:, :, c * P:(c + 1) * P], ALU.mult)
                        x = KS[:, d, :, :, :]
                        k = gK[:, :, c * P:(c + 1) * P].unsqueeze(2).to_broadcast([P, 2, 4, P])
                        ins = tt_(x, x, k, ALU.mult)
                    ins.then_inc(*E.sig("chunk_operands"))

                dve.wait_ge(*E.taken("gq", l, 1))
                chunk_exponents(OWN_CHUNKS[l][0])
                for c in OWN_CHUNKS[l]:
                    chunk_products(c)
                    if c + 1 < TT:
                        chunk_exponents(c + 1)
                    AT = gChunk(c % 2)[3]
                    dve.wait_ge(*E.own())
                    dve.wait_ge(*E.written("A", l, c))
                    ps = cols("A", l, c)
                    for d, m in enumerate(("upper", "lower")):
                        for b in range(2):
                            o = AT[:, d, :].rearrange("p (t b n) -> p t b n", t=2, b=2)[:, :, b, :]
                            at = b * 512 + d * 256
                            ins = tt_(o, split(ps[:, at:at + 256], t=2),
                                      C(m).unsqueeze(1).to_broadcast([P, 2, P]), ALU.mult)
                    ins.then_inc(*E.read("A", l, c))
                    dve.wait_ge(*E.taken("A", l, c))
                    tt_(AT[:, 0, :], AT[:, 0, :], AT[:, 1, :], ALU.add).then_inc(*E.sig("chunk_weights"))
                for h in range(4):
                    dve.wait_ge(*E.written("stat", ("gla", l, h)))
                    ps = cols("stat", ("gla", l, h))
                    ts_(tok_view(gRs[:, h, :], own), bank_view(ps, own), 1.0 / P, EPS,
                               ALU.mult, ALU.add).then_inc(*E.read("stat", ("gla", l, h)))
                for h in range(4):
                    dve.wait_ge(*E.next("std_ready"))
                    r, y = view(gRs[:, h, :]), view(YG[:, h, :])
                    V.reciprocal(r, r).then_inc(*E.sig("dve_step"))
                    dve.wait_ge(*E.own())
                    stt(y, y, Pm("glan" + L), r, ALU.mult, ALU.mult).then_inc(*E.sig("dve_step"))
                    dve.wait_ge(*E.own())
                for t in range(4):
                    dve.wait_ge(*E.taken("ggate", l, t))
                    y = view(YG[:, t, :])
                    tt_(y, y, view(SILU[:, t % 2, :]), ALU.mult).then_inc(*E.sig("silu_used"))
                dve.wait_ge(*E.own())
                V.memset(tick[:, 1:2], 0.0).then_inc(*E.sig("dve_stage_done"))
                dve.wait_ge(*E.next("act_stage_done"))
                dve.wait_ge(*E.next("pool_stage_done"))
                inverse_std(("qn", l), mRs, 0, own, 256)
                for t in range(2):
                    dve.wait_ge(*E.taken("mq", l, t))
                    x = view(mRaw[:, t, :])
                    stt(x, x, Pm("qnorm" + L)[:, t:t + 1], view(mRs), ALU.mult, ALU.mult)\
                        .then_inc(*E.sig("rank_norms"))
                inverse_std(("kvn", l), mRs, 0, ALL, 128)
                dve.wait_ge(*E.taken("mkv", l))
                stt(mKV, mKV, Pm("kvnorm" + L), mRs, ALU.mult, ALU.mult).then_inc(*E.sig("rank_norms"))
                for h in range(8):
                    dve.wait_ge(*E.written("uk", l, h))
                    ps = cols("uk", l, h)
                    V.tensor_copy(tok_view(mK[0:64, h, :], ALL), bank_view(ps[0:64, :], ALL)).then_inc(*E.read("uk", l, h))
                dve.wait_ge(*E.next("mla_tables_loaded", 16))
                for h in range(8):
                    rope(("uq", l, h), mQ[0:96, h, CTX:TOK], mCos[0:96, :], mSin[0:96, :], mTp[0:96, 0:512])
                dve.wait_ge(*E.next("rope_key_ready"))
                rope(("kr", l), mKR[64:96, CTX:TOK], mCos[64:96, :], mSin[64:96, :], mTp[64:96, 0:512],
                     mark=False)
                for h in range(8):
                    V.tensor_copy(mK[64:96, h, :], mKR[64:96, :]).then_inc(*E.sig("keys_complete"))
                attention(("mla", l), attn_area(MW), YM, CTX)
                if l == 0:
                    attention(("mlac", 0), attn_area(MW), YM, 0)
                dve.wait_ge(*E.own())
                V.memset(tick[:, 1:2], 0.0).then_inc(*E.sig("dve_stage_done"))
                dve.wait_ge(*E.next("act_stage_done"))
                dve.wait_ge(*E.next("pool_stage_done"))
                for t in range(4):
                    dve.wait_ge(*E.taken("mgate", l, t))
                    y = view(YM[:, t, :])
                    tt_(y, y, view(mSil[:, t % 2, :]), ALU.mult).then_inc(*E.sig("silu_used"))
                for g in range(4):
                    dve.wait_ge(*E.taken("pgate", l, g))
                    dve.wait_ge(*E.written("mixed", l, g))
                    ps = cols("mixed", l, g)
                    y = tok_view(YP[:, g, :], own)
                    stt(y, bank_view(ps, own), Pm("pscale" + L)[:, g:g + 1], y, ALU.mult, ALU.mult).then_inc(*E.read("mixed", l, g))
                dve.wait_ge(*E.taken("mixed", l, 3))
                V.tensor_copy(tick[:, 5:6], YP[:, 3, TOK - 1:TOK]).then_inc(*E.sig("branches_ready", 4))
                merge(("l", l), own)
                inverse_std(("post", l), nRs, 0, own, D)
                for k in range(KT):
                    if l == 0:
                        stt(mOUT[:, k, 0:CTX], mOUT[:, k, 0:CTX], pgB[:, k, 1:2], nRs[:, 0:CTX],
                            ALU.mult, ALU.mult)
                    stt(mOUT[:, k, CTX:TOK], mOUT[:, k, CTX:TOK], pgB[:, k, 0:1], nRs[:, CTX:TOK],
                        ALU.mult, ALU.mult).then_inc(*E.sig("update_ready"))

        @block.gpsimd
        def _(pool):
            E = Eng(pool, "pool")
            G_ = nc.gpsimd
            pool.dma_start(par[:, :], dram["params"]).then_inc(sem("params_loaded"), 16)
            pool.dma_start(con[:, :], dram["consts"]).then_inc(sem("consts_loaded"), 16)
            pool.dma_start(R3, dram["acts"]).then_inc(sem("residual_loaded"), 16)
            pool.dma_start(rTab, dram["t_ret"]).then_inc(sem("ret_tables_loaded"), 16)
            G_.memset(tick[:, 2:3], 0.0).then_inc(*E.sig("pool_stage_done"))
            pool.wait_ge(*E.next("act_stage_done"))
            pool.wait_ge(*E.next("dve_stage_done"))
            pool.dma_start(area(WIN + 3584, 1024), dram["t_win"]).then_inc(sem("win_tables_loaded"), 16)
            pool.dma_start(nMask, dram["t_colmask"]).then_inc(sem("mask_loaded"), 16)
            for h in range(8):
                for half in range(2):
                    src = bass.AP(dram["rpb"].tensor, (h * 15 + 1 - half) * 127, [[1, 64], [127, 14], [1, 64]])
                    pool.dma_start(nB[64 * half:64 * half + 64, h, :].rearrange("p (a c) -> p a c", a=14), src)\
                        .then_inc(sem("bias_loaded"), 16)
            pool.dma_start(R3[:, :, 0:CTX], dram["ctx2"]).then_inc(sem("ctx2_loaded"), 16)
            pool.wait_ge(*E.next("mask_loaded", 16))
            pool.wait_ge(*E.next("bias_loaded", 16 * 16))
            for h in range(8):
                b = nB[:, h, :].rearrange("p (a c) -> p a c", a=14)
                G_.tensor_tensor(b, b, nMask.unsqueeze(1).to_broadcast([P, 14, 64]), ALU.add)\
                    .then_inc(*E.sig("bias_ready"))
            pool.wait_ge(*E.own())
            G_.memset(tick[:, 2:3], 0.0).then_inc(*E.sig("pool_stage_done"))
            pool.wait_ge(*E.next("act_stage_done"))
            pool.wait_ge(*E.next("dve_stage_done"))
            pool.wait_ge(*E.own())
            G_.memset(tick[:, 2:3], 0.0).then_inc(*E.sig("pool_stage_done"))
            pool.wait_ge(*E.next("act_stage_done"))
            pool.wait_ge(*E.next("dve_stage_done"))
            pool.wait_ge(*E.own())
            G_.memset(tick[:, 2:3], 0.0).then_inc(*E.sig("pool_stage_done"))
            pool.wait_ge(*E.next("act_stage_done"))
            pool.wait_ge(*E.next("dve_stage_done"))
            pool.dma_start(eWR, dram["router"]).then_inc(sem("router_loaded"), 16)
            for l in LAYERS:
                pool.wait_ge(*E.own())
                G_.memset(tick[:, 2:3], 0.0).then_inc(*E.sig("pool_stage_done"))
                pool.wait_ge(*E.next("act_stage_done"))
                pool.wait_ge(*E.next("dve_stage_done"))
                pool.dma_start(area(MW, 1024), dram["t_mla"]).then_inc(sem("mla_tables_loaded"), 16)
                pool.wait_ge(*E.own())
                G_.memset(tick[:, 2:3], 0.0).then_inc(*E.sig("pool_stage_done"))
                pool.wait_ge(*E.next("act_stage_done"))
                pool.wait_ge(*E.next("dve_stage_done"))
                pool.dma_start(pCnt, dram["t_count"]).then_inc(sem("counts_loaded"), 16)
                for b in range(2):
                    for c0, n in ((0, 8), (264, 16), (792, 8)):
                        ins = G_.memset(pX[:, b * (TOK + 32) + c0:b * (TOK + 32) + c0 + n], 0.0)
                if l == 1:
                    for b in range(2):
                        ins = G_.memset(pX[:, b * (TOK + 32) + 8:b * (TOK + 32) + 264], 0.0)
                ins.then_inc(*E.sig("pads_zero"))
                pool.wait_ge(*E.next("pads_zero"))
                pool.wait_ge(*E.next("counts_loaded", 16))
                for g in range(4):
                    pool.wait_ge(*E.taken("px", l, g))
                    u = pX[:, (g % 2) * (TOK + 32):(g % 2 + 1) * (TOK + 32)]
                    a, w = u, TOK + 32
                    lo = 0
                    for n in range(g + 1):
                        o = pS[:, (n % 2) * w:(n % 2 + 1) * w]
                        s1 = 1 if n == 0 else 2 ** (n - 1)
                        s2 = 0 if n == 0 else 2 ** (n - 1)
                        new = lo + s1
                        G_.tensor_tensor(o[:, new:w - new], a[:, new - s1:w - new - s1],
                                                a[:, new + s2:w - new + s2], ALU.add).then_inc(*E.sig("pool_step"))
                        pool.wait_ge(*E.own())
                        a, lo = o, new
                    segs = ([(8, 0, CTX)] if l == 0 else []) + [(280, CTX, SEQ)]
                    for x0, c0, n in segs:
                        ins = G_.tensor_tensor(pO[:, g, c0:c0 + n], a[:, x0:x0 + n], pCnt[:, g, c0:c0 + n],
                                               ALU.mult)
                    ins.then_inc(*E.sig("pool_step"))
                    pool.wait_ge(*E.own())
                    for x0, c0, n in segs:
                        ins = G_.tensor_tensor(pO[:, g, c0:c0 + n], pO[:, g, c0:c0 + n], u[:, x0:x0 + n],
                                               ALU.subtract)
                    ins.then_inc(*E.sig("pooled"))
                for k in range(KT):
                    pool.wait_ge(*E.next("update_ready"))
                    v = slice(0, TOK) if l == 0 else slice(CTX, TOK)
                    G_.tensor_tensor(R3[:, k, v], R3[:, k, v], mOUT[:, k, v], ALU.add)\
                        .then_inc(*E.sig("residual_updated"))

        @block.sync
        def _(sp):
            for s in range(NSLOT):
                sp.dma_start(ring[:, s * UNIT:(s + 1) * UNIT], dram["weights"][s, :, :])\
                    .then_inc(loaded[s], 16)
            with sp.Fori(1, rounds) as it:
                for s in range(NSLOT):
                    sp.wait_ge(sem("weights_used"), it * NSLOT + (s + 1 - NSLOT))
                    sp.dma_start(ring[:, s * UNIT:(s + 1) * UNIT], dram["weights"][it * NSLOT + s, :, :])\
                        .then_inc(loaded[s], 16)
            for k in range(KT):
                sp.wait_ge(sem("residual_updated"), KT + k + 1)
                sp.dma_start(out[:, k, :], R3[:, k, CTX:TOK]).then_inc(sem("output_written"), 16)
            sp.wait_ge(sem("output_written"), 16 * KT)
            for s in range(NSLOT):
                sp.wait_ge(loaded[s], 16 * rounds)


def tiled(a):
    return a.reshape(-1, P, a.shape[1]).transpose(1, 0, 2).reshape(P, -1)


def pack_weights(x):
    plan = stream_plan()
    out = np.zeros((padded_tiles(len(plan)), P, 1024), np.float32)
    for i, (name, w, lead, rows, cols) in enumerate(plan):
        if name[0] == "decay_w2":
            out[i, 0:16, 0:256] = x["gla_af_w2_2"][lead]
            out[i, 32:48, 0:256] = x["gla_ab_w2_2"][lead]
        elif name[0] == "pool_w":
            out[i, :, 0:512] = x["pool_w_2"][lead].transpose(1, 0, 2).reshape(P, 512)
        else:
            a = x[w][lead]
            if rows is not None:
                a = a[rows]
            if cols[0] >= 0 and (np.diff(cols) == 1).all():
                a = a[:, cols[0]:cols[-1] + 1]
            else:
                a = np.where(cols < 0, np.float32(0), a[:, np.maximum(cols, 0)])
            t = tiled(a)
            out[i, :, :t.shape[1]] = t
    return np.ascontiguousarray(out.reshape(-1, 2, P, 1024).transpose(0, 2, 1, 3).reshape(-1, P, UNIT))


def pack_params(x):
    out = np.zeros((P, NPAR), np.float32)
    col = lambda v: v.reshape(-1, P).T
    twice = lambda v: np.repeat(col(v), 2, axis=1)
    both = lambda a, b: np.stack([col(a), col(b)], 2).reshape(P, -1)
    every = lambda v: np.broadcast_to(v.reshape(1, -1), (P, v.size))
    vals = {
        "bmod": twice(x["b_mod"][0]), "gmix": twice(x["g_mix"][0]), "gffn": col(x["g_ffn"][0]),
        "gfinal": col(x["g_final"]), "cond": both(x["c"][0], x["c_ctx"]),
        "cond2": both(x["c_2"][0], x["c_ctx_2"]), "retgn": col(x["ret_gn"][0]),
        "sink": every(x["win_sink"][0]), "decay": every(x["ret_decay_logit"][0]),
    }
    for l in LAYERS:
        for n, v in (("bmod2", twice(x["mod_b_2"][l])), ("pre", twice(x["pre_norm_2"][l])),
                     ("post", twice(x["post_norm_2"][l])), ("qnorm", col(x["mla_q_norm_2"][l])),
                     ("kvnorm", col(x["mla_kv_norm_2"][l])), ("pscale", col(x["pool_scale_2"][l])),
                     ("afb", col(x["gla_af_b_2"][l])), ("abb", col(x["gla_ab_b_2"][l])),
                     ("glan", col(x["gla_norm_2"][l]))):
            vals[n + str(l)] = v
    for n, (a, b) in PCOL.items():
        out[:, a:b] = vals[n]
    return out


def kernel(**inputs):
    import concourse.bacc as bacc
    from concourse.bass_utils import run_bass_kernel_spmd
    x = {k: np.asarray(v) for k, v in inputs.items()}
    feature_major = lambda a: a.T.reshape(KT, P, -1).transpose(1, 0, 2)
    arrays = {
        "weights": pack_weights(x),
        "params": pack_params(x),
        "acts": feature_major(np.concatenate([x["ctx"][0], x["x"][0]], 0)),
        "ctx2": feature_major(x["ctx_2"][0]),
        "router": x["w_router"][0].reshape(KT, P, NE).transpose(1, 0, 2),
        "rpb": np.pad(x["na_rpb"][0], ((0, 0), (0, 0), (48, 48))),
        **constants(),
    }
    arrays = {"in_" + k: np.ascontiguousarray(v) for k, v in arrays.items()}
    nc = bacc.Bacc("TRN2", target_bir_lowering=False, num_devices=1)
    f32 = mybir.dt.float32
    dram = {k[3:]: nc.dram_tensor(k, v.shape, f32, kind="ExternalInput").ap() for k, v in arrays.items()}
    out = nc.dram_tensor("out_x", (P, KT, SEQ), f32, kind="ExternalOutput").ap()
    program(nc, dram, out)
    got = run_bass_kernel_spmd(nc, [arrays], core_ids=[0]).results[0]["out_x"]
    return got.transpose(1, 0, 2).reshape(D, SEQ).T.reshape(1, SEQ, D)
```

```python
import concourse.bass as bass
from concourse import mybir
from contextlib import ExitStack
import numpy as np

P = 128
D = 1024
KT = D // P
CTX, SEQ = 256, 512
TOK = CTX + SEQ
TT = TOK // P
EPS = 1e-6
NE, CAP, FF = 16, 64, 1024
PAIRS = NE // 2
UNIT = 2048
NSLOT = 4
SPLIT = {"q_r", "k_r", "v_r", "g_r", "q_w", "k_w", "v_w", "q_n", "k_n", "v_n", "gate", "gq", "gk", "gv",
         "small", "ggate", "mq", "mkv", "mgate", "px", "pgate", "w_out"}
ALL = ((0, 384), (384, 384))
IMG = ((CTX, SEQ),)
CLAMP = 1280.0

B1 = dict(q_r=0, k_r=512, v_r=1024, g_r=1536, q_w=2048, k_w=2560, v_w=2688, q_n=2816, k_n=3328,
          v_n=3840, gates=4352)
B2 = dict(q=0, kv=256, kr=384, mgate=416, px=928, pgate=1440, gq=1952, gk=2208, gv=2464, af=2976,
          ab=2992, ggate=3008, merge=3520)
LAYERS = (0, 1)
SCAN = ((0, 1, 2, 3, 4, 5), (1, 0, 5, 4, 3, 2))
OWN_CHUNKS = (range(TT), range(2, TT))
PASSES = ("win", "na", ("mla", 0), ("mlac", 0), ("mla", 1))


def window_q_cols(t):
    return np.r_[t * 64:t * 64 + 64, (t + 4) * 64:(t + 4) * 64 + 64]


def stream_plan():
    def cols(w, lead, name, c0, n):
        return [((name, t), w, lead, None, np.arange(c0 + t * P, c0 + t * P + P)) for t in range(n)]

    def rhs(w, lead, name, c0, n, per=2):
        return [((name, i), w, lead, np.arange(i * per * P, (i + 1) * per * P), np.arange(c0, c0 + n))
                for i in range(KT // per)]

    out = []
    for b in range(6):
        out += rhs("w_mod", (0,), ("mod1", b), b * D, D, per=1)
    out += cols("w_in", (0,), "q_r", B1["q_r"], 4) + cols("w_in", (0,), "k_r", B1["k_r"], 4)
    out += rhs("w_in", (0,), "v_r", B1["v_r"], 512) + cols("w_in", (0,), "g_r", B1["g_r"], 4)
    out += [(("q_w", t), "w_in", (0,), None, B1["q_w"] + window_q_cols(t)) for t in range(4)]
    out += cols("w_in", (0,), "k_w", B1["k_w"], 1) + cols("w_in", (0,), "v_w", B1["v_w"], 1)
    out += cols("w_in", (0,), "q_n", B1["q_n"], 4) + cols("w_in", (0,), "k_n", B1["k_n"], 4)
    out += rhs("w_in", (0,), "v_n", B1["v_n"], 512)
    win_rows = np.concatenate([window_q_cols(t) for t in range(4)])
    for f in range(0, KT, 2):
        for b, w, rows in ((0, "w_ret", None), (1, "w_win", win_rows), (2, "w_na", None)):
            for g in (f, f + 1):
                c0 = B1["gates"] + b * D + g * P
                out.append((("gate", b, g), "w_in", (0,), None, np.arange(c0, c0 + P)))
            out.append((("branch", b, f), w, (0,), rows, np.arange(f * P, f * P + 2 * P)))
    out += cols("w_out", (0,), "w_out", 0, KT)
    for j in range(PAIRS):
        for kind in ("exp_gate", "exp_up", "exp_down"):
            both = [rhs("w_" + kind, (0, 2 * j + e), (kind, j, e), 0, FF, per=1) for e in (0, 1)]
            out += [tile for k in range(KT) for tile in (both[0][k], both[1][k])]
    for l in LAYERS:
        w = "w_in_2"
        for b in range(3):
            out += rhs("mod_w_2", (l,), (("mod2", l), b), b * D, D, per=1)
        out += cols(w, (l,), ("gq", l), B2["gq"], 2) + cols(w, (l,), ("gk", l), B2["gk"], 2)
        out += rhs(w, (l,), ("gv", l), B2["gv"], 512)
        small = np.full(P, -1)
        small[0:16] = B2["af"] + np.arange(16)
        small[32:48] = B2["ab"] + np.arange(16)
        small[64:96] = B2["kr"] + np.arange(32)
        out.append((("small", l), w, (l,), None, small))
        out.append((("decay_w2", l), None, (l,), None, None))
        out += cols(w, (l,), ("mq", l), B2["q"], 2) + cols(w, (l,), ("ggate", l), B2["ggate"], 4)
        out += cols(w, (l,), ("mkv", l), B2["kv"], 1)
        for h in (0, 4):
            out.append((("uq", l, h), "mla_w_uq_2", (l,), None, np.arange(h * 96, h * 96 + 384)))
        ukv = np.arange(8)[:, None] * 128 + np.arange(64)[None, :]
        out.append((("ukv", l), "mla_w_ukv_2", (l,), None, np.r_[ukv.ravel(), ukv.ravel() + 64]))
        out += cols(w, (l,), ("mgate", l), B2["mgate"], 4)
        for g in range(4):
            out += cols(w, (l,), ("px", l, g), B2["px"] + g * P, 1)
            out += cols(w, (l,), ("pgate", l, g), B2["pgate"] + g * P, 1)
        out.append((("pool_w", l), None, (l,), None, None))
        for f in range(0, KT, 2):
            for b, wb in ((0, "w_branch_mla_2"), (1, "w_branch_pool_2"), (2, "w_branch_gla_2")):
                for g in (f, f + 1):
                    c0 = B2["merge"] + b * D + g * P
                    out.append((("gate", l, b, g), w, (l,), None, np.arange(c0, c0 + P)))
                out.append((("branch", l, b, f), wb, (l,), None, np.arange(f * P, f * P + 2 * P)))
        out += cols("w_out_2", (l,), ("w_out", l), 0, KT)
    return out


def is_split(name):
    return (name[0] if isinstance(name[0], str) else name[0][0]) in SPLIT


def padded_tiles(n):
    per = NSLOT * (UNIT // 1024)
    return -(-n // per) * per


PARAMS = (("bmod", 96), ("gmix", 16), ("gffn", 8), ("gfinal", 8), ("cond", 16), ("cond2", 16),
          ("retgn", 4), ("sink", 8), ("decay", 8)) + tuple(
    (f"{n}{l}", c) for l in LAYERS for n, c in
    (("bmod2", 48), ("pre", 16), ("post", 16), ("qnorm", 2), ("kvnorm", 1), ("pscale", 4),
     ("afb", 2), ("abb", 2), ("glan", 1)))
PCOL, _at = {}, 0
for _n, _c in PARAMS:
    PCOL[_n] = (_at, _at + _c)
    _at += _c
NPAR = _at
CONST = (("ident", 128), ("ones", 128), ("rot_r", 128), ("rot_w", 128), ("rot_m", 128), ("flip", 128),
         ("slots", 64), ("upper", 128), ("lower", 128), ("wleft", 128), ("wright", 128), ("eps", 1))
CCOL, _at = {}, 0
for _n, _c in CONST:
    CCOL[_n] = (_at, _at + _c)
    _at += _c
NCONST = _at
DW = 1408
ARENA = 53184 - 2 * KT * TOK - NSLOT * UNIT - 4096 - NPAR - NCONST - 520


def constants():
    f = np.float32
    c = np.zeros((P, NCONST), f)
    put = lambda n, a: c.__setitem__((slice(None), slice(*CCOL[n])), a)
    put("ident", np.eye(P))
    put("ones", 1.0)

    def half_rot(d, blocks):
        m = np.zeros((P, P), f)
        for b in blocks:
            for i in range(d // 2):
                m[b + d // 2 + i, b + i] = -1.0
                m[b + i, b + d // 2 + i] = 1.0
        return m

    put("rot_r", half_rot(128, [0]))
    put("rot_w", half_rot(64, [0, 64]))
    put("rot_m", half_rot(16, [64, 80]))
    flip = np.zeros((P, P), f)
    q = np.arange(P)
    flip[63 - q % 64 + 64 * (q // 64), q] = 1.0
    put("flip", flip)
    put("slots", np.arange(64)[None, :])
    put("upper", (q[:, None] <= q[None, :]))
    put("lower", (q[:, None] >= q[None, :]))
    put("wleft", np.where(q[None, :] >= q[:, None], 0.0, -1e30))
    put("wright", np.where(q[None, :] <= q[:, None], 0.0, -1e30))
    put("eps", EPS)
    t = np.arange(SEQ)
    row, col = (t // 64).astype(f), (t % 64).astype(f)

    def tables(d):
        inv = (f(10000.0) ** (-np.arange(d // 4, dtype=f) / f(d // 4))).astype(f)
        ang = np.concatenate([row[:, None] * inv, col[:, None] * inv], -1).astype(f)
        ang = np.concatenate([ang, ang], -1)
        ang = np.concatenate([ang] * (P // d), -1)
        return np.cos(ang).T.astype(f), np.sin(ang).T.astype(f)

    inv = (f(10000.0) ** (-np.arange(0, 16, 2, dtype=f) / f(16))).astype(f)
    ar, ac = row[:, None] * inv, col[:, None] * inv
    ang = np.concatenate([ar, ar, ac, ac], -1).T.astype(f)
    cm, sm = np.ones((P, SEQ), f), np.zeros((P, SEQ), f)
    cm[64:96], sm[64:96] = np.cos(ang), np.sin(ang)
    u = np.arange(DW)[None, :] - 640 - q[:, None]
    ck = np.arange(64)[None, :]
    cq = (63 - q % 64)[:, None]
    start = np.clip(cq - 8, 0, 48)
    colmask = np.where((ck >= start) & (ck < start + 16), 0.0, -1e30)
    inv_count = np.zeros((4, TOK), f)
    for g, w in enumerate((2, 4, 8, 16)):
        for n, off in ((CTX, 0), (SEQ, CTX)):
            tt = np.arange(n)
            inv_count[g, off:off + n] = 1.0 / (np.clip(tt + w // 2, 0, n) - np.clip(tt - w // 2, 0, n))
    return {
        "consts": c,
        "t_ret": np.concatenate([*tables(128), u], 1).astype(f),
        "t_win": np.concatenate(tables(64), 1).astype(f),
        "t_mla": np.concatenate([cm, sm], 1).astype(f),
        "t_colmask": colmask.astype(f),
        "t_count": np.broadcast_to(inv_count.reshape(1, -1), (P, 4 * TOK)).astype(f),
    }


def program(nc, dram, scratch, out):
    f32, f32r = mybir.dt.float32, mybir.dt.float32r
    ACT = mybir.ActivationFunctionType
    ALU = mybir.AluOpType
    AXX = mybir.AxisListType.X
    plan = [p[0] for p in stream_plan()]
    rounds = padded_tiles(len(plan)) // (NSLOT * 2)

    with ExitStack() as ctx:
        def sbuf(name, cols):
            return ctx.enter_context(nc.sbuf_tensor(name, [P, cols], f32))

        with nc.sbuf_tensor("residual", [P, KT * TOK], f32) as R, nc.sbuf_tensor("hidden", [P, KT * TOK], f32) as H:
            R3, H3 = (a[:, :].rearrange("p (k t) -> p k t", k=KT) for a in (R, H))
        Hhi, Hlo = (ctx.enter_context(nc.sbuf_tensor(n, [P, KT * TOK], f32r))[:, :].rearrange("p (k t) -> p k t", k=KT)
                    for n in ("hidden_high", "hidden_low"))
        ring = sbuf("ring", NSLOT * UNIT)
        parts = ctx.enter_context(nc.sbuf_tensor("weight_parts", [P, 4096], f32r))[:, :]
        parts = parts.rearrange("p (s x n) -> p s x n", s=2, x=2)
        split_tiles = [n for n, name in enumerate(plan) if is_split(name)]
        split_reader = []
        par = sbuf("params_sb", NPAR)
        con = sbuf("consts_sb", NCONST)
        with nc.sbuf_tensor("arena", [P, ARENA], f32) as arena:
            pass
        arena_parts = ctx.enter_context(nc.sbuf_tensor("arena_parts", [P, ARENA], f32r))
        small = sbuf("small", 520)
        psum = ctx.enter_context(nc.psum_tensor("psum", [P, 8 * 512], f32))

        sems = {}

        def sem(name):
            if name not in sems:
                sems[name] = ctx.enter_context(nc.semaphore(name))
            return sems[name]

        psum_free = [sem(f"psum_free{i}") for i in range(3)]
        loaded = [sem(f"weights_loaded{i}") for i in range(NSLOT)]
        psum_full = sem("psum_full")
        group_no = {}

        def cols(*name):
            g = group_no[name]
            return psum[:, (g % 3) * 1024:(g % 3) * 1024 + 1024]

        def C(name, n=None):
            a, b = CCOL[name]
            return con[:, a:b]

        def Pm(name):
            a, b = PCOL[name]
            return par[:, a:b]

        def area(at, n):
            assert at + n <= ARENA, (at, n, ARENA)
            return arena[:, at:at + n]

        def split(ap, **kw):
            (k, v), = kw.items()
            return ap.rearrange(f"p ({k} n) -> p {k} n", **kw)

        def bank_view(ps, chunks):
            if chunks is ALL:
                return split(ps, a=2)[:, :, 0:384]
            return ps[:, 0:SEQ]

        def tok_view(ap, chunks):
            if chunks is ALL:
                return split(ap, a=2)
            return ap[:, CTX:TOK]

        def wide(col, like):
            return col.to_broadcast([P, like])

        modA = split(small[:, 0:96], a=48)
        gmA = split(small[:, 96:112], a=KT)
        gmF = small[:, 112:120]
        cond = split(small[:, 120:136], a=KT)
        cond2 = split(small[:, 136:152], a=KT)
        modB = split(small[:, 152:200], a=24)
        gmB = split(small[:, 200:216], a=KT)
        pgB = split(small[:, 216:232], a=KT)
        negmax = small[:, 232:248]
        sums = small[:, 248:264]
        esink = small[:, 264:280]
        rinv = small[:, 280:296]
        nsink = small[:, 296:304]
        lg = small[:, 304:312]
        lt1 = small[:, 312:320]
        lt2 = small[:, 320:328]
        expT = small[:, 328:352]
        m16 = small[:, 352:356]
        s16 = small[:, 356:360]
        r16 = small[:, 360:364]
        top8 = small[:, 364:372]
        aff = split(small[:, 372:436], a=4)
        posn = split(small[:, 436:500], a=4)
        tick = small[:, 500:512]
        totals = {}

        class Eng:

            def __init__(self, e, name):
                self.e, self.name, self.seen, self.it, self.per = e, name, {}, None, {}
                self.made, self.last = {}, None

            def at(self, value, key):
                return value if self.it is None else self.it * self.per.get(key, 0) + value

            def next(self, name, n=1):
                self.seen[name] = self.seen.get(name, 0) + n
                return sem(name), self.at(self.seen[name], name)

            def upto(self, name, total):
                self.seen[name] = max(total, self.seen.get(name, 0))
                return sem(name), self.at(total, name)

            def sig(self, name, n=1):
                self.made[name] = self.made.get(name, 0) + n
                self.last = (sem(name), self.made[name], name)
                return sem(name), n

            def read(self, *name):
                g = group_no[name]
                self.last = (psum_free[g % 3], g // 3 + 1, "slot")
                return psum_free[g % 3], 1

            def own(self):
                s, v, key = self.last
                return s, self.at(v, key)

            def written(self, *name):
                return psum_full, self.at(group_no[name] + 1, "groups")

            def taken(self, *name):
                g = group_no[name]
                return psum_free[g % 3], self.at(g // 3 + 1, "slot")

            def begin(self, it, per):
                self.it, self.per, self.start = it, per, (dict(self.seen), dict(self.made))

            def end(self, turns):
                seen, made = self.start
                for k, v in list(self.seen.items()):
                    d = v - seen.get(k, 0)
                    assert d == self.per.get(k, 0), (self.name, k, d)
                    self.seen[k] = v + (turns - 1) * d
                for k, v in list(self.made.items()):
                    self.made[k] = v + (turns - 1) * (v - made.get(k, 0))
                self.it = None

        block = ctx.enter_context(nc.Block())

        YA, YB, YC = (area(i * 2048, 2048) for i in range(3))
        RET = 6144
        rQ, rK = split(area(RET, 2048), a=4), split(area(RET + 2048, 3072), a=4)
        rV = split(area(RET + 5120, 3072), a=TT)
        rSG = split(area(RET + 8192, 2048), a=4)
        rTab = area(RET + 10240, 1024 + DW)
        rCos, rSin, rDist = rTab[:, 0:512], rTab[:, 512:1024], rTab[:, 1024:1024 + DW]
        rE = area(RET + 12672, DW)
        rCW = split(area(RET + 14080, 1024), a=2)
        rP = split(area(RET + 15104, 4096), a=4)
        rTmp = area(RET + 15104, 1024)
        rSq = split(area(RET + 15104, 2048), a=4)
        rRs = split(area(RET + 15104 + 2048, 2048), a=4)
        A3 = split(YA, a=4)

        WIN = 6144
        wQ = split(area(WIN, 2048), a=4)
        wK, wV = area(WIN + 2048, TOK), split(area(WIN + 2816, TOK), a=TT)
        wCos, wSin = area(WIN + 3584, 512), area(WIN + 4096, 512)
        wTmp = area(WIN + 4608, 1024)
        AT1 = WIN + 5632

        NA = 6144
        nQ, nK = split(area(NA, 2048), a=4), split(area(NA + 2048, 3072), a=4)
        nV = split(area(NA + 5120, 3072), a=TT)
        AT2 = NA + 8192
        nB = split(area(NA + 12288, 7168), h=8)
        nMask = area(NA + 19456, 64)

        MRG = 9216
        mSG = split(area(MRG, 6 * TOK), a=6)
        mTmp = split(area(MRG + 6 * TOK, 2 * TOK), a=2)
        mMG = split(area(MRG + 8 * TOK, KT * TOK), a=KT)
        mHi = split(arena_parts[:, MRG:MRG + KT * TOK], a=KT)
        mLo = split(arena_parts[:, MRG + 8 * TOK:MRG + (8 + KT) * TOK], a=KT)
        mOUT = split(area(0, KT * TOK), a=KT)

        modRow = {"mod1": area(0, 6 * D), ("mod2", 0): area(MRG, 3 * D), ("mod2", 1): area(MRG, 3 * D)}
        nSq = split(area(ARENA - 4 * TOK, 3 * TOK), a=3)
        nRs = area(ARENA - TOK, TOK)

        def attn_area(at):
            return (split(area(at, 2 * TOK), a=2), split(area(at + 2 * TOK, 2 * TOK), a=2),
                    split(area(at + 4 * TOK, 1024), a=2))

        XP = 0
        eP = H3[:, :, :].rearrange("p k t -> p (k t)")[:, 0:4096].rearrange("p (t n) -> p t n", t=4)
        eHT = split(area(XP, 4096), a=4)
        ePG = split(area(XP + 4096, 4096), a=PAIRS)
        eYE = area(XP + 8192, D)
        ePg = split(area(XP + 16384, 4096), a=4)
        eXE = split(area(XP + 16384, 1024), a=KT)
        eSG, eHID = area(XP + 17408, 1024), area(XP + 18432, 1024)
        eHF = split(area(XP + 19456, 1024), a=KT)
        eWR = split(area(XP + 20480, 128), a=KT)
        eA = area(XP + 20608, 512)
        eW = split(area(XP + 21120, 1024), a=2)
        eM = area(XP + 22144, 512)
        eC = area(XP + 22656, 512)

        YG, YM, YP = (split(area(i * 3072, 3072), a=4) for i in range(3))
        G = 3072
        gQ, gK = split(area(G, 1536), a=2), split(area(G + 1536, 1536), a=2)
        gV = split(area(G + 3072, 3072), a=TT)
        gSM = area(G + 6144, TOK)
        gB = split(area(G + 6912, 3072), a=4)
        gS = area(G + 9984, 3072).rearrange("p (d c t n) -> p d c t n", d=2, c=TT, t=2)
        gT1 = split(area(G + 13056, 3072), a=4)
        gLM = split(area(G + 17152, 3072), a=4)
        gKT = area(G + 17152, 3072)

        def gChunk(i):
            at = G + 13056 + 4096 * i
            return (split(area(at, 512), a=4), split(area(at + 512, 512), a=4),
                    area(at + 1024, 2048).rearrange("p (d t s n) -> p d t s n", d=2, t=2, s=4),
                    area(at + 3072, 1024).rearrange("p (a s b n) -> p a s b n", a=4, s=4, b=2))
        gAT = area(G + 21248, 512)
        gSq = split(area(G + 13056, 3072), a=4)
        gRs = split(area(G + 17152, 3072), a=4)
        SILU = split(area(G + 20224, 2 * TOK), a=2)

        M = 6144
        mQ, mK = split(area(M, 6144), a=8), split(area(M + 6144, 6144), a=8)
        mV = split(area(M + 12288, 3072), a=TT)
        MW = M + 15360
        mCos, mSin = area(MW, 512), area(MW + 512, 512)
        mRaw = split(area(G + 21760, 2 * TOK), a=2)
        mKV = area(MW + 1024 + 2 * TOK, TOK)
        mKR = area(3072, TOK)
        mTp = area(3072 + TOK, TOK)
        mSil = split(area(23040, 2 * TOK), a=2)
        mSq, mRs = split(area(3072 + 2 * TOK, TOK), a=1), area(3072 + 3 * TOK, TOK)
        PB = 9216
        pX = area(PB, 2 * (TOK + 32))
        pCnt = split(area(PB + 4096, 4 * TOK), a=4)
        pS = area(PB + 8192, 2 * (TOK + 32))
        pO = split(area(PB + 10240, 4 * TOK), a=4)

        def units(qts):
            return [(t, hh, qi) for t in range(4) for hh in range(2) for qi in range(len(qts))]

        ATT = {n: range(2) if n[0] == "mlac" else range(4) for n in PASSES}
        unit_base = {n: sum(8 * len(ATT[m]) for m in PASSES[:i]) for i, n in enumerate(PASSES)}

        def spans(name, qi):
            if name == "win":
                lo, hi = max(qi - 1, 0), min(qi + 1, 3)
                return (hi - lo + 1) * P, [2 + b for b in range(lo, hi + 1)] + [0, 1]
            if name[0] == "mlac":
                return 0, [0, 1]
            return SEQ, [2, 3, 4, 5, 0, 1]

        @block.tensor
        def _(pe):
            E = Eng(pe, "pe")
            state = dict(g=0, tile=0, owed=0, ended=0, token=0)

            def group(*name):
                g = state["g"]
                group_no[name] = g
                state["g"] += 1
                if g >= 3:
                    pe.wait_ge(psum_free[g % 3], E.at(g // 3, "slot"))
                return psum[:, (g % 3) * 1024:(g % 3) * 1024 + 1024]

            def mm(o, lhsT, rhs, start, stop):
                return nc.tensor.matmul(o, lhsT, rhs, start=start, stop=stop)

            def flip(o, a):
                return nc.tensor.transpose(o, a, C("ident")[0:a.shape[0], 0:a.shape[0]])

            def refill(ins):
                if state["owed"]:
                    ins.then_inc(sem("weights_used"), state["owed"])
                    state["owed"] = 0

            def weights(*name):
                n = state["tile"]
                assert plan[n] == name, (plan[n], name)
                state["tile"] += 1
                if n % 2 == 0:
                    u = n // 2
                    pe.wait_ge(loaded[u % NSLOT], E.at(16 * (u // NSLOT + 1), "ring"))
                at = (n // 2 % NSLOT) * UNIT + (n % 2) * 1024
                return ring[:, at:at + 1024]

            def done(n=1):
                for _ in range(n):
                    state["ended"] += 1
                    if state["ended"] % 2 == 0:
                        state["owed"] += 1

            def project(name, w, src, nk, chunks, M=P, src0=0):
                ps = group(*name)
                for k in range(nk):
                    for ci, (c0, n) in enumerate(chunks):
                        ins = mm(ps[0:M, ci * 512:ci * 512 + n], w[:, k, 0:M],
                                 src[:, k, c0 - src0:c0 - src0 + n], k == 0, k == nk - 1)
                        if k == 0 and ci == 0:
                            refill(ins)
                ins.then_inc(psum_full, 1)

            def part_products(hi, lo, src=(Hhi, Hlo)):
                return ((hi, src[0]), (hi, src[1]), (lo, src[0]))

            def weight_parts(*name):
                weights(*name)
                i = len(split_reader)
                assert split_tiles[i] == state["tile"] - 1
                pe.wait_ge(sem("tile_split"), i + 1)
                return parts[:, i % 2, 0, :], parts[:, i % 2, 1, :]

            def project_tile(tile, name, chunks, first=False, src=(Hhi, Hlo), ready="hidden_ready"):
                hi, lo = weight_parts(*tile)
                ps = group(*name)
                for k in range(KT):
                    if first:
                        pe.wait_ge(*E.next(ready))
                    for n, (w, h) in enumerate(part_products(split(hi, a=KT), split(lo, a=KT), src)):
                        for ci, (c0, cn) in enumerate(chunks):
                            ins = mm(ps[:, ci * 512:ci * 512 + cn], w[:, k, :], h[:, k, c0:c0 + cn],
                                     k == 0 and n == 0, k == KT - 1 and n == 2)
                            if k == 0 and n == 0 and ci == 0:
                                refill(ins)
                ins.then_inc(psum_full, 1)
                split_reader.append((psum_full, state["g"]))
                done()

            def project_tokens(tiles, name):
                ps = [group(*name, p) for p in range(TT // 2)]
                for i, tile in enumerate(tiles):
                    hi, lo = weight_parts(*tile)
                    for j in range(2):
                        k = 2 * i + j
                        for t in range(TT):
                            for n, (w, h) in enumerate(part_products(split(hi, a=2), split(lo, a=2))):
                                ins = mm(ps[t // 2][:, (t % 2) * 512:(t % 2 + 1) * 512],
                                         h[:, k, t * P:(t + 1) * P], w[:, j, :],
                                         k == 0 and n == 0, k == KT - 1 and n == 2)
                                if j == 0 and t == 0 and n == 0:
                                    refill(ins)
                            if k == KT - 1 and t % 2:
                                ins.then_inc(psum_full, 1)
                    if i < len(tiles) - 1:
                        ins.then_inc(sem("token_tile_used"), 1)
                        state["token"] += 1
                        split_reader.append((sem("token_tile_used"), state["token"]))
                    else:
                        split_reader.append((psum_full, state["g"]))
                    done()

            def modulation(name, blocks, c):
                for b in range(blocks):
                    ps = group(name, "row", b)
                    for k in range(KT):
                        w = weights((name, b), k)
                        for half in range(2):
                            ins = mm(ps[64 * half:64 * half + 2, half * 512:(half + 1) * 512], c[:, k, :],
                                     w[:, half * 512:(half + 1) * 512], k == 0, k == KT - 1)
                            if half == 0:
                                refill(ins)
                        done()
                    ins.then_inc(psum_full, 1)
                pe.wait_ge(*E.taken(name, "row", blocks - 1))
                ps = group(name)
                for half in range(2):
                    rows = slice(64 * half, 64 * half + 2)
                    for i in range(4 * blocks):
                        at = half * 512 + 2 * i
                        ins = nc.tensor.transpose(ps[:, at:at + 2], modRow[name][rows, i * P:(i + 1) * P],
                                                  C("ident")[rows, rows])
                        if half == 0 and i == 0:
                            refill(ins)
                ins.then_inc(psum_full, 1)

            def statistics(name, nk, chunks, sq, slots=3):
                ps = group("stat", name)
                for k in range(nk):
                    pe.wait_ge(*E.next("squares_ready"))
                    for ci, (c0, n) in enumerate(chunks):
                        ins = mm(ps[:, ci * 512:ci * 512 + n], C("ones"), sq[:, k % slots, c0:c0 + n],
                                 k == 0, k == nk - 1)
                    if k < nk - 1:
                        ins.then_inc(sem("squares_used"), 1)
                ins.then_inc(psum_full, 1)

            def rotations(name, rot, src, tiles, M=P):
                for t in tiles:
                    ps = group("rot", *name, t)
                    ins = mm(ps[0:M, 0:SEQ], rot[0:M, 0:M], src(t), True, True)
                    ins.then_inc(psum_full, 1)

            def attention(name, score, value, pw):
                pP, pT, pO_ = pw
                us = units(ATT[name])
                nq = len(ATT[name])

                def scores(i):
                    ps = group("S", name, i)
                    mms = score(ps, *us[i])
                    for n, (o, a, b, st, sp) in enumerate(mms):
                        ins = mm(o, a, b, st, sp)
                    ins.then_inc(psum_full, 1)

                def turn(i):
                    pe.wait_ge(*E.taken("S", name, i))
                    ps = group("T", name, i)
                    _, tiles = spans(name, us[i][2])
                    for b in range(len(tiles)):
                        ins = flip(ps[:, b * P:(b + 1) * P], pP[:, i % 2, b * P:(b + 1) * P])
                    ins.then_inc(psum_full, 1)

                def outputs(i):
                    pe.wait_ge(*E.taken("T", name, i))
                    t, hh, qi = us[i]
                    o = psum[:, (6 + t % 2) * 512 + qi * P + hh * 64:(6 + t % 2) * 512 + qi * P + hh * 64 + 64]
                    _, tiles = spans(name, qi)
                    for b, kt in enumerate(tiles):
                        ins = mm(o, pT[:, i % 2, b * P:(b + 1) * P], value(t, hh, kt), b == 0,
                                 b == len(tiles) - 1)
                    ins.then_inc(sem("outputs_done"), 1)

                def back(t):
                    pe.wait_ge(*E.next("outputs_scaled"))
                    ps = group("O", name, t)
                    for qi in range(nq):
                        ins = flip(ps[:, qi * P:(qi + 1) * P], pO_[:, t % 2, qi * P:(qi + 1) * P])
                    ins.then_inc(psum_full, 1)

                scores(0)
                for i in range(len(us)):
                    if i + 1 < len(us):
                        scores(i + 1)
                    turn(i)
                    if i >= 1:
                        outputs(i - 1)
                    if i >= 2 * nq + 2 and (i - 2) % (2 * nq) == 0:
                        back((i - 2) // (2 * nq) - 1)
                outputs(len(us) - 1)
                back(3)

            def merge(key, chunks, ys, tags, src0=0):
                for f in range(0, KT, 2):
                    for b in range(3):
                        for g in (f, f + 1):
                            project_tile(("gate", *tags, b, g), ("gate", key, b, g), chunks)
                        w = split(weights("branch", *tags, b, f), a=4)
                        for i, g in enumerate((f, f + 1)):
                            project(("branch", key, b, g), w[:, :, i * P:(i + 1) * P], ys[b], 4, chunks,
                                    src0=src0)
                        done()

            def w_out(key, tiles, chunks):
                for f in range(KT):
                    project_tile(tiles(f), ("out", key, f), chunks, first=f == 0, src=(mHi, mLo),
                                 ready="merged_parts")

            pe.wait_ge(*E.next("cond_ready"))
            modulation("mod1", 6, cond)
            statistics("mix", KT, ALL, nSq)
            for t in range(4):
                project_tile(("q_r", t), ("q_r", t), IMG, first=t == 0)
            for t in range(4):
                project_tile(("k_r", t), ("k_r", t), ALL)
            for t in range(4):
                pe.wait_ge(*E.taken("q_r", t))
            rotations(("q_r",), C("rot_r"), lambda t: rQ[:, t, :], range(4))
            for t in range(4):
                pe.wait_ge(*E.taken("k_r", t))
            rotations(("k_r",), C("rot_r"), lambda t: rK[:, t, CTX:TOK], range(4))
            project_tokens([("v_r", i) for i in range(4)], ("v_r",))
            for t in range(4):
                project_tile(("g_r", t), ("g_r", t), IMG)
            pe.wait_ge(*E.next("rotated", 8))
            for p in range(TT // 2):
                pe.wait_ge(*E.taken("v_r", p))

            def ret_scores(h):
                for pr in range(3):
                    ps = group("rS", h, pr)
                    for i in range(2):
                        kt = 2 * pr + i
                        ins = mm(ps[:, i * 512:(i + 1) * 512], rK[:, h, kt * P:(kt + 1) * P], rQ[:, h, :],
                                 True, True)
                    ins.then_inc(psum_full, 1)

            def ret_values(h):
                ps = group("rY", h)
                for pr in range(3):
                    pe.wait_ge(*E.taken("rS", h, pr))
                    n = 3 * h + pr
                    for i in range(2):
                        kt = 2 * pr + i
                        ins = mm(ps[:, 0:SEQ], rV[:, kt, h * P:(h + 1) * P], rP[:, n % 4, i * 512:(i + 1) * 512],
                                 kt == 0, kt == TT - 1)
                ins.then_inc(psum_full, 1)

            for h in range(4):
                ret_scores(h)
                ret_values(h)
            for kind in ("mean", "var"):
                for h in range(4):
                    if kind == "mean":
                        pe.wait_ge(*E.taken("rY", h))
                        src = A3[:, h, :]
                    else:
                        pe.wait_ge(*E.next("squares_ready"))
                        src = rSq[:, h, :]
                    ps = group("r" + kind, h)
                    ins = mm(ps[:, 0:SEQ], C("ones"), src, True, True)
                    ins.then_inc(psum_full, 1)
            for t in range(4):
                project_tile(("q_w", t), ("q_w", t), IMG)
            project_tile(("k_w", 0), ("k_w",), ALL)
            hi, lo = weight_parts("v_w", 0)
            ps = group("v_w")
            for t in range(TT):
                for k in range(KT):
                    for n, (w, h) in enumerate(part_products(split(hi, a=KT), split(lo, a=KT))):
                        ins = mm(ps[:, t * P:(t + 1) * P], h[:, k, t * P:(t + 1) * P], w[:, k, :],
                                 k == 0 and n == 0, k == KT - 1 and n == 2)
            ins.then_inc(psum_full, 1)
            split_reader.append((psum_full, state["g"]))
            done()
            for t in range(4):
                pe.wait_ge(*E.taken("q_w", t))
            rotations(("q_w",), C("rot_w"), lambda t: wQ[:, t, :], range(4))
            pe.wait_ge(*E.taken("k_w"))
            rotations(("k_w",), C("rot_w"), lambda t: wK[:, CTX:TOK], range(1))
            pe.wait_ge(*E.next("rotated", 5))
            pe.wait_ge(*E.taken("v_w"))

            def win_score(ps, t, hh, qi):
                L, tiles = spans("win", qi)
                q = wQ[hh * 64:hh * 64 + 64, t, qi * P:(qi + 1) * P]
                k = wK[hh * 64:hh * 64 + 64, :]
                lo = tiles[0] * P
                r = [(ps[:, 512 - L:512], q, k[:, lo:lo + L], True, False)]
                if qi > 0:
                    r.append((ps[:, 512 - L:512 - L + P], C("ident"), C("wleft"), False, qi == 3))
                if qi < 3:
                    r.append((ps[:, 512 - P:512], C("ident"), C("wright"), False, True))
                r.append((ps[:, 512:768], q, k[:, 0:CTX], True, True))
                return r

            attention("win", win_score, lambda t, hh, kt: wV[:, kt, hh * 64:hh * 64 + 64], attn_area(AT1))
            for t in range(4):
                project_tile(("q_n", t), ("q_n", t), IMG)
            for t in range(4):
                project_tile(("k_n", t), ("k_n", t), ALL)
            project_tokens([("v_n", i) for i in range(4)], ("v_n",))
            for t in range(4):
                pe.wait_ge(*E.taken("q_n", t))
                pe.wait_ge(*E.taken("k_n", t))
            for p in range(TT // 2):
                pe.wait_ge(*E.taken("v_n", p))
            pe.wait_ge(*E.next("bias_ready", 8))

            def na_score(ps, t, hh, qi):
                q = nQ[hh * 64:hh * 64 + 64, t, qi * P:(qi + 1) * P]
                k = nK[hh * 64:hh * 64 + 64, t, :]
                a0 = 6 - 2 * qi
                return [(ps[:, 0:512], q, k[:, CTX:TOK], True, False),
                        (ps[:, 0:512], C("flip"), nB[:, 2 * t + hh, a0 * 64:(a0 + 8) * 64], False, True),
                        (ps[:, 512:768], q, k[:, 0:CTX], True, True)]

            attention("na", na_score,
                      lambda t, hh, kt: nV[:, kt, (2 * t + hh) * 64:(2 * t + hh) * 64 + 64], attn_area(AT2))
            for n in ("win", "na"):
                pe.wait_ge(*E.taken("O", n, 3))
            pe.wait_ge(*E.next("retention_ready", 4))
            merge(0, IMG, [split(Y, a=4) for Y in (YA, YB, YC)], (), src0=CTX)
            w_out(0, lambda f: ("w_out", f), IMG)
            statistics("ffn", KT, IMG, nSq)
            pe.wait_ge(*E.next("ffn_hidden_ready", KT))
            for tt in range(4):
                ps = group("HT", tt)
                for k in range(KT):
                    ins = flip(ps[:, k * P:(k + 1) * P], H3[:, k, CTX + tt * P:CTX + (tt + 1) * P])
                ins.then_inc(psum_full, 1)
            pe.wait_ge(*E.next("router_loaded", 16))
            ps = group("router")
            for tt in range(4):
                for k in range(KT):
                    ins = mm(ps[:, tt * NE:(tt + 1) * NE], H3[:, k, CTX + tt * P:CTX + (tt + 1) * P], eWR[:, k, :],
                             k == 0, k == KT - 1)
            ins.then_inc(psum_full, 1)
            pe.wait_ge(*E.next("router_softmax"))
            ps = group("affT")
            for tt in range(4):
                ins = flip(ps[0:NE, tt * P:(tt + 1) * P], aff[:, tt, :])
            ins.then_inc(psum_full, 1)
            pe.wait_ge(*E.next("slots_ready"))
            ps = group("pos")
            for tt in range(4):
                ins = nc.tensor.transpose(ps[:, tt * NE:(tt + 1) * NE], eC[0:NE, tt * P:(tt + 1) * P],
                                          C("ident")[0:NE, 0:NE])
            ins.then_inc(psum_full, 1)
            pe.wait_ge(*E.next("assigned", 4))
            for q in range(4):
                ps = group("PG", q)
                for i in range(2):
                    for tt in range(4):
                        j = 2 * q + i
                        ins = flip(ps[:, i * 512 + tt * P:i * 512 + (tt + 1) * P], ePg[:, tt, j * P:(j + 1) * P])
                ins.then_inc(psum_full, 1)
            for q in range(4):
                pe.wait_ge(*E.taken("PG", q))
                pe.wait_ge(*E.taken("HT", q))

            def gather(ps, j, k):
                for tt in range(4):
                    ins = mm(ps[:, k * P:(k + 1) * P], eHT[:, tt, k * P:(k + 1) * P],
                             eP[:, tt, bass.ds(j * P, P)], tt == 0, tt == 3)
                return ins

            def expert_product(tag, kind, j, src, before=lambda e, k: None,
                               after=lambda e, k: None):
                ps = group(tag, kind)
                for k in range(KT):
                    for e in range(2):
                        w = weights((kind, j, e), k)
                        before(e, k)
                        for half in range(2):
                            ins = mm(ps[e * 64:e * 64 + 64, half * 512:(half + 1) * 512],
                                     src[:, k, e * 64:(e + 1) * 64], w[:, half * 512:(half + 1) * 512],
                                     k == 0, k == KT - 1)
                            if half == 0:
                                refill(ins)
                        done()
                        if (e, k) == (1, KT - 1):
                            ins.then_inc(psum_full, 1)
                        after(e, k)

            def pair(tag, named, j, following):
                g = state["g"] - 1

                def combine_step(e, k):
                    if e:
                        f = k
                        if f == 0:
                            pe.wait_ge(psum_free[g % 3], E.at(g // 3 + 1, "slot"))
                        pe.wait_ge(*E.next("combined"))
                        mm(psum[:, (6 + f % 2) * 512:(7 + f % 2) * 512], eYE[:, f * P:(f + 1) * P],
                           arena[:, bass.ds(j * SEQ + (XP + 4096 - SEQ), SEQ)], True, True)\
                            .then_inc(sem("combine_product"), 1)

                expert_product(tag, "exp_gate", named, eXE, after=combine_step)
                def gather_step(e, k):
                    if following is not None and e:
                        f = k
                        if f == 0:
                            group(tag, "XE")
                        ins = gather(cols(tag, "XE"), following, f)
                        if f == KT - 1:
                            ins.then_inc(psum_full, 1)

                expert_product(tag, "exp_up", named, eXE, after=gather_step)
                for half in range(2):
                    if half == 0:
                        pe.wait_ge(*E.next("expert_hidden"))
                    else:
                        pe.wait_ge(*E.taken(tag, "exp_up"))
                    ps = group(tag, "HF", half)
                    for i in range(4):
                        f = 4 * half + i
                        ins = flip(ps[:, i * P:(i + 1) * P], eHID[:, f * P:(f + 1) * P])
                    ins.then_inc(psum_full, 1)

                def transposed(e, k):
                    if e == 0 and k % 4 == 0:
                        pe.wait_ge(*E.taken(tag, "HF", k // 4))

                expert_product(tag, "exp_down", named, eHF, transposed)
                if following is not None:
                    pe.wait_ge(*E.taken(tag, "XE"))

            ps = group("XE", "first")
            for k in range(KT):
                ins = gather(ps, 0, k)
            ins.then_inc(psum_full, 1)
            pe.wait_ge(*E.taken("XE", "first"))
            while state["g"] % 3:
                ps = group("pad", state["g"])
                ins = mm(ps[:, 0:2], C("ident"), C("ident")[:, 0:2], True, True)
                ins.then_inc(psum_full, 1)
            assert state["owed"] == 1 and state["tile"] % 2 == 0, state
            assert state["ended"] == state["tile"]
            turns = PAIRS - 1
            with pe.Fori(0, turns) as it:
                E.begin(it, {"groups": 6, "slot": 2, "ring": 16 * 24 // NSLOT, "expert_hidden": 1,
                             "combined": 8})
                pair("loop", 0, it, it + 1)
                assert state["owed"] == 1
                E.end(turns)
            state["g"] += 6 * (turns - 1)
            state["tile"] += 48 * (turns - 1)
            state["ended"] = state["tile"]
            pair("last", PAIRS - 1, PAIRS - 1, None)
            pe.wait_ge(*E.taken("last", "exp_down"))
            for q in range(4):
                ps = group("comb", q)
                for i in range(2):
                    f = 2 * q + i
                    ins = mm(ps[:, i * 512:(i + 1) * 512], eYE[:, f * P:(f + 1) * P], ePG[:, PAIRS - 1, :],
                             True, True)
                ins.then_inc(psum_full, 1)
            statistics("final", KT, IMG, nSq)
            for l in LAYERS:
                own = ALL if l == 0 else IMG
                if l == 0:
                    pe.wait_ge(*E.next("cond2_ready"))
                modulation(("mod2", l), 3, cond2)
                statistics(("pre", l), KT, ALL, nSq)
                for t in range(2):
                    project_tile((("gq", l), t), ("gq", l, t), own, first=t == 0)
                for t in range(2):
                    project_tile((("gk", l), t), ("gk", l, t), ALL)
                project_tokens([(("gv", l), i) for i in range(4)], ("gv", l))
                project_tile(("small", l), ("small", l), ALL)
                w2 = weights("decay_w2", l)
                pe.wait_ge(*E.taken("small", l))
                for d in range(2):
                    for t in range(2):
                        ps = group("decay", l, d, t)
                        for ci, (c0, n) in enumerate(ALL):
                            ins = mm(ps[:, ci * 512:ci * 512 + n], w2[32 * d:32 * d + 16, t * P:(t + 1) * P],
                                     gSM[32 * d:32 * d + 16, c0:c0 + n], True, True)
                        ins.then_inc(psum_full, 1)
                done()
                for t in range(2):
                    project_tile((("mq", l), t), ("mq", l, t), own)
                pe.wait_ge(*E.next("decayed_keys", 2))
                for d in range(2):
                    for cp in range(3):
                        ps = group("KT", l, d, cp)
                        for i in range(2):
                            for t in range(2):
                                c = 2 * cp + i
                                ins = flip(ps[:, (2 * i + t) * P:(2 * i + t + 1) * P],
                                           gT1[:, 2 * d + t, c * P:(c + 1) * P])
                        ins.then_inc(psum_full, 1)
                for p in range(TT // 2):
                    pe.wait_ge(*E.taken("gv", l, p))
                for d in range(2):
                    for cp in range(3):
                        pe.wait_ge(*E.taken("KT", l, d, cp))
                for d, order in enumerate(SCAN):
                    for c in order[:-1]:
                        ps = group("U", l, d, c)
                        for h in range(4):
                            hp = 64 * (h % 2)
                            at = d * 1536 + c * 256 + (h // 2) * P + hp
                            ins = mm(ps[hp:hp + 64, (h // 2) * P:(h // 2 + 1) * P], gKT[:, at:at + 64],
                                     gV[:, c, h * P:(h + 1) * P], True, True)
                        ins.then_inc(psum_full, 1)
                for d in range(2):
                    pe.wait_ge(*E.taken("U", l, d, SCAN[d][-2]))
                for c in OWN_CHUNKS[l]:
                    QI, QS, KS, QZ = gChunk(c % 2)
                    pe.wait_ge(*E.next("chunk_operands"))
                    ps = group("A", l, c)
                    for d in range(2):
                        for t in range(2):
                            for s in range(4):
                                at = ((2 * d + t) * 4 + s) * 64
                                ins = mm(ps[:, at:at + 64], KS[:, d, t, s, :],
                                         QZ[:, 2 * d + t, s, :, :].rearrange("p b n -> p (b n)"), True, True)
                    ins.then_inc(psum_full, 1)
                    pe.wait_ge(*E.next("chunk_weights"))
                    ps = group("Y", l, c)
                    for h in range(4):
                        hp = 64 * (h % 2)
                        terms = [(gV[:, c, h * P:(h + 1) * P], gAT[:, h * P:(h + 1) * P])]
                        for d in range(2):
                            if c != SCAN[d][0]:
                                terms.append((gS[hp:hp + 64, d, c, h // 2, :],
                                              QI[hp:hp + 64, 2 * d + h // 2, :]))
                        for n, (a, b) in enumerate(terms):
                            at = (h % 2) * 512 + (h // 2) * P
                            ins = mm(ps[:, at:at + P], a, b, n == 0, n == len(terms) - 1)
                    ins.then_inc(psum_full, 1)
                for h in range(4):
                    statistics(("gla", l, h), 1, own, gSq[:, h:h + 1, :])
                for t in range(4):
                    project_tile((("ggate", l), t), ("ggate", l, t), own)
                project_tile((("mkv", l), 0), ("mkv", l), ALL)
                for t in range(2):
                    pe.wait_ge(*E.next("squares_ready"))
                    if t == 0:
                        ps = group("stat", ("qn", l))
                    for ci, (c0, n) in enumerate(own):
                        ins = mm(ps[:, ci * 512:ci * 512 + n], C("ones"), mSq[:, 0, c0:c0 + n],
                                 t == 0, t == 1)
                    if t == 0:
                        ins.then_inc(sem("squares_used"), 1)
                ins.then_inc(psum_full, 1)
                statistics(("kvn", l), 1, ALL, mSq)
                pe.wait_ge(*E.next("rank_norms", 3))
                for hb in (0, 4):
                    w = weights("uq", l, hb)[:, 0:768].rearrange("p (a n) -> p a n", a=2)
                    for h in range(hb, hb + 4):
                        project(("uq", l, h), w[:, :, (h - hb) * 96:(h - hb + 1) * 96], mRaw, 2, own, M=96)
                    done()
                w = weights("ukv", l)
                kv1 = mKV.rearrange("p (a n) -> p a n", a=1)
                for h in range(8):
                    project(("uk", l, h), w[:, h * 64:(h + 1) * 64].rearrange("p (a n) -> p a n", a=1),
                            kv1, 1, ALL, M=64)
                for t in range(TT):
                    ps = group("uv", l, t)
                    ins = mm(ps[:, 0:512], mKV[:, t * P:(t + 1) * P], w[:, 512:1024], True, True)
                    ins.then_inc(psum_full, 1)
                done()
                for h in range(8):
                    pe.wait_ge(*E.taken("uq", l, h))
                rotations(("uq", l), C("rot_m"), lambda h: mQ[0:96, h, CTX:TOK], range(8), M=96)
                ps = group("rot", "kr", l)
                ins = mm(ps[64:96, 0:SEQ], C("rot_m")[64:96, 64:96], mKR[64:96, CTX:TOK], True, True)
                ins.then_inc(psum_full, 1)
                pe.wait_ge(*E.next("rotated", 8))
                pe.wait_ge(*E.next("keys_complete", 8))
                for t in range(TT):
                    pe.wait_ge(*E.taken("uv", l, t))

                def mla_score(q0, whole):
                    def score(ps, t, hh, qi):
                        h = 2 * t + hh
                        q = mQ[0:96, h, q0 + qi * P:q0 + (qi + 1) * P]
                        r = [(ps[:, 0:512], q, mK[0:96, h, CTX:TOK], True, True)] if whole else []
                        return r + [(ps[:, 512:768], q, mK[0:96, h, 0:CTX], True, True)]
                    return score

                mla_value = lambda t, hh, kt: mV[:, kt, (2 * t + hh) * 64:(2 * t + hh) * 64 + 64]
                attention(("mla", l), mla_score(CTX, True), mla_value, attn_area(MW))
                if l == 0:
                    attention(("mlac", 0), mla_score(0, False), mla_value, attn_area(MW))
                for t in range(4):
                    project_tile((("mgate", l), t), ("mgate", l, t), own)
                for g in range(4):
                    project_tile((("px", l, g), 0), ("px", l, g), own)
                    project_tile((("pgate", l, g), 0), ("pgate", l, g), own)
                w = split(weights("pool_w", l)[:, 0:512], a=4)
                for g in range(4):
                    pe.wait_ge(*E.next("pooled"))
                    ps = group("mixed", l, g)
                    for ci, (c0, n) in enumerate(own):
                        ins = mm(ps[:, ci * 512:ci * 512 + n], w[:, g, :], pO[:, g, c0:c0 + n], True, True)
                    ins.then_inc(psum_full, 1)
                done()
                pe.wait_ge(*E.next("branches_ready", 4))
                merge(("l", l), own, [YM, YP, YG], (l,))
                w_out(("l", l), lambda f: (("w_out", l), f), own)
                statistics(("post", l), KT, own, nSq)
            assert state["tile"] == len(plan) and len(split_reader) == len(split_tiles)
            totals["groups"] = state["g"]


        @block.scalar
        def _(act):
            E = Eng(act, "act")
            act_ = nc.scalar.activation

            def squares(src, nk, sq, view=lambda a: a, slots=3, before=None):
                for k in range(nk):
                    if before:
                        before(k)
                    if k >= slots:
                        act.wait_ge(*E.next("squares_used"))
                    act_(view(sq[:, k % slots, :]), view(src[:, k, :]), ACT.Square)\
                        .then_inc(*E.sig("squares_ready"))
                if nk > slots:
                    act.wait_ge(*E.next("squares_used", slots - 1))

            def root(rs, need="var_ready"):
                act.wait_ge(*E.next(need))
                act_(rs, rs, ACT.Sqrt).then_inc(*E.sig("std_ready"))

            def high():
                i = E.made.get("high_written", 0)
                n = split_tiles[i]
                act.wait_ge(loaded[n // 2 % NSLOT], 16 * (n // 2 // NSLOT + 1))
                if i >= 2:
                    act.wait_ge(*split_reader[i - 2])
                at = (n // 2 % NSLOT) * UNIT + (n % 2) * 1024
                act_(parts[:, i % 2, 0, :], ring[:, at:at + 1024], ACT.Copy).then_inc(*E.sig("high_written"))

            def token_evac(name, dst):
                for i in range(4):
                    high()
                for p in range(TT // 2):
                    evac((*name, p), dst[:, 2 * p:2 * p + 2, :].rearrange("p a n -> p (a n)"), n=1024)

            def shift_in(mod, col, chunks, parted=True):
                for k in range(KT):
                    act.wait_ge(*E.next("scaled_ready"))
                    if chunks is ALL:
                        act_(H3[:, k, 0:CTX], H3[:, k, 0:CTX], ACT.Identity, bias=mod[:, col + k, 1:2])
                    ins = act_(H3[:, k, CTX:TOK], H3[:, k, CTX:TOK], ACT.Identity, bias=mod[:, col + k, 0:1])
                    if not parted:
                        ins.then_inc(*E.sig("ffn_hidden_ready"))
                        continue
                    ins.then_inc(*E.sig("act_step"))
                    act.wait_ge(*E.own())
                    act_(Hhi[:, k, :], H3[:, k, :], ACT.Copy).then_inc(*E.sig("hidden_high"))

            def evac(name, dst, chunks=None, n=None, func=ACT.Copy, rows=(0, P), ahead=False, **kw):
                if ahead:
                    high()
                act.wait_ge(*E.written(*name))
                ps = cols(*name)[rows[0]:rows[1], :]
                src = ps[:, 0:n] if chunks is None else bank_view(ps, chunks)
                act_(dst, src, func, **kw).then_inc(*E.read(*name))

            def attention(name, pw, sink=False, before=None):
                pP, pT, _ = pw
                us = units(ATT[name])
                base = unit_base[name]

                def exps(i):
                    t, hh, qi = us[i]
                    L, _ = spans(name, qi)
                    col = (t % 2) * 8 + qi * 2 + hh
                    act.wait_ge(*E.next("negmax_ready"))
                    if sink:
                        h = t + 4 * hh
                        act_(esink[:, col:col + 1], negmax[:, col:col + 1], ACT.Exp,
                             bias=Pm("sink")[:, h:h + 1])
                    if i >= 2:
                        act.wait_ge(*E.written("T", name, i - 2))
                    elif before:
                        act.wait_ge(*E.written("T", before, 8 * len(ATT[before]) - 1))
                    act.wait_ge(*E.written("S", name, i))
                    ps = cols("S", name, i)
                    act_(pP[:, i % 2, 0:L + CTX], ps[:, 512 - L:768], ACT.Exp,
                                bias=negmax[:, col:col + 1], accum_out=sums[:, col:col + 1]).then_inc(*E.read("S", name, i))

                exps(0)
                for i in range(len(us)):
                    if i + 1 < len(us):
                        exps(i + 1)
                    if i % 2:
                        act.wait_ge(*E.written("T", name, i))
                        ps = cols("T", name, i)
                        n = len(spans(name, us[i][2])[1]) * P
                        if base + i > 1:
                            act.wait_ge(*E.upto("outputs_done", base + i - 1))
                        act_(pT[:, i % 2, 0:n], ps[:, 0:n], ACT.Copy).then_inc(*E.read("T", name, i))

            def gates(key, chunks):
                base = E.seen.get("merged_ready", 0)
                for f in range(0, KT, 2):
                    if f:
                        act.wait_ge(*E.upto("merged_ready", base + f))
                    for b in range(3):
                        for g in (f, f + 1):
                            high()
                            evac(("gate", key, b, g), tok_view(mSG[:, 2 * b + g % 2, :], chunks),
                                 chunks, func=ACT.Sigmoid)
                act.wait_ge(*E.upto("merged_ready", base + KT))
                v = slice(0, TOK) if chunks is ALL else slice(CTX, TOK)
                for k in range(KT):
                    act_(mHi[:, k, v], mMG[:, k, v], ACT.Copy).then_inc(*E.sig("merged_high"))

            act.wait_ge(*E.next("params_loaded", 16))
            act_(cond.rearrange("p a b -> p (a b)"), Pm("cond"), ACT.Silu).then_inc(*E.sig("cond_ready"))
            act_(cond2.rearrange("p a b -> p (a b)"), Pm("cond2"), ACT.Silu).then_inc(*E.sig("cond2_ready"))
            act_(lt1, Pm("decay"), ACT.Abs).then_inc(*E.sig("act_step"))
            act.wait_ge(*E.own())
            act_(lt2, lt1, ACT.Exp, scale=-1.0).then_inc(*E.sig("act_step"))
            act.wait_ge(*E.own())
            act_(lt1, lt2, ACT.Ln, bias=1.0).then_inc(*E.sig("decay_ln"))
            act.wait_ge(*E.next("residual_loaded", 16))
            squares(R3, KT, nSq)
            high()
            high()
            root(nRs)
            shift_in(modA, 0, ALL)
            for t in range(4):
                evac(("q_r", t), rQ[:, t, :], IMG, ahead=True)
            for t in range(4):
                evac(("k_r", t), tok_view(rK[:, t, :], ALL), ALL, ahead=True)
            token_evac(("v_r",), rV)
            for t in range(4):
                evac(("g_r", t), rSG[:, t, :], IMG, func=ACT.Silu, ahead=True)
            for h in range(4):
                act.wait_ge(*E.next("exponent_ready"))
                e = rE if h % 2 == 0 else YC[:, 0:DW]
                act_(e, e, ACT.Exp).then_inc(*E.sig("decay_ready"))
                if h:
                    evac(("rY", h - 1), A3[:, h - 1, :], n=512)
            evac(("rY", 3), A3[:, 3, :], n=512)
            for h in range(4):
                act.wait_ge(*E.taken("rmean", h))
                act_(rSq[:, h, :], A3[:, h, :], ACT.Square).then_inc(*E.sig("squares_ready"))
            for h in range(4):
                act.wait_ge(*E.taken("rvar", h))
                act_(rRs[:, h, :], rRs[:, h, :], ACT.Sqrt).then_inc(*E.sig("std_ready"))
            act.wait_ge(*E.own())
            act_(tick[:, 0:1], C("eps"), ACT.Copy).then_inc(*E.sig("act_stage_done"))
            for t in range(4):
                evac(("q_w", t), wQ[:, t, :], IMG, scale=0.125, ahead=True)
            evac(("k_w",), tok_view(wK, ALL), ALL, ahead=True)
            evac(("v_w",), wV.rearrange("p a n -> p (a n)"), n=TOK, ahead=True)
            act.wait_ge(*E.next("dve_stage_done"))
            act.wait_ge(*E.next("pool_stage_done"))
            attention("win", attn_area(AT1), sink=True)
            act.wait_ge(*E.own())
            act_(tick[:, 0:1], C("eps"), ACT.Copy).then_inc(*E.sig("act_stage_done"))
            for t in range(4):
                evac(("q_n", t), nQ[:, t, :], IMG, scale=0.125, ahead=True)
            for t in range(4):
                evac(("k_n", t), tok_view(nK[:, t, :], ALL), ALL, ahead=True)
            token_evac(("v_n",), nV)
            act.wait_ge(*E.next("dve_stage_done"))
            act.wait_ge(*E.next("pool_stage_done"))
            attention("na", attn_area(AT2))
            act.wait_ge(*E.own())
            act_(tick[:, 0:1], C("eps"), ACT.Copy).then_inc(*E.sig("act_stage_done"))
            act.wait_ge(*E.next("dve_stage_done"))
            act.wait_ge(*E.next("pool_stage_done"))
            gates(0, IMG)
            for f in range(KT - 2):
                high()
            img = lambda a: a[:, CTX:TOK]
            squares(R3, KT, nSq, img, before=lambda k: act.wait_ge(*E.next("residual_ready")))
            root(img(nRs))
            shift_in(modA, 24, IMG, parted=False)
            act.wait_ge(*E.own())
            act_(tick[:, 0:1], C("eps"), ACT.Copy).then_inc(*E.sig("act_stage_done"))
            act.wait_ge(*E.next("dve_stage_done"))
            act.wait_ge(*E.next("pool_stage_done"))
            for tt in (0, 2):
                evac(("HT", tt), eHT[:, tt, :], n=1024)
            act.wait_ge(*E.next("router_max"))
            act.wait_ge(*E.written("router"))
            ps = cols("router")
            for tt in range(4):
                ins = act_(aff[:, tt, :], ps[:, tt * NE:(tt + 1) * NE], ACT.Exp, bias=m16[:, tt:tt + 1],
                           accum_out=s16[:, tt:tt + 1])
            ins.then_inc(*E.read("router"))
            for q in (0, 2):
                evac(("PG", q), ePG[:, 2 * q:2 * q + 2, :].rearrange("p a n -> p (a n)"), n=1024)

            def pair(tag):
                evac((tag, "exp_gate"), eSG, n=1024, func=ACT.Silu)
                evac((tag, "HF", 0), eHF[:, 0:4, :].rearrange("p a n -> p (a n)"), n=512)
                evac((tag, "exp_down"), eYE, n=1024)

            with act.Fori(0, PAIRS - 1) as it:
                E.begin(it, {"groups": 6, "slot": 2})
                pair("loop")
                E.end(PAIRS - 1)
            pair("last")
            squares(R3, KT, nSq, img, before=lambda k: act.wait_ge(*E.next("residual_ready")))
            root(img(nRs))
            for l in LAYERS:
                own = ALL if l == 0 else IMG
                view = (lambda a: a) if l == 0 else img
                if l == 0:
                    act.wait_ge(*E.next("ctx2_loaded", 16))
                    act.wait_ge(*E.next("residual_ready", KT))
                    squares(R3, KT, nSq)
                else:
                    squares(R3, KT, nSq, before=lambda k: act.wait_ge(*E.next("residual_updated")))
                high()
                high()
                root(nRs)
                act.wait_ge(*E.next("residual_saved", 16))
                shift_in(modB, 0, ALL)
                for t in range(2):
                    evac(("gq", l, t), tok_view(gQ[:, t, :], own), own, scale=0.125, ahead=True)
                for t in range(2):
                    evac(("gk", l, t), tok_view(gK[:, t, :], ALL), ALL, ahead=True)
                token_evac(("gv", l), gV)
                evac(("small", l), tok_view(gSM, ALL), ALL, ahead=True)
                for d in range(2):
                    for t in range(2):
                        act.wait_ge(*E.written("decay", l, d, t))
                        ps = cols("decay", l, d, t)
                        bias = Pm(("afb", "abb")[d] + str(l))[:, t:t + 1]
                        act_(tok_view(gT1[:, 2 * d + t, :], ALL), bank_view(ps, ALL), ACT.Abs, bias=bias)\
                            .then_inc(*E.sig("decay_abs"))
                flat = gT1.rearrange("p a n -> p (a n)")
                act.wait_ge(*E.next("decay_abs", 4))
                act_(flat, flat, ACT.Exp, scale=-1.0).then_inc(*E.sig("act_step"))
                act.wait_ge(*E.own())
                act_(flat, flat, ACT.Ln, bias=1.0).then_inc(*E.sig("gla_ln"))
                act.wait_ge(*E.next("scans_ready"))
                last = gB.rearrange("p a (c n) -> p (a c) n", n=P)[:, :, P - 1:P]
                act_(expT.rearrange("p (a b) -> p a b", b=1), last, ACT.Exp, scale=1.0 / 16)\
                    .then_inc(*E.sig("chunk_decay_ready"))
                for t in range(2):
                    evac(("mq", l, t), tok_view(mRaw[:, t, :], own), own, ahead=True)
                act.wait_ge(*E.next("key_exponents"))
                act_(flat, flat, ACT.Exp, scale=1.0 / 16).then_inc(*E.sig("key_decays"))
                for d in range(2):
                    for cp in range(3):
                        at = d * 1536 + cp * 512
                        evac(("KT", l, d, cp), gKT[:, at:at + 512], n=512)

                def chunk_exps(c):
                    QI, QS, KS, _ = gChunk(c % 2)
                    act.wait_ge(*E.next("chunk_exponents"))
                    act_(QS, QS, ACT.Exp, scale=1.0 / 16)
                    ks = KS.rearrange("p d t s n -> p (d t s n)")
                    act_(ks, ks, ACT.Exp, scale=1.0 / 16)
                    act_(QI, gB[:, :, c * P:(c + 1) * P], ACT.Exp, scale=1.0 / 16)\
                        .then_inc(*E.sig("chunk_decays"))

                chunk_exps(OWN_CHUNKS[l][0])
                for c in OWN_CHUNKS[l]:
                    if c + 1 < TT:
                        chunk_exps(c + 1)
                    act.wait_ge(*E.written("Y", l, c))
                    ps = cols("Y", l, c)
                    y = YG[:, :, c * P:(c + 1) * P].rearrange("p (t b) n -> p t b n", b=2)
                    src = split(ps, b=2)[:, :, 0:256].rearrange("p b (t n) -> p t b n", t=2)
                    act_(y, src, ACT.Copy).then_inc(*E.read("Y", l, c))
                act.wait_ge(*E.taken("Y", l, TT - 1))
                for h in range(4):
                    act_(view(gSq[:, h, :]), view(YG[:, h, :]), ACT.Square).then_inc(*E.sig("squares_ready"))
                for h in range(4):
                    act.wait_ge(*E.taken("stat", ("gla", l, h)))
                    act_(view(gRs[:, h, :]), view(gRs[:, h, :]), ACT.Sqrt).then_inc(*E.sig("std_ready"))
                base = 8 * l
                for t in range(4):
                    if t >= 2:
                        act.wait_ge(*E.upto("silu_used", base + t - 1))
                    evac(("ggate", l, t), tok_view(SILU[:, t % 2, :], own), own, func=ACT.Silu, ahead=True)
                act.wait_ge(*E.own())
                act_(tick[:, 0:1], C("eps"), ACT.Copy).then_inc(*E.sig("act_stage_done"))
                act.wait_ge(*E.next("dve_stage_done"))
                act.wait_ge(*E.next("pool_stage_done"))
                act_(mKR[64:96, :], gSM[64:96, :], ACT.Copy).then_inc(*E.sig("rope_key_ready"))
                act.wait_ge(*E.next("rope_key_ready"))
                for t in range(2):
                    if t:
                        act.wait_ge(*E.next("squares_used"))
                    act_(view(mSq[:, 0, :]), view(mRaw[:, t, :]), ACT.Square).then_inc(*E.sig("squares_ready"))
                root(view(mRs))
                act.wait_ge(*E.written("mkv", l))
                ps = cols("mkv", l)
                act_(tok_view(mSq[:, 0, :], ALL), bank_view(ps, ALL), ACT.Square)\
                    .then_inc(*E.sig("squares_ready"))
                evac(("mkv", l), tok_view(mKV, ALL), ALL, ahead=True)
                root(mRs)
                for h in range(8):
                    evac(("uq", l, h), tok_view(mQ[0:96, h, :], own), own, rows=(0, 96), scale=96 ** -0.5)
                for t in range(TT):
                    evac(("uv", l, t), mV[:, t, :], n=512)
                attention(("mla", l), attn_area(MW))
                if l == 0:
                    attention(("mlac", 0), attn_area(MW), before=("mla", 0))
                act.wait_ge(*E.own())
                act_(tick[:, 0:1], C("eps"), ACT.Copy).then_inc(*E.sig("act_stage_done"))
                act.wait_ge(*E.next("dve_stage_done"))
                act.wait_ge(*E.next("pool_stage_done"))
                base = 8 * l + 4
                for t in range(4):
                    if t >= 2:
                        act.wait_ge(*E.upto("silu_used", base + t - 1))
                    evac(("mgate", l, t), tok_view(mSil[:, t % 2, :], own), own, func=ACT.Silu, ahead=True)
                act.wait_ge(*E.next("pads_zero"))
                base = E.seen.get("pooled", 0)
                for g in range(4):
                    if g >= 2:
                        act.wait_ge(*E.upto("pooled", base + g - 1))
                    high()
                    act.wait_ge(*E.written("px", l, g))
                    ps = cols("px", l, g)
                    x0 = (g % 2) * (TOK + 32)
                    if l == 0:
                        act_(pX[:, x0 + 8:x0 + 8 + CTX], ps[:, 0:CTX], ACT.Copy)
                        act_(pX[:, x0 + 280:x0 + 408], ps[:, CTX:384], ACT.Copy)
                        act_(pX[:, x0 + 408:x0 + 792], ps[:, 512:896], ACT.Copy).then_inc(*E.read("px", l, g))
                    else:
                        act_(pX[:, x0 + 280:x0 + 792], ps[:, 0:SEQ], ACT.Copy).then_inc(*E.read("px", l, g))
                    evac(("pgate", l, g), tok_view(YP[:, g, :], own), own, func=ACT.Silu, ahead=True)
                act.wait_ge(*E.upto("pooled", base + 4))
                gates(("l", l), own)
                for f in range(KT):
                    evac(("out", ("l", l), f), tok_view(mOUT[:, f, :], own), own, ahead=f < KT - 2)
                act.wait_ge(*E.taken("out", ("l", l), KT - 1))
                squares(mOUT, KT, nSq, view)
                root(view(nRs))

        @block.vector
        def _(dve):
            E = Eng(dve, "dve")
            V = nc.vector
            stt, tt_, ts_ = V.scalar_tensor_tensor, V.tensor_tensor, V.tensor_scalar

            def inverse_std(name, rs, width, chunks, n, mark="var_ready"):
                dve.wait_ge(*E.written("stat", name))
                ps = cols("stat", name)
                dve.wait_ge(*E.own())
                ins = ts_(tok_view(rs, chunks), bank_view(ps, chunks), 1.0 / n, EPS, ALU.mult, ALU.add)
                ins.then_inc(*E.read("stat", name))
                dve.wait_ge(*E.taken("stat", name))
                V.tensor_copy(tick[:, 3:4], rs[:, CTX:CTX + 1]).then_inc(*E.sig(mark))
                dve.wait_ge(*E.next("std_ready"))
                r = rs if chunks is ALL else rs[:, CTX:TOK]
                V.reciprocal(r, r).then_inc(*E.sig("dve_step"))
                dve.wait_ge(*E.own())

            def scale_in(gain, chunks):
                for k in range(KT):
                    stt(H3[:, k, CTX:TOK], R3[:, k, CTX:TOK], gain(k, 0), nRs[:, CTX:TOK],
                        ALU.mult, ALU.mult).then_inc(*E.sig("scaled_ready"))

            def scale_and_part(gain):
                def low(k):
                    dve.wait_ge(*E.next("hidden_high"))
                    tt_(Hlo[:, k, :], H3[:, k, :], Hhi[:, k, :], ALU.subtract).then_inc(*E.sig("hidden_ready"))

                for k in range(KT):
                    stt(H3[:, k, 0:CTX], R3[:, k, 0:CTX], gain(k, 1), nRs[:, 0:CTX], ALU.mult, ALU.mult)
                    stt(H3[:, k, CTX:TOK], R3[:, k, CTX:TOK], gain(k, 0), nRs[:, CTX:TOK],
                        ALU.mult, ALU.mult).then_inc(*E.sig("scaled_ready"))
                    if k >= 2:
                        low(k - 2)
                low(KT - 2)
                low(KT - 1)

            def rope(name, x, cos, sin, tmp, mark=True):
                dve.wait_ge(*E.written("rot", *name))
                ps = cols("rot", *name)
                dve.wait_ge(*E.own())
                p0, p1 = (64, 96) if name[0] == "kr" else (0, x.shape[0])
                tt_(tmp, ps[p0:p1, 0:SEQ], sin, ALU.mult).then_inc(*E.read("rot", *name))
                tt_(x, x, cos, ALU.mult).then_inc(*E.sig("dve_step"))
                dve.wait_ge(*E.own())
                dve.wait_ge(*E.taken("rot", *name))
                ins = tt_(x, x, tmp, ALU.add)
                if mark:
                    ins.then_inc(*E.sig("rotated"))
                else:
                    ins.then_inc(*E.sig("dve_step"))
                    dve.wait_ge(*E.own())

            def attention(name, pw, y, col0, sink=False):
                pP, pT, pO_ = pw
                us = units(ATT[name])
                nq, base = len(ATT[name]), unit_base[name]

                def maxes(i):
                    t, hh, qi = us[i]
                    L, _ = spans(name, qi)
                    col = (t % 2) * 8 + qi * 2 + hh
                    dve.wait_ge(*E.written("S", name, i))
                    ps = cols("S", name, i)
                    nm = negmax[:, col:col + 1]
                    ins = V.reduce_max(nm, ps[:, 512 - L:768], AXX, negate=True)
                    if sink:
                        ins.then_inc(*E.sig("dve_step"))
                        dve.wait_ge(*E.own())
                        h = t + 4 * hh
                        ins = V.tensor_scalar_min(nm, nm, nsink[:, h:h + 1])
                    ins.then_inc(*E.sig("negmax_ready"))

                def scale_outputs(t):
                    c0, n = (t % 2) * 8, 2 * nq
                    dve.wait_ge(*E.taken("S", name, 2 * nq * (t + 1) - 1))
                    r = rinv[:, c0:c0 + n]
                    if sink:
                        tt_(r, sums[:, c0:c0 + n], esink[:, c0:c0 + n], ALU.add).then_inc(*E.sig("dve_step"))
                        dve.wait_ge(*E.own())
                        V.reciprocal(r, r).then_inc(*E.sig("dve_step"))
                        dve.wait_ge(*E.own())
                    else:
                        V.reciprocal(r, sums[:, c0:c0 + n]).then_inc(*E.sig("dve_step"))
                        dve.wait_ge(*E.own())
                    dve.wait_ge(*E.upto("outputs_done", base + 2 * nq * (t + 1)))
                    dve.wait_ge(*E.own())
                    if t >= 2:
                        dve.wait_ge(*E.written("O", name, t - 2))
                    o = psum[:, (6 + t % 2) * 512:(6 + t % 2) * 512 + nq * P]
                    tt_(split(pO_[:, t % 2, 0:nq * P], a=n), split(o, a=n),
                        r.unsqueeze(2).to_broadcast([P, n, 64]), ALU.mult).then_inc(*E.sig("outputs_scaled"))

                def collect(t):
                    dve.wait_ge(*E.written("O", name, t))
                    ps = cols("O", name, t)
                    V.tensor_copy(y[:, t, col0:col0 + nq * P], ps[:, 0:nq * P]).then_inc(*E.read("O", name, t))

                maxes(0)
                for i in range(len(us)):
                    if i + 1 < len(us):
                        maxes(i + 1)
                    if i % 2 == 0:
                        dve.wait_ge(*E.written("T", name, i))
                        ps = cols("T", name, i)
                        n = len(spans(name, us[i][2])[1]) * P
                        if base + i > 1:
                            dve.wait_ge(*E.upto("outputs_done", base + i - 1))
                        V.tensor_copy(pT[:, i % 2, 0:n], ps[:, 0:n]).then_inc(*E.read("T", name, i))
                    if i >= 2 * nq + 1 and (i - 1) % (2 * nq) == 0:
                        scale_outputs((i - 1) // (2 * nq) - 1)
                    if i >= 2 * nq + 2 and (i - 2) % (2 * nq) == 0:
                        collect((i - 2) // (2 * nq) - 1)
                scale_outputs(3)
                collect(3)

            def merge(key, chunks):
                for f in range(0, KT, 2):
                    for b in range(3):
                        for g in (f, f + 1):
                            dve.wait_ge(*E.taken("gate", key, b, g))
                            dve.wait_ge(*E.written("branch", key, b, g))
                            ps = cols("branch", key, b, g)
                            o = tok_view(mMG[:, g, :], chunks)
                            to = o if b == 0 else tok_view(mTmp[:, g % 2, :], chunks)
                            dve.wait_ge(*E.own())
                            tt_(to, tok_view(mSG[:, 2 * b + g % 2, :], chunks),
                                       bank_view(ps, chunks), ALU.mult).then_inc(*E.read("branch", key, b, g))
                            dve.wait_ge(*E.taken("branch", key, b, g))
                            if b:
                                ins = tt_(o, o, to, ALU.add)
                                if b == 1:
                                    ins.then_inc(*E.sig("dve_step"))
                                    dve.wait_ge(*E.own())
                                else:
                                    ins.then_inc(*E.sig("merged_ready"))
                v = slice(0, TOK) if chunks is ALL else slice(CTX, TOK)
                for k in range(KT):
                    dve.wait_ge(*E.next("merged_high"))
                    tt_(mLo[:, k, v], mMG[:, k, v], mHi[:, k, v], ALU.subtract).then_inc(*E.sig("merged_parts"))

            def modulation(name, mod, bias, gm, gain):
                for b in range(mod.shape[1] // 8):
                    dve.wait_ge(*E.written(name, "row", b))
                    ps = cols(name, "row", b)
                    V.tensor_copy(modRow[name][0:2, b * 512:(b + 1) * 512], ps[0:2, 0:512])
                    V.tensor_copy(modRow[name][64:66, b * 512:(b + 1) * 512], ps[64:66, 512:1024])\
                        .then_inc(*E.read(name, "row", b))
                dve.wait_ge(*E.written(name))
                ps = cols(name)
                n = mod.shape[1]
                by_half = lambda a: a.rearrange("p (b h n) -> p b h n", h=2, n=8)
                src = split(ps, h=2)[:, :, 0:n].rearrange("p h (b n) -> p b h n", n=8)
                tt_(by_half(mod.rearrange("p a b -> p (a b)")), src, by_half(Pm(bias)), ALU.add)\
                    .then_inc(*E.read(name))
                dve.wait_ge(*E.taken(name))
                stt(gm, mod[:, 8:16, :], 1.0, split(Pm(gain), a=KT), ALU.add, ALU.mult).then_inc(*E.sig("dve_step"))
                dve.wait_ge(*E.own())

            dve.wait_ge(*E.next("params_loaded", 16))
            dve.wait_ge(*E.next("consts_loaded", 16))
            ts_(nsink, Pm("sink"), -1.0, None, ALU.mult)
            dve.wait_ge(*E.next("decay_ln"))
            ts_(lt2, Pm("decay"), 0.0, None, ALU.min).then_inc(*E.sig("dve_step"))
            dve.wait_ge(*E.own())
            tt_(lg, lt2, lt1, ALU.subtract).then_inc(*E.sig("dve_step"))
            dve.wait_ge(*E.own())
            ts_(lg[:, 4:8], lg[:, 4:8], -1.0, None, ALU.mult).then_inc(*E.sig("dve_step"))
            dve.wait_ge(*E.own())
            modulation("mod1", modA, "bmod", gmA, "gmix")
            stt(gmF.rearrange("p (a b) -> p a b", b=1), modA[:, 32:40, 0:1], 1.0,
                       Pm("gffn").rearrange("p (a b) -> p a b", b=1), ALU.add, ALU.mult).then_inc(*E.sig("dve_step"))
            dve.wait_ge(*E.own())
            inverse_std("mix", nRs, TOK, ALL, D)
            dve.wait_ge(*E.next("residual_loaded", 16))
            scale_and_part(lambda k, c: gmA[:, k, c:c + 1])
            dve.wait_ge(*E.next("ret_tables_loaded", 16))
            for t in range(4):
                rope(("q_r", t), rQ[:, t, :], rCos, rSin, rTmp[:, 0:512])
            for t in range(4):
                rope(("k_r", t), rK[:, t, CTX:TOK], rCos, rSin, rTmp[:, 0:512])

            def exponents(h):
                e = rE if h % 2 == 0 else YC[:, 0:DW]
                x2 = YB[:, 0:DW]
                dve.wait_ge(*E.own())
                ts_(x2, rDist, 0.0, lg[:, 4 + h:5 + h], ALU.min, ALU.mult)
                ts_(e, rDist, 0.0, lg[:, h:h + 1], ALU.max, ALU.mult).then_inc(*E.sig("dve_step"))
                dve.wait_ge(*E.own())
                tt_(e, e, x2, ALU.add).then_inc(*E.sig("exponent_ready"))

            exponents(0)
            for h in range(4):
                if h < 3:
                    exponents(h + 1)
                dve.wait_ge(*E.next("decay_ready"))
                e = rE if h % 2 == 0 else YC[:, 0:DW]
                dve.wait_ge(*E.own())
                for m in range(2):
                    a, b = 896 - P * m, P - P * m
                    ins = tt_(rCW[:, m, :], e[:, a:a + 512], e[:, b:b + 512], ALU.add)
                ins.then_inc(*E.sig("dve_step"))
                dve.wait_ge(*E.own())
                for pr in range(3):
                    dve.wait_ge(*E.written("rS", h, pr))
                    ps = cols("rS", h, pr)
                    n = 3 * h + pr
                    if n >= 4:
                        dve.wait_ge(*E.written("rY", (n - 4) // 3))
                    for i in range(2):
                        kt = 2 * pr + i
                        w = rCW[:, kt, :] if kt < 2 else e[:, 640 - P * (kt - 2):640 - P * (kt - 2) + 512]
                        ins = stt(rP[:, n % 4, i * 512:(i + 1) * 512], ps[:, i * 512:(i + 1) * 512],
                                  128 ** -0.5, w, ALU.mult, ALU.mult)
                    ins.then_inc(*E.read("rS", h, pr))
            for h in range(4):
                dve.wait_ge(*E.written("rmean", h))
                ps = cols("rmean", h)
                stt(A3[:, h, :], ps[:, 0:512], -1.0 / P, A3[:, h, :], ALU.mult, ALU.add).then_inc(*E.read("rmean", h))
            dve.wait_ge(*E.own())
            for h in range(4):
                dve.wait_ge(*E.written("rvar", h))
                ps = cols("rvar", h)
                ts_(rRs[:, h, :], ps[:, 0:512], 1.0 / P, EPS, ALU.mult, ALU.add).then_inc(*E.read("rvar", h))
            for h in range(4):
                dve.wait_ge(*E.next("std_ready"))
                V.reciprocal(rRs[:, h, :], rRs[:, h, :]).then_inc(*E.sig("dve_step"))
                dve.wait_ge(*E.own())
                stt(A3[:, h, :], A3[:, h, :], Pm("retgn")[:, h:h + 1], rRs[:, h, :], ALU.mult, ALU.mult).then_inc(*E.sig("dve_step"))
                dve.wait_ge(*E.own())
                dve.wait_ge(*E.taken("g_r", h))
                tt_(A3[:, h, :], A3[:, h, :], rSG[:, h, :], ALU.mult).then_inc(*E.sig("retention_ready"))
            dve.wait_ge(*E.own())
            V.memset(tick[:, 1:2], 0.0).then_inc(*E.sig("dve_stage_done"))
            dve.wait_ge(*E.next("act_stage_done"))
            dve.wait_ge(*E.next("pool_stage_done"))
            dve.wait_ge(*E.next("win_tables_loaded", 16))
            for t in range(4):
                rope(("q_w", t), wQ[:, t, :], wCos, wSin, wTmp[:, 0:512])
            rope(("k_w", 0), wK[:, CTX:TOK], wCos, wSin, wTmp[:, 0:512])
            attention("win", attn_area(AT1), split(YB, a=4), 0, sink=True)
            dve.wait_ge(*E.own())
            V.memset(tick[:, 1:2], 0.0).then_inc(*E.sig("dve_stage_done"))
            dve.wait_ge(*E.next("act_stage_done"))
            dve.wait_ge(*E.next("pool_stage_done"))
            attention("na", attn_area(AT2), split(YC, a=4), 0)
            dve.wait_ge(*E.own())
            V.memset(tick[:, 1:2], 0.0).then_inc(*E.sig("dve_stage_done"))
            dve.wait_ge(*E.next("act_stage_done"))
            dve.wait_ge(*E.next("pool_stage_done"))
            merge(0, IMG)
            dve.wait_ge(*E.next("residual_reloaded", 16))
            for f in range(KT):
                dve.wait_ge(*E.written("out", 0, f))
                ps = cols("out", 0, f)
                stt(R3[:, f, CTX:TOK], ps[:, 0:SEQ], modA[:, 16 + f, 0:1], R3[:, f, CTX:TOK],
                           ALU.mult, ALU.add).then_inc(*E.read("out", 0, f))
                dve.wait_ge(*E.taken("out", 0, f))
                V.tensor_copy(tick[:, 4:5], R3[:, f, TOK - 1:TOK]).then_inc(*E.sig("residual_ready"))
            inverse_std("ffn", nRs, SEQ, IMG, D)
            scale_in(lambda k, c: gmF[:, k:k + 1], IMG)
            dve.wait_ge(*E.own())
            V.memset(tick[:, 1:2], 0.0).then_inc(*E.sig("dve_stage_done"))
            dve.wait_ge(*E.next("act_stage_done"))
            dve.wait_ge(*E.next("pool_stage_done"))
            for tt in (1, 3):
                dve.wait_ge(*E.written("HT", tt))
                ps = cols("HT", tt)
                V.tensor_copy(eHT[:, tt, :], ps[:, 0:1024]).then_inc(*E.read("HT", tt))
            dve.wait_ge(*E.written("router"))
            ps = cols("router")
            V.reduce_max(m16, split(ps[:, 0:4 * NE], a=4), AXX, negate=True).then_inc(*E.sig("router_max"))
            dve.wait_ge(*E.taken("router"))
            V.reciprocal(r16, s16).then_inc(*E.sig("dve_step"))
            dve.wait_ge(*E.own())
            tt_(aff, aff, r16.unsqueeze(2).to_broadcast([P, 4, NE]), ALU.mult)\
                .then_inc(*E.sig("router_softmax"))
            dve.wait_ge(*E.written("affT"))
            ps = cols("affT")
            V.tensor_copy(eW[0:NE, 0, :], ps[0:NE, 0:512]).then_inc(*E.read("affT"))
            dve.wait_ge(*E.taken("affT"))
            for n in range(CAP // 8):
                a, b = eW[0:NE, n % 2, :], eW[0:NE, (n + 1) % 2, :]
                V.max(top8[0:NE, :], a).then_inc(*E.sig("dve_step"))
                dve.wait_ge(*E.own())
                V.match_replace(b, top8[0:NE, :], a, -1.0).then_inc(*E.sig("dve_step"))
                dve.wait_ge(*E.own())
            ts_(eM[0:NE, :], eW[0:NE, (CAP // 8) % 2, :], 0.0, None, ALU.is_lt).then_inc(*E.sig("dve_step"))
            dve.wait_ge(*E.own())
            V.memset(eA[0:NE, :], 1.0).then_inc(*E.sig("dve_step"))
            dve.wait_ge(*E.own())
            V.tensor_tensor_scan(eC[0:NE, :], eA[0:NE, :], eM[0:NE, :], 0.0, ALU.mult, ALU.add).then_inc(*E.sig("dve_step"))
            dve.wait_ge(*E.own())
            tt_(eC[0:NE, :], eC[0:NE, :], eM[0:NE, :], ALU.mult).then_inc(*E.sig("dve_step"))
            dve.wait_ge(*E.own())
            V.tensor_scalar_add(eC[0:NE, :], eC[0:NE, :], -1.0).then_inc(*E.sig("slots_ready"))
            dve.wait_ge(*E.written("pos"))
            ps = cols("pos")
            V.tensor_copy(posn, split(ps[:, 0:4 * NE], a=4)).then_inc(*E.read("pos"))
            dve.wait_ge(*E.taken("pos"))
            slots = C("slots").unsqueeze(1).to_broadcast([P, NE, CAP])
            for tt in range(4):
                p3 = split(eP[:, tt, :], a=NE)
                tt_(p3, slots, posn[:, tt, :].unsqueeze(2).to_broadcast([P, NE, CAP]), ALU.is_equal).then_inc(*E.sig("dve_step"))
                dve.wait_ge(*E.own())
                tt_(split(ePg[:, tt, :], a=NE), p3, aff[:, tt, :].unsqueeze(2).to_broadcast([P, NE, CAP]),
                    ALU.mult).then_inc(*E.sig("assigned"))
            for q in (1, 3):
                dve.wait_ge(*E.written("PG", q))
                ps = cols("PG", q)
                V.tensor_copy(ePG[:, 2 * q:2 * q + 2, :].rearrange("p a n -> p (a n)"),
                                     ps[:, 0:1024]).then_inc(*E.read("PG", q))

            def tokens(*name):
                dve.wait_ge(*E.written(*name))
                ps = cols(*name)
                V.tensor_copy(eXE.rearrange("p a n -> p (a n)"), ps).then_inc(*E.read(*name))

            tokens("XE", "first")
            for i in range(2):
                V.memset(eYE[:, i * 512:(i + 1) * 512], 0.0).then_inc(*E.sig("combined"))
            for n in [k for k in group_no if k[0] == "pad"]:
                dve.wait_ge(*E.written(*n))
                ps = cols(*n)
                dve.wait_ge(*E.own())
                V.tensor_copy(tick[:, 6:7], ps[:, 0:1]).then_inc(*E.read(*n))

            def pair(tag, following):
                for f in range(KT):
                    dve.wait_ge(*E.next("combine_product"))
                    stt(R3[:, f, CTX:TOK], psum[:, (6 + f % 2) * 512:(7 + f % 2) * 512], modA[:, 40 + f, 0:1],
                        R3[:, f, CTX:TOK], ALU.mult, ALU.add).then_inc(*E.sig("combined"))
                dve.wait_ge(*E.taken(tag, "exp_gate"))
                dve.wait_ge(*E.written(tag, "exp_up"))
                ps = cols(tag, "exp_up")
                tt_(eHID[:, 0:512], eSG[:, 0:512], ps[:, 0:512], ALU.mult).then_inc(*E.sig("expert_hidden"))
                tt_(eHID[:, 512:1024], eSG[:, 512:1024], ps[:, 512:1024], ALU.mult)\
                    .then_inc(*E.read(tag, "exp_up"))
                if following:
                    tokens(tag, "XE")
                dve.wait_ge(*E.written(tag, "HF", 1))
                ps = cols(tag, "HF", 1)
                V.tensor_copy(eHF[:, 4:8, :].rearrange("p a n -> p (a n)"), ps[:, 0:512])\
                    .then_inc(*E.read(tag, "HF", 1))

            with dve.Fori(0, PAIRS - 1) as it:
                E.begin(it, {"groups": 6, "slot": 2, "combine_product": 8})
                pair("loop", True)
                E.end(PAIRS - 1)
            pair("last", False)
            dve.wait_ge(*E.upto("combined", E.made["combined"]))
            for q in range(4):
                dve.wait_ge(*E.written("comb", q))
                ps = cols("comb", q)
                for i in range(2):
                    f = 2 * q + i
                    ins = stt(R3[:, f, CTX:TOK], ps[:, i * 512:(i + 1) * 512], modA[:, 40 + f, 0:1],
                              R3[:, f, CTX:TOK], ALU.mult, ALU.add)
                    if i == 0:
                        ins.then_inc(*E.sig("residual_ready"))
                    else:
                        ins.then_inc(*E.read("comb", q))
                        dve.wait_ge(*E.taken("comb", q))
                        V.tensor_copy(tick[:, 4:5], R3[:, f, TOK - 1:TOK]).then_inc(*E.sig("residual_ready"))
            inverse_std("final", nRs, SEQ, IMG, D)
            for k in range(KT):
                stt(R3[:, k, CTX:TOK], R3[:, k, CTX:TOK], Pm("gfinal")[:, k:k + 1], nRs[:, CTX:TOK],
                    ALU.mult, ALU.mult).then_inc(*E.sig("residual_ready"))
            for l in LAYERS:
                own = ALL if l == 0 else IMG
                view = (lambda a: a) if l == 0 else (lambda a: a[:, CTX:TOK])
                L = str(l)
                modulation(("mod2", l), modB, "bmod2" + L, gmB, "pre" + L)
                tt_(pgB, modB[:, 16:24, :], split(Pm("post" + L), a=KT), ALU.mult).then_inc(*E.sig("dve_step"))
                dve.wait_ge(*E.own())
                inverse_std(("pre", l), nRs, TOK, ALL, D)
                if l == 0:
                    dve.wait_ge(*E.next("ctx2_loaded", 16))
                    dve.wait_ge(*E.next("residual_ready", 3 * KT))
                else:
                    dve.wait_ge(*E.next("residual_updated", KT))
                scale_and_part(lambda k, c: gmB[:, k, c:c + 1])
                for d in range(2):
                    for t in range(2):
                        dve.wait_ge(*E.next("decay_abs"))
                        dve.wait_ge(*E.written("decay", l, d, t))
                        ps = cols("decay", l, d, t)
                        bias = Pm(("afb", "abb")[d] + L)[:, t:t + 1]
                        ts_(tok_view(gLM[:, 2 * d + t, :], ALL), bank_view(ps, ALL), bias, 0.0,
                                   ALU.add, ALU.min).then_inc(*E.read("decay", l, d, t))
                flat = lambda a: a.rearrange("p a n -> p (a n)")
                dve.wait_ge(*E.next("gla_ln"))
                dve.wait_ge(*E.taken("decay", l, 1, 1))
                tt_(flat(gLM), flat(gLM), flat(gT1), ALU.subtract).then_inc(*E.sig("dve_step"))
                dve.wait_ge(*E.own())
                for a in range(4):
                    for c in range(TT):
                        sl = slice(c * P, (c + 1) * P)
                        ins = V.tensor_tensor_scan(gB[:, a, sl], C("ones"), gLM[:, a, sl], 0.0,
                                                   ALU.mult, ALU.add)
                ins.then_inc(*E.sig("scans_ready"))
                dve.wait_ge(*E.next("scans_ready"))
                dve.wait_ge(*E.next("chunk_decay_ready"))
                chunks = lambda a: a.rearrange("p a (c n) -> p (a c) n", n=P)
                gBc, gTc = chunks(gB), chunks(gT1)
                end = lambda lo, hi, j: gBc[:, lo:hi, j:j + 1].to_broadcast([P, hi - lo, P])
                tt_(gTc[:, 12:24, :], end(12, 24, P - 1), gBc[:, 12:24, :], ALU.subtract).then_inc(*E.sig("dve_step"))
                dve.wait_ge(*E.own())
                tt_(flat(gB[:, 2:4, :]), flat(gT1[:, 2:4, :]), flat(gLM[:, 2:4, :]), ALU.add).then_inc(*E.sig("dve_step"))
                dve.wait_ge(*E.own())
                tt_(gTc[:, 0:12, :], end(0, 12, P - 1), gBc[:, 0:12, :], ALU.subtract)
                tt_(gTc[:, 12:24, :], end(12, 24, 0), gBc[:, 12:24, :], ALU.subtract)\
                    .then_inc(*E.sig("key_exponents"))
                dve.wait_ge(*E.next("key_decays"))
                dve.wait_ge(*E.taken("gk", l, 1))
                for d in range(2):
                    a = flat(gT1[:, 2 * d:2 * d + 2, :])
                    tt_(a, a, flat(gK), ALU.mult).then_inc(*E.sig("decayed_keys"))
                for d, order in enumerate(SCAN):
                    for n, c in enumerate(order[:-1]):
                        dve.wait_ge(*E.written("U", l, d, c))
                        ps = cols("U", l, d, c)
                        to = order[n + 1]
                        if n == 0:
                            ins = V.tensor_copy(gS[:, d, to, :, :], split(ps[:, 0:256], a=2))
                        else:
                            for t in range(2):
                                ins = stt(gS[:, d, to, t, :], gS[:, d, c, t, :],
                                          expT[:, (2 * d + t) * TT + c:(2 * d + t) * TT + c + 1],
                                          ps[:, t * P:(t + 1) * P], ALU.mult, ALU.add)
                        ins.then_inc(*E.read("U", l, d, c))
                        dve.wait_ge(*E.taken("U", l, d, c))

                def chunk_exponents(c):
                    QI, QS, KS, _ = gChunk(c % 2)
                    b = gB[:, :, c * P:(c + 1) * P]
                    b4 = b.rearrange("p a (s n) -> p a s n", s=4)
                    mid = b4[:, :, :, 15:16]
                    dve.wait_ge(*E.own())
                    tt_(QS.rearrange("p a (s n) -> p a s n", s=4), b4, mid.to_broadcast([P, 4, 4, 32]),
                        ALU.subtract)
                    for d in range(2):
                        E_in = mid[:, 2 * d:2 * d + 2, :, :].to_broadcast([P, 2, 4, P])
                        E_b = b[:, 2 * d:2 * d + 2, :].unsqueeze(2).to_broadcast([P, 2, 4, P])
                        ins = tt_(KS[:, d, :, :, :], E_in, E_b, ALU.subtract)
                    ins.then_inc(*E.sig("dve_step"))
                    dve.wait_ge(*E.own())
                    q, k = QS.rearrange("p a n -> p (a n)"), KS.rearrange("p d t s n -> p (d t s n)")
                    V.tensor_scalar_min(q, q, CLAMP)
                    V.tensor_scalar_min(k, k, CLAMP).then_inc(*E.sig("chunk_exponents"))

                def chunk_products(c):
                    QI, QS, KS, QZ = gChunk(c % 2)
                    dve.wait_ge(*E.next("chunk_decays"))
                    dve.wait_ge(*E.own())
                    for d in range(2):
                        x = QI[:, 2 * d:2 * d + 2, :]
                        tt_(x, x, gQ[:, :, c * P:(c + 1) * P], ALU.mult)
                        for b in range(2):
                            rows = slice(64 * b, 64 * b + 64)
                            tt_(QZ[rows, 2 * d:2 * d + 2, :, b, :],
                                QS[rows, 2 * d:2 * d + 2, :].rearrange("p a (s n) -> p a s n", s=4),
                                gQ[rows, :, c * P:(c + 1) * P].rearrange("p a (s n) -> p a s n", s=4), ALU.mult)
                        x = KS[:, d, :, :, :]
                        k = gK[:, :, c * P:(c + 1) * P].unsqueeze(2).to_broadcast([P, 2, 4, P])
                        ins = tt_(x, x, k, ALU.mult)
                    ins.then_inc(*E.sig("chunk_operands"))

                for i in range(2):
                    V.memset(gChunk(i)[3].rearrange("p a s b n -> p (a s b n)"), 0.0).then_inc(*E.sig("dve_step"))
                dve.wait_ge(*E.taken("gq", l, 1))
                chunk_exponents(OWN_CHUNKS[l][0])
                for c in OWN_CHUNKS[l]:
                    chunk_products(c)
                    if c + 1 < TT:
                        chunk_exponents(c + 1)
                    back = gChunk(c % 2)[1].rearrange("p a n -> p (a n)")
                    dve.wait_ge(*E.own())
                    dve.wait_ge(*E.written("A", l, c))
                    ps = cols("A", l, c)
                    for AT, d, m in ((gAT, 0, "upper"), (back, 1, "lower")):
                        for t in range(2):
                            o = AT[:, t * 256:(t + 1) * 256].rearrange("p (b s n) -> p s b n", b=2, s=4)
                            at = (2 * d + t) * 256
                            ins = tt_(o, ps[:, at:at + 256].rearrange("p (s b n) -> p s b n", s=4, b=2),
                                      C(m).rearrange("p (s n) -> p s n", s=4).unsqueeze(2)
                                      .to_broadcast([P, 4, 2, 32]), ALU.mult)
                    ins.then_inc(*E.read("A", l, c))
                    dve.wait_ge(*E.taken("A", l, c))
                    tt_(gAT, gAT, back, ALU.add).then_inc(*E.sig("chunk_weights"))
                for h in range(4):
                    dve.wait_ge(*E.written("stat", ("gla", l, h)))
                    ps = cols("stat", ("gla", l, h))
                    ts_(tok_view(gRs[:, h, :], own), bank_view(ps, own), 1.0 / P, EPS,
                               ALU.mult, ALU.add).then_inc(*E.read("stat", ("gla", l, h)))
                for h in range(4):
                    dve.wait_ge(*E.next("std_ready"))
                    r, y = view(gRs[:, h, :]), view(YG[:, h, :])
                    V.reciprocal(r, r).then_inc(*E.sig("dve_step"))
                    dve.wait_ge(*E.own())
                    stt(y, y, Pm("glan" + L), r, ALU.mult, ALU.mult).then_inc(*E.sig("dve_step"))
                    dve.wait_ge(*E.own())
                for t in range(4):
                    dve.wait_ge(*E.taken("ggate", l, t))
                    y = view(YG[:, t, :])
                    tt_(y, y, view(SILU[:, t % 2, :]), ALU.mult).then_inc(*E.sig("silu_used"))
                dve.wait_ge(*E.own())
                V.memset(tick[:, 1:2], 0.0).then_inc(*E.sig("dve_stage_done"))
                dve.wait_ge(*E.next("act_stage_done"))
                dve.wait_ge(*E.next("pool_stage_done"))
                inverse_std(("qn", l), mRs, 0, own, 256)
                for t in range(2):
                    dve.wait_ge(*E.taken("mq", l, t))
                    x = view(mRaw[:, t, :])
                    stt(x, x, Pm("qnorm" + L)[:, t:t + 1], view(mRs), ALU.mult, ALU.mult)\
                        .then_inc(*E.sig("rank_norms"))
                inverse_std(("kvn", l), mRs, 0, ALL, 128)
                dve.wait_ge(*E.taken("mkv", l))
                stt(mKV, mKV, Pm("kvnorm" + L), mRs, ALU.mult, ALU.mult).then_inc(*E.sig("rank_norms"))
                for h in range(8):
                    dve.wait_ge(*E.written("uk", l, h))
                    ps = cols("uk", l, h)
                    V.tensor_copy(tok_view(mK[0:64, h, :], ALL), bank_view(ps[0:64, :], ALL)).then_inc(*E.read("uk", l, h))
                dve.wait_ge(*E.next("mla_tables_loaded", 16))
                for h in range(8):
                    rope(("uq", l, h), mQ[0:96, h, CTX:TOK], mCos[0:96, :], mSin[0:96, :], mTp[0:96, 0:512])
                dve.wait_ge(*E.next("rope_key_ready"))
                rope(("kr", l), mKR[64:96, CTX:TOK], mCos[64:96, :], mSin[64:96, :], mTp[64:96, 0:512],
                     mark=False)
                for h in range(8):
                    V.tensor_copy(mK[64:96, h, :], mKR[64:96, :]).then_inc(*E.sig("keys_complete"))
                attention(("mla", l), attn_area(MW), YM, CTX)
                if l == 0:
                    attention(("mlac", 0), attn_area(MW), YM, 0)
                dve.wait_ge(*E.own())
                V.memset(tick[:, 1:2], 0.0).then_inc(*E.sig("dve_stage_done"))
                dve.wait_ge(*E.next("act_stage_done"))
                dve.wait_ge(*E.next("pool_stage_done"))
                for t in range(4):
                    dve.wait_ge(*E.taken("mgate", l, t))
                    y = view(YM[:, t, :])
                    tt_(y, y, view(mSil[:, t % 2, :]), ALU.mult).then_inc(*E.sig("silu_used"))
                for g in range(4):
                    dve.wait_ge(*E.taken("pgate", l, g))
                    dve.wait_ge(*E.written("mixed", l, g))
                    ps = cols("mixed", l, g)
                    y = tok_view(YP[:, g, :], own)
                    stt(y, bank_view(ps, own), Pm("pscale" + L)[:, g:g + 1], y, ALU.mult, ALU.mult).then_inc(*E.read("mixed", l, g))
                dve.wait_ge(*E.taken("mixed", l, 3))
                V.tensor_copy(tick[:, 5:6], YP[:, 3, TOK - 1:TOK]).then_inc(*E.sig("branches_ready", 4))
                merge(("l", l), own)
                inverse_std(("post", l), nRs, 0, own, D)
                for k in range(KT):
                    if l == 0:
                        stt(mOUT[:, k, 0:CTX], mOUT[:, k, 0:CTX], pgB[:, k, 1:2], nRs[:, 0:CTX],
                            ALU.mult, ALU.mult)
                    stt(mOUT[:, k, CTX:TOK], mOUT[:, k, CTX:TOK], pgB[:, k, 0:1], nRs[:, CTX:TOK],
                        ALU.mult, ALU.mult).then_inc(*E.sig("update_ready"))

        @block.gpsimd
        def _(pool):
            E = Eng(pool, "pool")
            G_ = nc.gpsimd
            pool.dma_start(par[:, :], dram["params"]).then_inc(sem("params_loaded"), 16)
            pool.dma_start(con[:, :], dram["consts"]).then_inc(sem("consts_loaded"), 16)
            pool.dma_start(R3, dram["acts"]).then_inc(sem("residual_loaded"), 16)
            pool.dma_start(rTab, dram["t_ret"]).then_inc(sem("ret_tables_loaded"), 16)

            def low(n=1):
                for _ in range(n):
                    i = E.made.get("tile_split", 0)
                    t = split_tiles[i]
                    pool.wait_ge(*E.next("high_written"))
                    at = (t // 2 % NSLOT) * UNIT + (t % 2) * 1024
                    G_.tensor_tensor(parts[:, i % 2, 1, :], ring[:, at:at + 1024], parts[:, i % 2, 0, :],
                                     ALU.subtract).then_inc(*E.sig("tile_split"))

            low(22)
            G_.memset(tick[:, 2:3], 0.0).then_inc(*E.sig("pool_stage_done"))
            pool.wait_ge(*E.next("act_stage_done"))
            pool.wait_ge(*E.next("dve_stage_done"))
            pool.dma_start(area(WIN + 3584, 1024), dram["t_win"]).then_inc(sem("win_tables_loaded"), 16)
            low(2)
            pool.dma_start(nMask, dram["t_colmask"]).then_inc(sem("mask_loaded"), 16)
            for h in range(8):
                for half in range(2):
                    src = bass.AP(dram["rpb"].tensor, (h * 15 + 1 - half) * 127, [[1, 64], [127, 14], [1, 64]])
                    pool.dma_start(nB[64 * half:64 * half + 64, h, :].rearrange("p (a c) -> p a c", a=14), src)\
                        .then_inc(sem("bias_loaded"), 16)
            pool.wait_ge(*E.next("mask_loaded", 16))
            pool.wait_ge(*E.next("bias_loaded", 16 * 16))
            for h in range(8):
                b = nB[:, h, :].rearrange("p (a c) -> p a c", a=14)
                G_.tensor_tensor(b, b, nMask.unsqueeze(1).to_broadcast([P, 14, 64]), ALU.add)\
                    .then_inc(*E.sig("bias_ready"))
            pool.wait_ge(*E.own())
            G_.memset(tick[:, 2:3], 0.0).then_inc(*E.sig("pool_stage_done"))
            pool.wait_ge(*E.next("act_stage_done"))
            pool.wait_ge(*E.next("dve_stage_done"))
            low(12)
            pool.wait_ge(*E.own())
            G_.memset(tick[:, 2:3], 0.0).then_inc(*E.sig("pool_stage_done"))
            pool.wait_ge(*E.next("act_stage_done"))
            pool.wait_ge(*E.next("dve_stage_done"))
            low(24)
            pool.wait_ge(*E.written("gate", 0, 2, KT - 1))
            pool.dma_start(R3[:, :, CTX:TOK], dram["acts"][:, :, CTX:TOK]).then_inc(sem("residual_reloaded"), 16)
            pool.dma_start(R3[:, :, 0:CTX], dram["ctx2"]).then_inc(sem("ctx2_loaded"), 16)
            low(6)
            pool.wait_ge(*E.own())
            G_.memset(tick[:, 2:3], 0.0).then_inc(*E.sig("pool_stage_done"))
            pool.wait_ge(*E.next("act_stage_done"))
            pool.wait_ge(*E.next("dve_stage_done"))
            pool.dma_start(eWR, dram["router"]).then_inc(sem("router_loaded"), 16)
            for l in LAYERS:
                if l == 0:
                    pool.wait_ge(*E.next("ctx2_loaded", 16))
                    pool.wait_ge(*E.next("residual_ready", 3 * KT))
                else:
                    pool.wait_ge(*E.own())
                pool.dma_start(scratch, R3).then_inc(sem("residual_saved"), 16)
                low(17)
                pool.wait_ge(*E.own())
                G_.memset(tick[:, 2:3], 0.0).then_inc(*E.sig("pool_stage_done"))
                pool.wait_ge(*E.next("act_stage_done"))
                pool.wait_ge(*E.next("dve_stage_done"))
                pool.dma_start(area(MW, 1024), dram["t_mla"]).then_inc(sem("mla_tables_loaded"), 16)
                low(1)
                pool.wait_ge(*E.own())
                G_.memset(tick[:, 2:3], 0.0).then_inc(*E.sig("pool_stage_done"))
                pool.wait_ge(*E.next("act_stage_done"))
                pool.wait_ge(*E.next("dve_stage_done"))
                pool.dma_start(pCnt, dram["t_count"]).then_inc(sem("counts_loaded"), 16)
                for b in range(2):
                    for c0, n in ((0, 8), (264, 16), (792, 8)):
                        ins = G_.memset(pX[:, b * (TOK + 32) + c0:b * (TOK + 32) + c0 + n], 0.0)
                if l == 1:
                    for b in range(2):
                        ins = G_.memset(pX[:, b * (TOK + 32) + 8:b * (TOK + 32) + 264], 0.0)
                ins.then_inc(*E.sig("pads_zero"))
                pool.wait_ge(*E.next("pads_zero"))
                pool.wait_ge(*E.next("counts_loaded", 16))
                low(4)
                for g in range(4):
                    low()
                    pool.wait_ge(*E.taken("px", l, g))
                    u = pX[:, (g % 2) * (TOK + 32):(g % 2 + 1) * (TOK + 32)]
                    a, w = u, TOK + 32
                    lo = 0
                    for n in range(g + 1):
                        o = pS[:, (n % 2) * w:(n % 2 + 1) * w]
                        s1 = 1 if n == 0 else 2 ** (n - 1)
                        s2 = 0 if n == 0 else 2 ** (n - 1)
                        new = lo + s1
                        G_.tensor_tensor(o[:, new:w - new], a[:, new - s1:w - new - s1],
                                                a[:, new + s2:w - new + s2], ALU.add).then_inc(*E.sig("pool_step"))
                        pool.wait_ge(*E.own())
                        a, lo = o, new
                    segs = ([(8, 0, CTX)] if l == 0 else []) + [(280, CTX, SEQ)]
                    for x0, c0, n in segs:
                        ins = G_.tensor_tensor(pO[:, g, c0:c0 + n], a[:, x0:x0 + n], pCnt[:, g, c0:c0 + n],
                                               ALU.mult)
                    ins.then_inc(*E.sig("pool_step"))
                    pool.wait_ge(*E.own())
                    for x0, c0, n in segs:
                        ins = G_.tensor_tensor(pO[:, g, c0:c0 + n], pO[:, g, c0:c0 + n], u[:, x0:x0 + n],
                                               ALU.subtract)
                    ins.then_inc(*E.sig("pooled"))
                    low()
                low(24)
                pool.wait_ge(*E.written("gate", ("l", l), 2, KT - 1))
                pool.wait_ge(*E.next("residual_saved", 16))
                pool.dma_start(R3, scratch).then_inc(sem("residual_reloaded"), 16)
                low(6)
                pool.wait_ge(sem("residual_reloaded"), 16 * (l + 2))
                for k in range(KT):
                    pool.wait_ge(*E.next("update_ready"))
                    v = slice(0, TOK) if l == 0 else slice(CTX, TOK)
                    G_.tensor_tensor(R3[:, k, v], R3[:, k, v], mOUT[:, k, v], ALU.add)\
                        .then_inc(*E.sig("residual_updated"))

        @block.sync
        def _(sp):
            for s in range(NSLOT):
                sp.dma_start(ring[:, s * UNIT:(s + 1) * UNIT], dram["weights"][s, :, :])\
                    .then_inc(loaded[s], 16)
            with sp.Fori(1, rounds) as it:
                for s in range(NSLOT):
                    sp.wait_ge(sem("weights_used"), it * NSLOT + (s + 1 - NSLOT))
                    sp.dma_start(ring[:, s * UNIT:(s + 1) * UNIT], dram["weights"][it * NSLOT + s, :, :])\
                        .then_inc(loaded[s], 16)
            for k in range(KT):
                sp.wait_ge(sem("residual_updated"), KT + k + 1)
                sp.dma_start(out[:, k, :], R3[:, k, CTX:TOK]).then_inc(sem("output_written"), 16)
            sp.wait_ge(sem("output_written"), 16 * KT)
            for s in range(NSLOT):
                sp.wait_ge(loaded[s], 16 * rounds)


def tiled(a):
    return a.reshape(-1, P, a.shape[1]).transpose(1, 0, 2).reshape(P, -1)


def pack_weights(x):
    plan = stream_plan()
    out = np.zeros((padded_tiles(len(plan)), P, 1024), np.float32)
    for i, (name, w, lead, rows, cols) in enumerate(plan):
        if name[0] == "decay_w2":
            out[i, 0:16, 0:256] = x["gla_af_w2_2"][lead]
            out[i, 32:48, 0:256] = x["gla_ab_w2_2"][lead]
        elif name[0] == "pool_w":
            out[i, :, 0:512] = x["pool_w_2"][lead].transpose(1, 0, 2).reshape(P, 512)
        else:
            a = x[w][lead]
            if rows is not None:
                a = a[rows]
            if cols[0] >= 0 and (np.diff(cols) == 1).all():
                a = a[:, cols[0]:cols[-1] + 1]
            else:
                a = np.where(cols < 0, np.float32(0), a[:, np.maximum(cols, 0)])
            t = tiled(a)
            out[i, :, :t.shape[1]] = t
    return np.ascontiguousarray(out.reshape(-1, 2, P, 1024).transpose(0, 2, 1, 3).reshape(-1, P, UNIT))


def pack_params(x):
    out = np.zeros((P, NPAR), np.float32)
    col = lambda v: v.reshape(-1, P).T
    twice = lambda v: np.repeat(col(v), 2, axis=1)
    both = lambda a, b: np.stack([col(a), col(b)], 2).reshape(P, -1)
    every = lambda v: np.broadcast_to(v.reshape(1, -1), (P, v.size))
    vals = {
        "bmod": twice(x["b_mod"][0]), "gmix": twice(x["g_mix"][0]), "gffn": col(x["g_ffn"][0]),
        "gfinal": col(x["g_final"]), "cond": both(x["c"][0], x["c_ctx"]),
        "cond2": both(x["c_2"][0], x["c_ctx_2"]), "retgn": col(x["ret_gn"][0]),
        "sink": every(x["win_sink"][0]), "decay": every(x["ret_decay_logit"][0]),
    }
    for l in LAYERS:
        for n, v in (("bmod2", twice(x["mod_b_2"][l])), ("pre", twice(x["pre_norm_2"][l])),
                     ("post", twice(x["post_norm_2"][l])), ("qnorm", col(x["mla_q_norm_2"][l])),
                     ("kvnorm", col(x["mla_kv_norm_2"][l])), ("pscale", col(x["pool_scale_2"][l])),
                     ("afb", col(x["gla_af_b_2"][l])), ("abb", col(x["gla_ab_b_2"][l])),
                     ("glan", col(x["gla_norm_2"][l]))):
            vals[n + str(l)] = v
    for n, (a, b) in PCOL.items():
        out[:, a:b] = vals[n]
    return out


def kernel(**inputs):
    import concourse.bacc as bacc
    from concourse.bass_utils import run_bass_kernel_spmd
    x = {k: np.asarray(v) for k, v in inputs.items()}
    feature_major = lambda a: a.T.reshape(KT, P, -1).transpose(1, 0, 2)
    arrays = {
        "weights": pack_weights(x),
        "params": pack_params(x),
        "acts": feature_major(np.concatenate([x["ctx"][0], x["x"][0]], 0)),
        "ctx2": feature_major(x["ctx_2"][0]),
        "router": x["w_router"][0].reshape(KT, P, NE).transpose(1, 0, 2),
        "rpb": np.pad(x["na_rpb"][0], ((0, 0), (0, 0), (48, 48))),
        **constants(),
    }
    arrays = {"in_" + k: np.ascontiguousarray(v) for k, v in arrays.items()}
    nc = bacc.Bacc("TRN2", target_bir_lowering=False, num_devices=1)
    f32 = mybir.dt.float32
    dram = {k[3:]: nc.dram_tensor(k, v.shape, f32, kind="ExternalInput").ap() for k, v in arrays.items()}
    out = nc.dram_tensor("out_x", (P, KT, SEQ), f32, kind="ExternalOutput").ap()
    scratch = nc.dram_tensor("saved_residual", (P, KT, TOK), f32, kind="Internal").ap()
    program(nc, dram, scratch, out)
    got = run_bass_kernel_spmd(nc, [arrays], core_ids=[0]).results[0]["out_x"]
    return got.transpose(1, 0, 2).reshape(D, SEQ).T.reshape(1, SEQ, D)
```
